# Optimizing a Trainium2 kernel written in Bass

```python
import math
import jax, jax.numpy as jnp
from jax import lax
import numpy as np

D_MODEL = 1024
BATCH = 1
SEQ = 256
DEPTH = 1

D_MIX = D_MODEL
ATTN_WIDTH = D_MIX // 2
N_DIFF_HEADS = 4
DIFF_HEAD_DIM = ATTN_WIDTH // (2 * N_DIFF_HEADS)
DIFF_V_DIM = 2 * DIFF_HEAD_DIM
ATTN_QK = N_DIFF_HEADS * 2 * DIFF_HEAD_DIM
POOL_WIDTH = D_MIX - ATTN_WIDTH
POOL_WINDOWS = (2, 4, 8, 16)
N_POOL_GROUPS = len(POOL_WINDOWS)
POOL_GROUP_DIM = POOL_WIDTH // N_POOL_GROUPS
D_IN_PROJ = 2 * ATTN_QK + ATTN_WIDTH + POOL_WIDTH

ROPE_THETA = 500000.0
ROPE_DIM = DIFF_HEAD_DIM // 4
Q_BLOCK = 128

N_EXPERTS = 32
TOP_K = 4
D_EXPERT = D_MODEL
SWIGLU_LIMIT = 7.0
SWIGLU_ALPHA = 1.702
MOE_BLOCK = 128

PLE_DIM = 256
EPS = 1e-6


def rms_norm(t, g):
    tf = t.astype(jnp.float32)
    y = tf * lax.rsqrt(jnp.mean(tf * tf, axis=-1, keepdims=True) + EPS)
    return (y * g.astype(jnp.float32)).astype(t.dtype)

def apply_partial_rope(t, cos, sin):
    tf = t.astype(jnp.float32)
    half = ROPE_DIM // 2
    t1 = tf[..., :half]
    t2 = tf[..., half:ROPE_DIM]
    out = jnp.concatenate([t1 * cos - t2 * sin, t2 * cos + t1 * sin, tf[..., ROPE_DIM:]], axis=-1)
    return out.astype(t.dtype)

def diff_attention(q, k, v, positions, q_norm, k_norm, lam_q1, lam_k1, lam_q2, lam_k2, subln, lambda_init):
    B, S, _ = q.shape
    H, d = N_DIFF_HEADS, DIFF_HEAD_DIM
    q = rms_norm(q.reshape(B, S, H, 2, d), q_norm)
    k = rms_norm(k.reshape(B, S, H, 2, d), k_norm)
    v = v.reshape(B, S, H, DIFF_V_DIM)
    freqs = ROPE_THETA ** (-jnp.arange(0, ROPE_DIM, 2, dtype=jnp.float32) / ROPE_DIM)
    ang = positions.astype(jnp.float32)[..., None] * freqs
    cos = jnp.cos(ang)[:, :, None, None, :]
    sin = jnp.sin(ang)[:, :, None, None, :]
    q = apply_partial_rope(q, cos, sin)
    k = apply_partial_rope(k, cos, sin)
    lam = (jnp.exp(jnp.sum(lam_q1.astype(jnp.float32) * lam_k1.astype(jnp.float32)))
           - jnp.exp(jnp.sum(lam_q2.astype(jnp.float32) * lam_k2.astype(jnp.float32)))
           + lambda_init)
    scale = 1.0 / math.sqrt(d)
    nb = S // Q_BLOCK
    qb = q.transpose(0, 2, 3, 1, 4).reshape(B, H, 2, nb, Q_BLOCK, d)
    qb = jnp.moveaxis(qb, 3, 0)
    kt = k.transpose(0, 2, 3, 1, 4)
    vt = v.transpose(0, 2, 1, 3)
    key_idx = jnp.arange(S)

    def block(args):
        qblk, start = args
        s = jnp.einsum('bhcqd,bhckd->bhcqk', qblk, kt).astype(jnp.float32) * scale
        q_idx = start + jnp.arange(Q_BLOCK)
        mask = key_idx[None, :] <= q_idx[:, None]
        s = jnp.where(mask, s, -jnp.inf)
        a = jax.nn.softmax(s, axis=-1)
        w = a[:, :, 0] - lam * a[:, :, 1]
        return jnp.einsum('bhqk,bhkv->bhqv', w.astype(vt.dtype), vt)

    starts = jnp.arange(nb) * Q_BLOCK
    o = lax.map(block, (qb, starts))
    o = o.transpose(1, 0, 3, 2, 4).reshape(B, S, H, DIFF_V_DIM)
    o = rms_norm(o, subln) * (1.0 - lambda_init)
    return o.reshape(B, S, H * DIFF_V_DIM)

def pool_mixer(u, w_pool, pool_scale):
    B, S, _ = u.shape
    ug = u.reshape(B, S, N_POOL_GROUPS, POOL_GROUP_DIM)
    t_idx = jnp.arange(S)
    outs = []
    for g, w in enumerate(POOL_WINDOWS):
        uf = ug[:, :, g].astype(jnp.float32)
        cs = jnp.cumsum(uf, axis=1)
        shifted = jnp.pad(cs, ((0, 0), (w, 0), (0, 0)))[:, :S]
        count = jnp.minimum(t_idx + 1, w).astype(jnp.float32)
        outs.append((cs - shifted) / count[None, :, None] - uf)
    pooled = jnp.stack(outs, axis=2).astype(u.dtype)
    y = jnp.einsum('bsgc,gcd->bsgd', pooled, w_pool)
    return y.reshape(B, S, POOL_WIDTH) * pool_scale

def moe(xn, w_router, b_router, w_gate, b_gate, w_up, b_up, w_down, b_down):
    B, S, D = xn.shape
    N = B * S
    xt = xn.reshape(N, D)
    logits = (xt @ w_router).astype(jnp.float32) + b_router.astype(jnp.float32)
    top_vals, top_idx = lax.top_k(logits, TOP_K)
    gates = jax.nn.softmax(top_vals, axis=-1).astype(xn.dtype)
    NK = N * TOP_K
    expert_flat = top_idx.reshape(NK)
    token_flat = jnp.repeat(jnp.arange(N), TOP_K)
    gate_flat = gates.reshape(NK)
    order = jnp.argsort(expert_flat, stable=True)
    se = expert_flat[order]
    st = token_flat[order]
    sg = gate_flat[order]
    counts = jnp.bincount(expert_flat, length=N_EXPERTS)
    padded = ((counts + MOE_BLOCK - 1) // MOE_BLOCK) * MOE_BLOCK
    pend = jnp.cumsum(padded)
    pstart = pend - padded
    start = jnp.cumsum(counts) - counts
    dest = pstart[se] + (jnp.arange(NK) - start[se])
    n_blocks = -(-NK // MOE_BLOCK) + N_EXPERTS
    P = n_blocks * MOE_BLOCK
    xbuf = jnp.zeros((P, D), xn.dtype).at[dest].set(xt[st])
    block_expert = jnp.clip(jnp.searchsorted(pend, jnp.arange(n_blocks) * MOE_BLOCK, side='right'),
                            0, N_EXPERTS - 1)

    def expert_block(args):
        xb, e = args
        gt = xb @ w_gate[e] + b_gate[e]
        up = xb @ w_up[e] + b_up[e]
        gt = jnp.minimum(gt, SWIGLU_LIMIT)
        up = jnp.clip(up, -SWIGLU_LIMIT, SWIGLU_LIMIT)
        hdn = (up + 1.0) * (gt * jax.nn.sigmoid(SWIGLU_ALPHA * gt))
        return hdn @ w_down[e] + b_down[e]

    ybuf = lax.map(expert_block, (xbuf.reshape(n_blocks, MOE_BLOCK, D), block_expert)).reshape(P, D)
    y = ybuf[dest] * sg[:, None]
    out = jnp.zeros((N, D), xn.dtype).at[st].add(y)
    return out.reshape(B, S, D)

def first_inputs(seed: int = 0) -> dict:
    key = jax.random.key(seed)
    ks = jax.random.split(key, 32)
    f32 = jnp.float32
    L = DEPTH

    def nrm(k, shape, scale):
        return jax.random.normal(k, shape, f32) * scale

    def gain(k, shape):
        return 1.0 + 0.02 * jax.random.normal(k, shape, f32)

    x = jax.random.normal(ks[0], (BATCH, SEQ, D_MODEL), f32)
    p = jax.random.normal(ks[1], (DEPTH, BATCH, SEQ, PLE_DIM), f32)
    offsets = jax.random.randint(ks[2], (BATCH, 1), 0, SEQ, dtype=jnp.int32)
    positions = (offsets + jnp.arange(SEQ, dtype=jnp.int32)[None, :]).astype(jnp.int32)
    return {
        "x": x,
        "p": p,
        "positions": positions,
        "attn_norm": gain(ks[3], (L, D_MODEL)),
        "w_in": nrm(ks[4], (L, D_MODEL, D_IN_PROJ), D_MODEL ** -0.5),
        "q_norm": gain(ks[5], (L, DIFF_HEAD_DIM)),
        "k_norm": gain(ks[6], (L, DIFF_HEAD_DIM)),
        "lam_q1": nrm(ks[7], (L, DIFF_HEAD_DIM), 0.1),
        "lam_k1": nrm(ks[8], (L, DIFF_HEAD_DIM), 0.1),
        "lam_q2": nrm(ks[9], (L, DIFF_HEAD_DIM), 0.1),
        "lam_k2": nrm(ks[10], (L, DIFF_HEAD_DIM), 0.1),
        "subln": gain(ks[11], (L, DIFF_V_DIM)),
        "w_pool": nrm(ks[12], (L, N_POOL_GROUPS, POOL_GROUP_DIM, POOL_GROUP_DIM), POOL_GROUP_DIM ** -0.5),
        "pool_scale": gain(ks[13], (L, POOL_WIDTH)),
        "w_out": nrm(ks[14], (L, D_MIX, D_MODEL), D_MIX ** -0.5),
        "ffn_norm": gain(ks[15], (L, D_MODEL)),
        "w_router": nrm(ks[16], (L, D_MODEL, N_EXPERTS), D_MODEL ** -0.5),
        "b_router": nrm(ks[17], (L, N_EXPERTS), 0.01),
        "w_gate": nrm(ks[18], (L, N_EXPERTS, D_MODEL, D_EXPERT), D_MODEL ** -0.5),
        "b_gate": nrm(ks[19], (L, N_EXPERTS, D_EXPERT), 0.02),
        "w_up": nrm(ks[20], (L, N_EXPERTS, D_MODEL, D_EXPERT), D_MODEL ** -0.5),
        "b_up": nrm(ks[21], (L, N_EXPERTS, D_EXPERT), 0.02),
        "w_down": nrm(ks[22], (L, N_EXPERTS, D_EXPERT, D_MODEL), D_EXPERT ** -0.5),
        "b_down": nrm(ks[23], (L, N_EXPERTS, D_MODEL), 0.02),
        "ple_gate_norm": gain(ks[24], (L, D_MODEL)),
        "w_ple_gate": nrm(ks[25], (L, D_MODEL, D_MODEL), D_MODEL ** -0.5),
        "w_ple_proj": nrm(ks[26], (L, PLE_DIM, D_MODEL), PLE_DIM ** -0.5),
        "ple_post_norm": gain(ks[27], (L, D_MODEL)),
    }

def first_block(x, p, positions, attn_norm, w_in, q_norm, k_norm, lam_q1, lam_k1, lam_q2, lam_k2,
              subln, w_pool, pool_scale, w_out, ffn_norm, w_router, b_router, w_gate, b_gate,
              w_up, b_up, w_down, b_down, ple_gate_norm, w_ple_gate, w_ple_proj, ple_post_norm):
    h = x
    for i in range(DEPTH):
        lambda_init = 0.8 - 0.6 * math.exp(-0.3 * i)
        hn = rms_norm(h, attn_norm[i])
        z = hn @ w_in[i]
        q = z[..., :ATTN_QK]
        k = z[..., ATTN_QK:2 * ATTN_QK]
        v = z[..., 2 * ATTN_QK:2 * ATTN_QK + ATTN_WIDTH]
        u = z[..., 2 * ATTN_QK + ATTN_WIDTH:]
        a_out = diff_attention(q, k, v, positions, q_norm[i], k_norm[i], lam_q1[i], lam_k1[i],
                               lam_q2[i], lam_k2[i], subln[i], lambda_init)
        p_out = pool_mixer(u, w_pool[i], pool_scale[i])
        h = h + jnp.concatenate([a_out, p_out], axis=-1) @ w_out[i]
        h = h + moe(rms_norm(h, ffn_norm[i]), w_router[i], b_router[i], w_gate[i], b_gate[i],
                    w_up[i], b_up[i], w_down[i], b_down[i])
        gate = jax.nn.sigmoid(rms_norm(h, ple_gate_norm[i]) @ w_ple_gate[i])
        e = rms_norm(p[i].astype(h.dtype) @ w_ple_proj[i], ple_post_norm[i])
        h = h + gate * e
    return h


N_Q_HEADS = 8
N_KV_HEADS = 2
GROUP = N_Q_HEADS // N_KV_HEADS
HEAD_DIM = 64
ROT_DIM = HEAD_DIM // 4
WINDOW = 128
ATTN_BLOCK = 128
ATTN_WIDTH_2 = N_Q_HEADS * HEAD_DIM
KV_WIDTH = N_KV_HEADS * HEAD_DIM

HGRN_HEADS = 4
HGRN_KEY_DIM = 128
HGRN_VAL_DIM = 128
HGRN_KEY_WIDTH = HGRN_HEADS * HGRN_KEY_DIM
HGRN_WIDTH = HGRN_HEADS * HGRN_VAL_DIM
HGRN_CHUNK = 64

IN_SIZES = (ATTN_WIDTH_2, KV_WIDTH, KV_WIDTH,
            HGRN_KEY_WIDTH, HGRN_KEY_WIDTH, HGRN_WIDTH, HGRN_WIDTH,
            D_MODEL, D_MODEL)
IN_WIDTH = sum(IN_SIZES)

N_GROUPS = 4
EXPERTS_PER_GROUP = 8
N_EXPERTS_2 = N_GROUPS * EXPERTS_PER_GROUP
TOP_K_2 = 2
EXPERT_FF = 512

NORM_EPS = 1e-6


def rms_norm_2(x, w):
    xf = x.astype(jnp.float32)
    y = xf * lax.rsqrt(jnp.mean(xf * xf, axis=-1, keepdims=True) + NORM_EPS)
    return (y * w.astype(jnp.float32)).astype(x.dtype)

def rope_tables(positions):
    inv_freq = ROPE_THETA ** (-jnp.arange(0, ROT_DIM, 2, dtype=jnp.float32) / ROT_DIM)
    ang = positions.astype(jnp.float32)[..., None] * inv_freq
    return jnp.cos(ang)[:, :, None, :], jnp.sin(ang)[:, :, None, :]

def partial_rope(x, cos, sin):
    half = ROT_DIM // 2
    xf = x.astype(jnp.float32)
    x1, x2 = xf[..., :half], xf[..., half:ROT_DIM]
    out = jnp.concatenate([x1 * cos - x2 * sin, x2 * cos + x1 * sin, xf[..., ROT_DIM:]], axis=-1)
    return out.astype(x.dtype)

def sliding_window_gqa(q, k, v, sinks):
    B, S = q.shape[0], q.shape[1]
    nb = S // ATTN_BLOCK
    qb = q.reshape(B, nb, ATTN_BLOCK, N_KV_HEADS, GROUP, HEAD_DIM).astype(jnp.float32)
    kb = k.reshape(B, nb, ATTN_BLOCK, N_KV_HEADS, HEAD_DIM).astype(jnp.float32)
    vb = v.reshape(B, nb, ATTN_BLOCK, N_KV_HEADS, HEAD_DIM).astype(jnp.float32)
    pad = ((0, 0), (1, 0), (0, 0), (0, 0), (0, 0))
    kk = jnp.concatenate([jnp.pad(kb[:, :-1], pad), kb], axis=2)
    vv = jnp.concatenate([jnp.pad(vb[:, :-1], pad), vb], axis=2)
    s = jnp.einsum('bnqhgd,bnkhd->bnhgqk', qb, kk) * (HEAD_DIM ** -0.5)
    qi = jnp.arange(ATTN_BLOCK)[:, None] + ATTN_BLOCK
    kj = jnp.arange(2 * ATTN_BLOCK)[None, :]
    band = (kj <= qi) & (qi - kj < WINDOW)
    has_prev = (jnp.arange(nb)[:, None, None] > 0) | (kj[None] >= ATTN_BLOCK)
    valid = band[None] & has_prev
    s = jnp.where(valid[None, :, None, None], s, -jnp.inf)
    sink = sinks.astype(jnp.float32).reshape(N_KV_HEADS, GROUP)[None, None, :, :, None, None]
    m = jnp.maximum(jnp.max(s, axis=-1, keepdims=True), sink)
    p = jnp.exp(s - m)
    denom = jnp.sum(p, axis=-1, keepdims=True) + jnp.exp(sink - m)
    o = jnp.einsum('bnhgqk,bnkhd->bnqhgd', p / denom, vv)
    return o.reshape(B, S, ATTN_WIDTH_2).astype(q.dtype)

def hgrn2_chunkwise(q, k, v, log_f):
    B, S = q.shape[0], q.shape[1]
    nc = S // HGRN_CHUNK

    def to_chunks(t):
        return t.reshape(B, nc, HGRN_CHUNK, HGRN_HEADS, t.shape[-1]).transpose(1, 0, 3, 2, 4)

    causal = jnp.tril(jnp.ones((HGRN_CHUNK, HGRN_CHUNK), dtype=bool))

    def step(state, inp):
        qc, kc, vc, gc = inp
        b = jnp.cumsum(gc, axis=2)
        o_inter = jnp.einsum('bhtk,bhkv->bhtv', qc * jnp.exp(b), state)
        diff = b[:, :, :, None, :] - b[:, :, None, :, :]
        decay = jnp.exp(jnp.where(causal[:, :, None], diff, -jnp.inf))
        a = jnp.einsum('bhtk,bhsk,bhtsk->bhts', qc, kc, decay)
        o_intra = jnp.einsum('bhts,bhsv->bhtv', a, vc)
        b_last = b[:, :, -1:, :]
        state = jnp.exp(b_last[:, :, 0])[..., None] * state + jnp.einsum(
            'bhsk,bhsv->bhkv', kc * jnp.exp(b_last - b), vc)
        return state, o_inter + o_intra

    init = jnp.zeros((B, HGRN_HEADS, HGRN_KEY_DIM, HGRN_VAL_DIM), jnp.float32)
    _, o = lax.scan(step, init, (to_chunks(q), to_chunks(k), to_chunks(v), to_chunks(log_f)))
    return o.transpose(1, 0, 3, 2, 4).reshape(B, S, HGRN_HEADS, HGRN_VAL_DIM)

def hierarchical_moe(xn, w_rg, b_rg, w_re, b_re, w_gate, w_up, w_down):
    T, D = xn.shape
    lg = (xn @ w_rg).astype(jnp.float32) + b_rg.astype(jnp.float32)
    pg = jax.nn.softmax(lg, axis=-1)
    gsel = jnp.argmax(pg, axis=-1)
    pgsel = jnp.take_along_axis(pg, gsel[:, None], axis=1)[:, 0]
    le = ((xn @ w_re).astype(jnp.float32) + b_re.astype(jnp.float32)).reshape(T, N_GROUPS, EXPERTS_PER_GROUP)
    le_sel = jnp.take_along_axis(le, gsel[:, None, None], axis=1)[:, 0]
    pe = jax.nn.softmax(le_sel, axis=-1)
    topv, topi = lax.top_k(pe, TOP_K_2)
    gate_w = pgsel[:, None] * topv / jnp.sum(topv, axis=-1, keepdims=True)
    eid = gsel[:, None] * EXPERTS_PER_GROUP + topi

    TK = T * TOP_K_2
    flat_e = eid.reshape(-1).astype(jnp.int32)
    flat_tok = jnp.repeat(jnp.arange(T, dtype=jnp.int32), TOP_K_2)
    flat_w = gate_w.reshape(-1)
    order = jnp.argsort(flat_e)
    se = flat_e[order]
    counts = jnp.bincount(flat_e, length=N_EXPERTS_2)
    starts = jnp.cumsum(counts) - counts
    padded = ((counts + MOE_BLOCK - 1) // MOE_BLOCK) * MOE_BLOCK
    pends = jnp.cumsum(padded)
    pstarts = pends - padded
    dest = pstarts[se] + jnp.arange(TK, dtype=jnp.int32) - starts[se]
    P = TK + N_EXPERTS_2 * MOE_BLOCK
    P = ((P + MOE_BLOCK - 1) // MOE_BLOCK) * MOE_BLOCK
    nblk = P // MOE_BLOCK
    row_tok = jnp.full((P,), T, jnp.int32).at[dest].set(flat_tok[order])
    row_w = jnp.zeros((P,), jnp.float32).at[dest].set(flat_w[order])
    blk_e = jnp.minimum(jnp.searchsorted(pends, jnp.arange(nblk, dtype=jnp.int32) * MOE_BLOCK, side='right'),
                        N_EXPERTS_2 - 1)
    x_pad = jnp.concatenate([xn, jnp.zeros((1, D), xn.dtype)], axis=0)
    x_blocks = x_pad[row_tok].reshape(nblk, MOE_BLOCK, D)

    def expert_block(args):
        xb, e = args
        h = jax.nn.silu(xb @ w_gate[e]) * (xb @ w_up[e])
        return h @ w_down[e]

    y_blocks = lax.map(expert_block, (x_blocks, blk_e))
    y_rows = y_blocks.reshape(P, D) * row_w[:, None].astype(y_blocks.dtype)
    return jax.ops.segment_sum(y_rows, row_tok, num_segments=T + 1)[:T]

def second_inputs(seed: int = 0) -> dict:
    key = jax.random.key(seed)
    ks = jax.random.split(key, 24)
    f32 = jnp.float32
    nrm = lambda k, shape, scale: jax.random.normal(k, shape, f32) * scale
    x = jax.random.normal(ks[0], (BATCH, SEQ, D_MODEL), f32)
    offs = jax.random.randint(ks[1], (BATCH, 1), 0, 4096, dtype=jnp.int32)
    positions = offs + jnp.arange(SEQ, dtype=jnp.int32)[None, :]
    return {
        "x": x,
        "positions": positions,
        "norm1_w": 1.0 + nrm(ks[2], (DEPTH, D_MODEL), 0.02),
        "w_in": nrm(ks[3], (DEPTH, D_MODEL, IN_WIDTH), D_MODEL ** -0.5),
        "q_norm_w": 1.0 + nrm(ks[4], (DEPTH, HEAD_DIM), 0.02),
        "k_norm_w": 1.0 + nrm(ks[5], (DEPTH, HEAD_DIM), 0.02),
        "attn_sinks": nrm(ks[6], (DEPTH, N_Q_HEADS), 0.5),
        "hgrn_lower_bounds": nrm(ks[7], (DEPTH + 1, HGRN_KEY_WIDTH), 0.5),
        "hgrn_norm_w": 1.0 + nrm(ks[8], (DEPTH, HGRN_VAL_DIM), 0.02),
        "w_branch_attn": nrm(ks[9], (DEPTH, ATTN_WIDTH_2, D_MODEL), ATTN_WIDTH_2 ** -0.5),
        "w_branch_hgrn": nrm(ks[10], (DEPTH, HGRN_WIDTH, D_MODEL), HGRN_WIDTH ** -0.5),
        "w_out": nrm(ks[11], (DEPTH, D_MODEL, D_MODEL), D_MODEL ** -0.5),
        "norm2_w": 1.0 + nrm(ks[12], (DEPTH, D_MODEL), 0.02),
        "w_router_group": nrm(ks[13], (DEPTH, D_MODEL, N_GROUPS), D_MODEL ** -0.5),
        "b_router_group": nrm(ks[14], (DEPTH, N_GROUPS), 0.01),
        "w_router_expert": nrm(ks[15], (DEPTH, D_MODEL, N_EXPERTS_2), D_MODEL ** -0.5),
        "b_router_expert": nrm(ks[16], (DEPTH, N_EXPERTS_2), 0.01),
        "w_gate_experts": nrm(ks[17], (DEPTH, N_EXPERTS_2, D_MODEL, EXPERT_FF), D_MODEL ** -0.5),
        "w_up_experts": nrm(ks[18], (DEPTH, N_EXPERTS_2, D_MODEL, EXPERT_FF), D_MODEL ** -0.5),
        "w_down_experts": nrm(ks[19], (DEPTH, N_EXPERTS_2, EXPERT_FF, D_MODEL), EXPERT_FF ** -0.5),
    }

def second_block(x, positions, norm1_w, w_in, q_norm_w, k_norm_w, attn_sinks, hgrn_lower_bounds,
              hgrn_norm_w, w_branch_attn, w_branch_hgrn, w_out, norm2_w, w_router_group,
              b_router_group, w_router_expert, b_router_expert, w_gate_experts, w_up_experts,
              w_down_experts):
    B, S, D = x.shape
    cos, sin = rope_tables(positions)
    split_points = [int(v) for v in np.cumsum(IN_SIZES)[:-1]]
    lower_bounds = jnp.cumsum(jax.nn.softmax(hgrn_lower_bounds.astype(jnp.float32), axis=0), axis=0)
    for l in range(DEPTH):
        xn = rms_norm_2(x, norm1_w[l])
        proj = xn @ w_in[l]
        q_a, k_a, v_a, q_h, f_h, i_h, g_h, z_a, z_b = jnp.split(proj, split_points, axis=-1)

        q_a = partial_rope(rms_norm_2(q_a.reshape(B, S, N_Q_HEADS, HEAD_DIM), q_norm_w[l]), cos, sin)
        k_a = partial_rope(rms_norm_2(k_a.reshape(B, S, N_KV_HEADS, HEAD_DIM), k_norm_w[l]), cos, sin)
        v_a = v_a.reshape(B, S, N_KV_HEADS, HEAD_DIM)
        attn = sliding_window_gqa(q_a, k_a, v_a, attn_sinks[l])

        lb = lower_bounds[l]
        fg = lb + (1.0 - lb) * jax.nn.sigmoid(f_h.astype(jnp.float32))
        hq = jax.nn.silu(q_h.astype(jnp.float32)).reshape(B, S, HGRN_HEADS, HGRN_KEY_DIM)
        hk = (1.0 - fg).reshape(B, S, HGRN_HEADS, HGRN_KEY_DIM)
        hlogf = jnp.log(fg).reshape(B, S, HGRN_HEADS, HGRN_KEY_DIM)
        hv = i_h.astype(jnp.float32).reshape(B, S, HGRN_HEADS, HGRN_VAL_DIM)
        ho = rms_norm_2(hgrn2_chunkwise(hq, hk, hv, hlogf), hgrn_norm_w[l]).reshape(B, S, HGRN_WIDTH)
        hgrn = (ho * jax.nn.silu(g_h.astype(jnp.float32))).astype(x.dtype)

        mixed = (jax.nn.sigmoid(z_a) * (attn @ w_branch_attn[l])
                 + jax.nn.sigmoid(z_b) * (hgrn @ w_branch_hgrn[l]))
        x = x + mixed @ w_out[l]

        hn = rms_norm_2(x, norm2_w[l]).reshape(B * S, D)
        moe = hierarchical_moe(hn, w_router_group[l], b_router_group[l], w_router_expert[l],
                               b_router_expert[l], w_gate_experts[l], w_up_experts[l], w_down_experts[l])
        x = x + moe.reshape(B, S, D).astype(x.dtype)
    return x


def setup_inputs(seed=0):
    out = dict(first_inputs(seed))
    for name, value in second_inputs(seed + 1).items():
        if name != "x":
            out[name + "_2"] = value
    return out


def reference(
    x, p, positions, attn_norm, w_in, q_norm, k_norm, lam_q1, lam_k1, lam_q2, lam_k2, subln,
    w_pool, pool_scale, w_out, ffn_norm, w_router, b_router, w_gate, b_gate, w_up, b_up, w_down,
    b_down, ple_gate_norm, w_ple_gate, w_ple_proj, ple_post_norm, positions_2, norm1_w_2,
    w_in_2, q_norm_w_2, k_norm_w_2, attn_sinks_2, hgrn_lower_bounds_2, hgrn_norm_w_2,
    w_branch_attn_2, w_branch_hgrn_2, w_out_2, norm2_w_2, w_router_group_2, b_router_group_2,
    w_router_expert_2, b_router_expert_2, w_gate_experts_2, w_up_experts_2, w_down_experts_2,
):
    x = first_block(
        x, p, positions, attn_norm, w_in, q_norm, k_norm, lam_q1, lam_k1, lam_q2, lam_k2, subln,
        w_pool, pool_scale, w_out, ffn_norm, w_router, b_router, w_gate, b_gate, w_up, b_up,
        w_down, b_down, ple_gate_norm, w_ple_gate, w_ple_proj, ple_post_norm,
    )
    return second_block(
        x, positions_2, norm1_w_2, w_in_2, q_norm_w_2, k_norm_w_2, attn_sinks_2,
        hgrn_lower_bounds_2, hgrn_norm_w_2, w_branch_attn_2, w_branch_hgrn_2, w_out_2,
        norm2_w_2, w_router_group_2, b_router_group_2, w_router_expert_2, b_router_expert_2,
        w_gate_experts_2, w_up_experts_2, w_down_experts_2,
    )


_drawn_inputs = setup_inputs


def setup_inputs(seed=0):
    import zlib

    import numpy as np

    out = dict(_drawn_inputs(seed))
    spreads = {}
    factors = {'lam_k2': 5.372,
     'b_gate': 3.732,
     'b_up': 8.0,
     'b_down': 6.212,
     'ple_gate_norm': 6.747,
     'ple_post_norm': 5.24,
     'norm1_w_2': 4.134,
     'q_norm_w_2': 8.0,
     'k_norm_w_2': 7.299,
     'attn_sinks_2': 200.0,
     'hgrn_lower_bounds_2': 2.836,
     'hgrn_norm_w_2': 20.326,
     'b_router_group_2': 64.0,
     'b_router_expert_2': 64.0,
     'norm2_w_2': 8.0,
     'w_router_group_2': 3.638,
     'w_router_expert_2': 3.527,
     'w_gate_experts_2': 3.305,
     'w_up_experts_2': 3.115,
     'w_down_experts_2': 3.111}
    for name, (base, spread) in spreads.items():
        noise = np.random.default_rng([zlib.crc32(name.encode()), seed]).standard_normal(out[name].shape)
        drawn = base * np.exp(spread * noise) if base else spread * noise
        out[name] = __import__('jax').numpy.asarray(drawn.astype(out[name].dtype))
    for name, factor in factors.items():
        out[name] = (out[name] * factor).astype(out[name].dtype)
    return out
```

```python
import math
from contextlib import ExitStack

import numpy as np

import concourse.bass as bass
from concourse import mybir
from concourse.bass import ds

F32 = mybir.dt.float32
I32 = mybir.dt.int32
ALU = mybir.AluOpType
ACT = mybir.ActivationFunctionType
X = mybir.AxisListType.X

P = 128
T = 256
TT = T // P
D = 1024
DC = D // P
EPS = 1e-6
NEG = -1.0e30
E = 32
CAP = 64
ROUNDS = T // CAP
NLIST = 16
SLOTS = 6
SLOT = 4096
ROPE_THETA = 500000.0
ROT = 16
SUB = 16
NSUB = T // SUB
LAMBDA_INIT = 0.8 - 0.6 * math.exp(-0.3 * 0)
A_NORM, F_NORM, G_NORM, N1_NORM, N2_NORM = range(5)
NORM_NTH = (1, 4, 5, 7, 10)
QK_NTH, SUB_NTH, EMB_NTH, QK2_NTH, HG_NTH = 2, 3, 6, 8, 9


def two_blocks(nc, w, out):
    ctx = ExitStack()
    sems = {}

    def sem(name):
        if name not in sems:
            sems[name] = ctx.enter_context(nc.semaphore(name))
        return sems[name]

    def sb(name, shape, dt=F32):
        return ctx.enter_context(nc.sbuf_tensor(name, shape, dt))

    with ctx:
        ring = sb("ring", [P, SLOTS, SLOT])
        h = sb("h", [P, TT, D])
        xs = sb("xs", [P, TT, D])
        xT = sb("xT", [P, DC, T])
        Z = sb("Z", [P, TT, 4864])
        scr = sb("scr", [P, 9216])
        ps = ctx.enter_context(nc.psum_tensor("ps", [P, 8, 512], F32))

        ident = sb("ident", [P, P])
        zeros = sb("zeros", [P, P])
        ones = sb("ones", [P, P])
        mask_own = sb("mask_own", [P, 2 * P])
        mask_win = sb("mask_win", [P, 2 * P])
        tri = sb("tri", [P, P])
        blk = sb("blk", [P, P])
        iota = sb("iota", [P, CAP])
        pcol = sb("pcol", [P, 1])
        par = sb("par", [P, 2])
        thr = sb("thr", [P, ROUNDS - 1])
        gcol = sb("gcol", [P, 5, DC])
        freq = sb("freq", [P, ROT // 2])
        posi = sb("posi", [P, 2 * TT], I32)
        posf = sb("posf", [P, 2 * TT])
        ang = sb("ang", [P, 4, 8])
        red = sb("red", [P, 2, 4, 8])
        trig = sb("trig", [P, 2, 4, 8])
        qkw = sb("qkw", [P, 2, 64])
        qkw2 = sb("qkw2", [P, 2, 64])
        lams = sb("lams", [P, 4, 64])
        subln = sb("subln", [P, P])
        brt = sb("brt", [P, E])
        brt2 = sb("brt2", [P, 36])
        sinks = sb("sinks", [P, 8])
        lbc = sb("lbc", [P, 2, 4])
        lb = sb("lb", [P, 3, 4])
        hnorm = sb("hnorm", [P, P])
        st = sb("st", [P, 160])
        lst = sb("lst", [1, 48], I32)

        def bank(k):
            return ps[:, k, :]

        ss, ms, rt, rstd = (st[:, 2 * k:2 * k + 2] for k in range(4))
        qss, qms, qrt, qrs = (st[:, 8 + 32 * k:40 + 32 * k] for k in range(4))
        lam = st[:, 136:144]

        qkT = scr[:, 0:2048].rearrange("p (g t) -> p g t", t=T)
        sc1 = scr[:, 2048:4096].rearrange("p (g k) -> p g k", k=T)
        sc0 = scr[:, 4096:5120].rearrange("p (g k) -> p g k", k=P)
        tmp = scr[:, 5120:6144]
        wT = scr[:, 6144:7680].rearrange("p (g q) -> p g q", q=P)
        poolT = scr[:, 7680:8704].rearrange("p (g t) -> p g t", t=T)
        poolM = Z[:, 0, 2048:4096].rearrange("p (s g t) -> p s g t", s=2, g=4)
        wpool = Z[:, 1, 2048:2560].rearrange("p (g d) -> p g d", g=4)
        pscale = Z[:, 1, 2560:3072]
        post = Z[:, 1, 3840:4864]

        bias_gu = Z[0:E, 0, 0:2048].rearrange("e (g n) -> e g n", g=2)
        bias_dn = Z[0:E, 0, 2048:3072]
        act_g, act_t, act_h = (Z[:, 0, 3072 + 512 * k:3584 + 512 * k] for k in range(3))
        moe = Z[:, 1, :]
        wrt = moe[:, 0:288].rearrange("p (c e) -> p c e", c=DC)
        logit = moe[:, 288:360].rearrange("p (a e) -> p a e", a=TT)
        msk, gat, eqs, pre = (moe[:, 360 + 64 * k:424 + 64 * k].rearrange("p (a e) -> p a e", a=TT) for k in range(4))
        rank = moe[:, 616:872].rearrange("p (a r) -> p a r", a=TT)
        top = moe[:, 872:888].rearrange("p (a k) -> p a k", a=TT)
        few = moe[:, 888:1000]
        one_hot = moe[:, 1000:1128].rearrange("p (a s) -> p a s", a=TT)
        gated = moe[:, 1128:1384].rearrange("p (a j s) -> p a j s", a=TT, j=2)
        back = moe[:, 1384:1640]
        picked = moe[:, 1640:2152]
        hid = moe[:, 2152:2664]
        y = moe[:, 2664:3176]
        pick_bias = moe[0:E, 3176:3176 + CAP]

        def cols(name, lo, n):
            src = w[name][0].rearrange("(p c) n -> p c n", p=P)
            return src[:, :, lo:lo + n], src.shape[1], n

        front = [cols("w_in", 512 * k, 512) for k in range(4)] + [cols("w_out", 512 * k, 512) for k in range(2)]

        def slot(s, c, n):
            return ring[:, s, 0:c * n].rearrange("p (c n) -> p c n", c=c)

        W2 = "w_in_2"
        middle = [(cols("w_ple_gate", 0, 512), 2), (cols("w_ple_gate", 512, 512), 4), (cols("w_ple_proj", 0, 1024), 8),
                  (cols(W2, 0, 512), 10), (cols(W2, 512, 256), 12), (cols(W2, 768, 512), 14),
                  (cols(W2, 1280, 512), 16), (cols(W2, 1792, 512), 18), (cols(W2, 2304, 512), 20),
                  (cols(W2, 2816, 512), 22), (cols(W2, 3328, 512), 24), (cols(W2, 3840, 512), 26),
                  (cols(W2, 4352, 512), 28), (cols("w_branch_attn_2", 0, 1024), 32),
                  (cols("w_branch_hgrn_2", 0, 1024), 36), (cols("w_out_2", 0, 512), 38), (cols("w_out_2", 512, 512), 40)]

        in_slot = [len(range(s, len(middle), SLOTS)) for s in range(SLOTS)]
        FULL0 = ([1] * SLOTS, [1 + E + n for n in in_slot])
        FREE0 = ([0] * SLOTS, [E] * SLOTS)
        FF = (1024, 512)
        HC = (4, 2)
        GATES = ("w_gate", "w_gate_experts_2")
        UPS = ("w_up", "w_up_experts_2")
        DOWNS = ("w_down", "w_down_experts_2")
        PER = (6, 3)
        TOPK = (4, 2)
        NR = (32, 36)

        def expert_loads(k, e, s0):
            def src(name, text, **sizes):
                return w[name][0, ds(e, 1)].rearrange(text, p=P, **sizes)
            if k == 0:
                loads = []
                for i, name in enumerate((GATES[0], UPS[0])):
                    for q in range(2):
                        v = src(name, "a (p c) n -> p (a c n)")
                        loads.append((s0 + 2 * i + q, ring[:, s0 + 2 * i + q, :], v[:, SLOT * q:SLOT * (q + 1)]))
                v = src(DOWNS[0], "a (j p c) n -> p j (a c n)", j=2)
                for j in range(2):
                    loads.append((s0 + 4 + j, ring[:, s0 + 4 + j, :], v[:, j, :]))
                return loads
            loads = []
            for q in range(2):
                for i, name in enumerate((GATES[1], UPS[1])):
                    v = src(name, "a (p c) n -> p (a c n)")
                    loads.append((s0 + q, ring[:, s0 + q, 2048 * i:2048 * (i + 1)], v[:, 2048 * q:2048 * (q + 1)]))
            v = src(DOWNS[1], "a (j p c) n -> p j (a c n)", j=2)
            loads.append((s0 + 2, ring[:, s0 + 2, :].rearrange("p (j n) -> p j n", j=2), v))
            return loads

        LOADS = ((1,) * 6, (2, 2, 1))
        LAST = ({"gate": 1, "up": 3, "down": 5}, {"gate_up": 1, "down": 2})

        PAIR = (1, 2)

        NEXT = (["one_hot", "one_hot", "bias", "picked"], ["one_hot", "one_hot", "picked"])
        OWN = (["gated", "gated", "gate_min", "clip", "prod", "hidden"], ["gated", "gated", "prod", "hidden"])
        STEPS = {"act": ["sigmoid", "back", "hid", "y"], "pe": ["back", "hid", "scattered"]}

        def count(k, q, who, step, p):
            if who != "dve":
                steps, ahead = STEPS[who], 0
            elif q[0] == "m":
                steps, ahead = OWN[k] + NEXT[k], len(NEXT[k])
            else:
                steps, ahead = NEXT[k] + OWN[k], 0
            last = len(steps) - steps[::-1].index(step)
            if who == "dve" and q[0] == "m" and step in NEXT[k]:
                ahead, last = 0, last - len(OWN[k])
            return p * len(steps) + ahead + last

        def stage(eng, k, q, n, s0, name):
            s = s0 + LAST[k][name]
            if q[0] == "m":
                eng.wait_ge(free[s], n + 1 + FREE0[k][s])
            else:
                eng.wait_ge(sem(f"over_free{k}_{s}"), n + 1)

        def middle_full(i):
            s = i % SLOTS
            return full[s], 16 * (1 + E + i // SLOTS + 1)

        p_tok = scr[:, 0:512].rearrange("p (a n) -> p a n", a=TT)
        pT = scr[:, 512:1024].rearrange("p (c t) -> p c t", t=T)
        emb = scr[:, 2048:4096].rearrange("p (a n) -> p a n", a=TT)
        junk2 = scr[:, 4096:6144].rearrange("p (a n) -> p a n", a=TT)
        qT2 = scr[:, 0:1024].rearrange("p (i t) -> p i t", t=T)
        kT2 = scr[:, 1024:1280]
        sA0 = scr[:, 1280:2304].rearrange("p (g k) -> p g k", k=P)
        sA1 = scr[:, 2304:4352].rearrange("p (g k) -> p g k", k=T)
        pT2 = scr[:, 4352:7424].rearrange("p (g q) -> p g q", q=P)
        ao = scr[:, 8192:9216].rearrange("p (a n) -> p a n", a=TT)
        hq, fg = Z[:, 0, 3840:4864], Z[:, 1, 3840:4864]
        k1, pre_f, suf_f, r_q, w_a, w_b, q_e, ke_even, ke_odd = (scr[:, 1024 * k:1024 * (k + 1)] for k in range(9))
        by_sub = "p (b j) -> p b j"
        states = xs[:, :, :].rearrange("p a n -> p (a n)").rearrange("p (k n) -> p k n", k=4)

        full = [sem(f"slot_full{s}") for s in range(SLOTS)]
        free = [sem(f"slot_free{s}") for s in range(SLOTS)]

        block = ctx.enter_context(nc.Block())

        @block.sync
        def _(sp):
            for s, (src, c, n) in enumerate(front):
                sp.dma_start(slot(s, c, n), src).then_inc(full[s], 16)
            def experts(k, first):
                for u in range(PAIR[k]):
                    for s, dst, src in expert_loads(k, u, PER[k] * u):
                        first(s)
                        sp.dma_start(dst, src).then_inc(full[s], 16)
                with sp.Fori(1, E // PAIR[k]) as n:
                    for u in range(PAIR[k]):
                        for s, dst, src in expert_loads(k, n * PAIR[k] + u, PER[k] * u):
                            sp.wait_ge(free[s], n + FREE0[k][s])
                            sp.dma_start(dst, src).then_inc(full[s], 16)
                sp.wait_ge(sem("list"), k + 1)
                n = sp.value_load(lst[0:1, 0:1], min_val=0, max_val=NLIST)
                with sp.If(n > 0):
                    for s in range(PER[k]):
                        sp.wait_ge(free[s], E // PAIR[k] + FREE0[k][s])
                    with sp.Fori(0, n) as i:
                        e = sp.value_load(lst[0:1, ds(i + 1, 1)], min_val=0, max_val=E - 1)
                        seen = [0] * SLOTS
                        for s, dst, src in expert_loads(k, e, 0):
                            if not seen[s]:
                                sp.wait_ge(sem(f"over_free{k}_{s}"), i)
                            seen[s] = 1
                            sp.dma_start(dst, src).then_inc(sem(f"over_full{k}_{s}"), 16)
                    sp.wait_ge(sem(f"over_free{k}_{PER[k] - 1}"), n)
                    sp.sem_inc(sem("over_left"), 1)

            experts(0, lambda s: sp.wait_ge(sem("proj"), 2 * s + 2) if s < 4 else sp.wait_ge(sem("out1"), 2 * s - 6))
            for i, ((src, c, n), _) in enumerate(middle):
                s = i % SLOTS
                if i < SLOTS:
                    sp.wait_ge(free[s], E)
                else:
                    sp.wait_ge(sem("dense2"), middle[i - SLOTS][1])
                sp.dma_start(slot(s, c, n), src).then_inc(full[s], 16)
            last_use = [max(x[1] for x in middle[s::SLOTS]) for s in range(SLOTS)]
            experts(1, lambda s: sp.wait_ge(sem("dense2"), last_use[s]))
            for a in range(TT):
                sp.wait_ge(sem("moe_out"), 4)
                sp.dma_start(out[0, a * P:(a + 1) * P, :], h[:, a, :]).then_inc(sem("stored"), 16)
            sp.wait_ge(sem("stored"), 16 * TT)

        @block.gpsimd
        def _(pool):
            done = [0]

            def step(ins):
                ins.then_inc(sem("pool_chain"), 1)
                done[0] += 1
                pool.wait_ge(sem("pool_chain"), done[0])

            def select(view, op, fill, base, pattern, cm):
                step(pool.affine_select(out=view, in_=view, compare_op=op, fill=fill, base=base,
                                        pattern=pattern, channel_multiplier=cm))

            step(pool.memset(ident[:, :], 0.0))
            select(ident[:, :], ALU.not_equal, 1.0, 0, [[-1, P]], 1)
            for k in range(ROT // 2):
                pool.memset(freq[:, k:k + 1], float(np.float32(ROPE_THETA) ** np.float32(-2 * k / ROT)))
            pool.memset(zeros[:, :], 0.0)
            step(pool.memset(ones[:, :], 1.0))
            pool.memset(mask_own[:, :], 0.0)
            pool.memset(mask_win[:, :], 0.0)
            pool.memset(tri[:, :], 1.0)
            step(pool.memset(blk[:, :], 1.0))
            for m in (mask_own, mask_win):
                select(m[:, P:2 * P], ALU.is_ge, NEG, 0, [[-1, P]], 1)
            select(mask_win[:, 0:P], ALU.is_gt, NEG, 0, [[1, P]], -1)
            select(tri[:, :], ALU.is_gt, 0.0, 0, [[1, P]], -1)
            select(blk[:, :], ALU.is_ge, 0.0, 0, [[-SUB, P // SUB], [0, SUB]], 1)
            select(blk[:, :], ALU.is_ge, 0.0, SUB - 1, [[SUB, P // SUB], [0, SUB]], -1)
            step(pool.iota(iota[:, :], pattern=[[1, CAP]], base=0, channel_multiplier=0,
                           allow_small_or_imprecise_dtypes=True))
            step(pool.iota(pcol[:, :], pattern=[[1, 1]], base=0, channel_multiplier=1,
                           allow_small_or_imprecise_dtypes=True))
            for k in range(ROUNDS - 1):
                pool.memset(thr[:, k:k + 1], float(CAP * (k + 1)))
            for g, win in enumerate((2, 4, 8, 16)):
                band = poolM[:, :, g, :]
                step(pool.memset(band, 1.0 / win))
                for t in range(win - 1):
                    last = pool.memset(poolM[:, 0, g, t:t + 1], 1.0 / (t + 1))
                step(last)
                select(band, ALU.is_ge, 0.0, 0, [[-P, 2], [1, T]], -1)
                select(band, ALU.is_ge, 0.0, win - 1, [[P, 2], [-1, T]], 1)
            for s in range(2):
                v = poolM[:, s, :, s * P:(s + 1) * P]
                step(pool.tensor_tensor(v, v, ident[:, None, :].broadcast_to([P, 4, P]), ALU.subtract))
            step(pool.memset(st[:, 150:152], 0.0))
            pool.memset(st[:, 152:153], 0.0).then_inc(sem("consts"), 1)

            pool.wait_ge(sem("mix_ready"), 4)
            for dst, src in ((wrt[:, :, 0:E], w["w_router"][0].rearrange("(p c) e -> p c e", p=P)),
                             (bias_gu[:, 0, :], w["b_gate"][0]), (bias_gu[:, 1, :], w["b_up"][0]),
                             (bias_dn, w["b_down"][0])):
                pool.dma_start(dst, src).then_inc(sem("router_loaded"), 16)
            pool.dma_start(p_tok, w["p"][0, 0].rearrange("(a p) n -> p a n", p=P)).then_inc(sem("p_loaded"), 16)
            step(pool.tensor_copy(par[:, 1:2], blk[:, SUB:SUB + 1]))
            for k in (3, 5, 7):
                step(pool.tensor_tensor(par[:, 1:2], par[:, 1:2], blk[:, SUB * k:SUB * k + 1], ALU.add))
            pool.tensor_tensor(par[:, 0:1], ones[:, 0:1], par[:, 1:2], ALU.subtract).then_inc(sem("parity"), 1)
            pool.wait_ge(sem("mixed"), 4)
            for dst, src in ((wrt[:, :, 0:4], w["w_router_group_2"][0].rearrange("(p c) e -> p c e", p=P)),
                             (wrt[:, :, 4:36], w["w_router_expert_2"][0].rearrange("(p c) e -> p c e", p=P))):
                pool.dma_start(dst, src).then_inc(sem("router_loaded"), 16)

        @block.scalar
        def _(act):
            def load(dst, src, name="small_loaded"):
                act.dma_start(dst, src, allow_slow_non_contiguous=src.shape[-1] * src.ap[-1][0] != src.shape[-1]).then_inc(sem(name), 16)

            for a in range(TT):
                load(h[:, a, :], w["x"][0, a * P:(a + 1) * P, :], "x_loaded")
            for k, name in enumerate(("positions", "positions_2")):
                load(posi[:, 2 * k:2 * k + 2], w[name][0].rearrange("(a p) -> p a", p=P), "pos_loaded")
            n_small = [0]

            def small(dst, src):
                n_small[0] += 1
                load(dst, src)

            for k, name in enumerate(("attn_norm", "ffn_norm", "ple_gate_norm", "norm1_w_2", "norm2_w_2")):
                small(gcol[:, k, :], w[name][0].rearrange("(p c) -> p c", p=P))
            for k, name in enumerate(("q_norm", "k_norm")):
                small(qkw[:, k, :], w[name][0].partition_broadcast(P))
                small(qkw2[:, k, :], w[name + "_w_2"][0].partition_broadcast(P))
            for k, name in enumerate(("lam_q1", "lam_k1", "lam_q2", "lam_k2")):
                small(lams[:, k, :], w[name][0].partition_broadcast(P))
            small(subln[:, :], w["subln"][0].partition_broadcast(P))
            small(pscale, w["pool_scale"][0].partition_broadcast(P))
            small(wpool, w["w_pool"][0].rearrange("g c d -> c g d"))
            small(brt[:, :], w["b_router"][0].partition_broadcast(P))
            small(brt2[:, 0:4], w["b_router_group_2"][0].partition_broadcast(P))
            small(brt2[:, 4:36], w["b_router_expert_2"][0].partition_broadcast(P))
            small(post, w["ple_post_norm"][0].partition_broadcast(P))
            small(sinks[:, :], w["attn_sinks_2"][0].partition_broadcast(P))
            small(lbc[:, :, :], w["hgrn_lower_bounds_2"].rearrange("l (h p) -> p l h", p=P))
            small(hnorm[:, :], w["hgrn_norm_w_2"][0].partition_broadcast(P))
            assert n_small[0] == N_SMALL

            act.wait_ge(sem("angles"), 1)
            act.activation(trig[:, :, :, :], red[:, :, :, :], ACT.Sin).then_inc(sem("trig"), 1)

            def norm(k, ready):
                ready()
                for a in range(TT):
                    act.activation(xs[:, a, :], h[:, a, :], ACT.Square,
                                   accum_out=ss[:, a:a + 1]).then_inc(sem("norm_sumsq"), 1)
                act.wait_ge(sem("mean_sq"), NORM_NTH[k])
                act.activation(rt, ms, ACT.Sqrt).then_inc(sem("root"), 1)

            norm(A_NORM, lambda: act.wait_ge(sem("x_loaded"), 32))
            for j in range(8):
                act.wait_ge(sem("proj"), j + 1)
                act.copy(Z[:, j % 2, (j // 2) * 512:(j // 2 + 1) * 512], bank((4 + j) % 8)).then_inc(sem("z_copied"), 1)
            act.wait_ge(sem("mean_sq"), QK_NTH)
            act.activation(qrt, qms, ACT.Sqrt).then_inc(sem("root"), 1)
            act.wait_ge(sem("pooled"), 1)
            for g in range(2):
                act.copy(poolT[:, 2 * g:2 * g + 2, :], bank(4 + g).rearrange("p (g t) -> p g t", g=2)).then_inc(sem("pool_copied"), 1)
            for a in range(TT):
                act.wait_ge(sem("qk_turned"), 2 * a + 1)
                act.copy(qkT[:, 0:4, a * P:(a + 1) * P],
                         bank((6, 0)[a]).rearrange("p (g t) -> p g t", g=4)).then_inc(sem("q_copied"), 1)
            act.wait_ge(sem("lam_sums"), 1)
            act.activation(lam[:, 2:4], lam[:, 0:2], ACT.Exp).then_inc(sem("lam_exp"), 1)
            act.wait_ge(sem("row_max"), 1)
            for g in range(8):
                act.activation(sc0[:, g, :], sc0[:, g, :], ACT.Exp, bias=qss[:, g:g + 1],
                               accum_out=qms[:, g:g + 1]).then_inc(sem("probs"), 1)
            act.wait_ge(sem("row_max"), 2)
            for g in range(8):
                act.activation(sc1[:, g, :], sc1[:, g, :], ACT.Exp, bias=qss[:, 8 + g:9 + g],
                               accum_out=qms[:, 8 + g:9 + g]).then_inc(sem("probs"), 1)
            act.wait_ge(sem("w_turned"), 2)
            act.copy(wT[:, 4:8, :], bank(5).rearrange("p (g q) -> p g q", g=4)).then_inc(sem("w_copied_act"), 1)
            act.wait_ge(sem("mean_sq"), SUB_NTH)
            act.activation(qrt[:, 0:8], qms[:, 0:8], ACT.Sqrt).then_inc(sem("root"), 1)
            for b in (1, 3):
                act.wait_ge(sem("mix_turned"), b + 1)
                act.copy(xT[:, 4:8, (b // 2) * P:(b // 2 + 1) * P],
                         bank(1 + b).rearrange("p (g t) -> p g t", g=4)).then_inc(sem("mix_copied_act"), 1)

            def experts(k, ready):
                norm((F_NORM, N2_NORM)[k], ready)
                if k == 1:
                    act.wait_ge(sem("group_max"), 1)
                    for a in range(TT):
                        act.activation(few[:, 100 + 4 * a:104 + 4 * a], logit[:, a, 0:4], ACT.Exp, bias=few[:, 8 + a:9 + a],
                                       accum_out=few[:, 12 + a:13 + a]).then_inc(sem("group_exp"), 1)
                act.wait_ge(sem("top"), k + 1)
                for a in range(TT):
                    act.activation(gat[:, a, :], logit[:, a, NR[k] - E:NR[k]], ACT.Exp, bias=few[:, a:a + 1])\
                        .then_inc(sem("gate_exp"), 1)
                if k == 0:
                    act.wait_ge(sem("gates_turned"), 1)
                    act.copy(y[0:E, 0:T], bank(6)[0:E, 0:T]).then_inc(sem("gates_copied"), 1)

                def one(q, p, n=None, s0=0):
                    n = p if n is None else n
                    half = FF[k] // 2
                    if k == 0:
                        act.wait_ge(sem(q + "dve"), count(k, q, "dve", "gate_min", p))
                        act.activation(act_t, act_g, ACT.Sigmoid, scale=1.702).then_inc(sem(q + "act"), 1)
                    else:
                        stage(act, k, q, n, s0, "gate_up")
                        act.activation(act_t[:, 0:half], bank(4)[:, 0:half], ACT.Sigmoid).then_inc(sem(q + "act"), 1)
                    act.wait_ge(sem(q + "pe"), count(k, q, "pe", "back", p))
                    act.copy(back, bank(7)[:, 0:T]).then_inc(sem(q + "act"), 1)
                    act.wait_ge(sem(q + "pe"), count(k, q, "pe", "hid", p))
                    m = HC[k] * P // 2
                    act.copy(hid[:, m:2 * m], bank(7)[:, T:T + m]).then_inc(sem(q + "act"), 1)
                    stage(act, k, q, n, s0, "down")
                    act.copy(y, bank(4)).then_inc(sem(q + "act"), 1)

                with act.Fori(0, E // PAIR[k]) as n:
                    for u in range(PAIR[k]):
                        one(f"m{k}_", n * PAIR[k] + u, n, PER[k] * u)
                act.wait_ge(sem("list"), k + 1)
                n = act.value_load(lst[0:1, 0:1], min_val=0, max_val=NLIST)
                with act.If(n > 0):
                    with act.Fori(0, n) as p:
                        one(f"o{k}_", p)
                act.wait_ge(sem("moe_sum"), k + 1)
                act.copy(h[:, 1, :], ps[:, 2:4, :]).then_inc(sem("moe_out"), 1)

            experts(0, lambda: act.wait_ge(sem("residual"), 4))

            norm(G_NORM, lambda: act.wait_ge(sem("moe_out"), 2))
            act.wait_ge(sem("p_turned"), 1)
            act.copy(pT, bank(0).rearrange("p (c t) -> p c t", c=2)).then_inc(sem("p_copied"), 1)
            for b in range(4):
                n, a = b // 2, b % 2
                act.wait_ge(sem("dense2"), b + 1)
                act.activation(xs[:, a, 512 * n:512 * (n + 1)], bank(4 + b), ACT.Sigmoid).then_inc(sem("ple_gate"), 1)
            for a in range(TT):
                act.wait_ge(sem("dense2"), 6 + 2 * a)
                act.activation(junk2[:, a, :], ps[:, 2 * a:2 * a + 2, :].rearrange("p b n -> p (b n)"), ACT.Square,
                               accum_out=ss[:, a:a + 1]).then_inc(sem("emb_sumsq"), 1)
            act.wait_ge(sem("mean_sq"), EMB_NTH)
            act.activation(rt, ms, ACT.Sqrt).then_inc(sem("root"), 1)

            norm(N1_NORM, lambda: act.wait_ge(sem("embedded"), 2))

            def leave(i):
                act.wait_ge(sem("dense2"), 9 + i)
                b, a = bank(i % 4), i % 2
                half = Z[:, a, 0:0]
                if i < 2:
                    ins = act.copy(Z[:, a, 0:512].rearrange("p (i j d) -> p j i d", i=4, j=2),
                                   b.rearrange("p (j i d) -> p j i d", j=2, i=4))
                elif i < 4:
                    ins = act.copy(Z[:, a, 512:768], b[:, 0:256])
                elif i < 6:
                    ins = act.copy(hq[:, 512 * a:512 * (a + 1)], b)
                elif i < 8:
                    ins = act.activation(fg[:, 512 * a:512 * (a + 1)], b, ACT.Sigmoid)
                elif i < 12:
                    lo = 768 + 512 * ((i - 8) // 2)
                    ins = act.copy(Z[:, a, lo:lo + 512], b)
                else:
                    lo = 1792 + 512 * ((i - 12) // 2)
                    ins = act.activation(Z[:, a, lo:lo + 512], b, ACT.Sigmoid)
                ins.then_inc(sem("d2_copied"), 1)

            for i in range(4):
                leave(i)
            act.wait_ge(sem("mean_sq"), QK2_NTH)
            act.activation(qrt[:, 0:20], qms[:, 0:20], ACT.Sqrt).then_inc(sem("root"), 1)
            for i in range(4, 8):
                leave(i)
            act.wait_ge(sem("lb_diff"), 1)
            act.activation(lb[:, 0, :], lb[:, 2, :], ACT.Sigmoid).then_inc(sem("lb_sig"), 1)
            act.wait_ge(sem("d2_copied"), 6)
            act.activation(xs[:, 0, :], hq, ACT.Sigmoid).then_inc(sem("q_sig"), 1)
            for i in range(8, 12):
                leave(i)
            act.wait_ge(sem("d2_copied"), 12)
            for a in range(TT):
                act.activation(xs[:, 1, 512 * a:512 * (a + 1)], Z[:, a, 1280:1792], ACT.Sigmoid).then_inc(sem("g_sig"), 1)
            act.wait_ge(sem("row_max"), 3)
            for g in range(8):
                act.activation(sA0[:, g, :], sA0[:, g, :], ACT.Exp, bias=qss[:, g:g + 1],
                               accum_out=qms[:, g:g + 1]).then_inc(sem("probs"), 1)
            for i in range(12, 16):
                leave(i)
            act.wait_ge(sem("row_max"), 4)
            for g in range(8):
                act.activation(sA1[:, g, :], sA1[:, g, :], ACT.Exp, bias=qss[:, 8 + g:9 + g],
                               accum_out=qms[:, 8 + g:9 + g]).then_inc(sem("probs"), 1)
            act.activation(qrt[:, 0:16], qrt[:, 0:16], ACT.Exp).then_inc(sem("sink_exp"), 1)
            for i in range(16, 20):
                leave(i)
            act.wait_ge(sem("hgrn_o"), 1)
            act.copy(w_b[:, 0:512], bank(4)).then_inc(sem("oT_act"), 1)
            act.wait_ge(sem("mean_sq"), HG_NTH)
            act.activation(qrt[:, 0:8], qms[:, 0:8], ACT.Sqrt).then_inc(sem("root"), 1)
            for b in (1, 3):
                act.wait_ge(sem("mix_turned"), 4 + b + 1)
                act.copy(xT[:, 4:8, (b // 2) * P:(b // 2 + 1) * P],
                         bank(b).rearrange("p (g t) -> p g t", g=4)).then_inc(sem("mix_copied_act"), 1)

            experts(1, lambda: act.wait_ge(sem("residual"), 8))

        @block.vector
        def _(dve):
            done = [0]

            def step(ins):
                ins.then_inc(sem("dve_chain"), 1)
                done[0] += 1
                dve.wait_ge(sem("dve_chain"), done[0])

            tt, ts, stt = dve.tensor_tensor, dve.tensor_scalar, dve.scalar_tensor_tensor

            dve.wait_ge(sem("consts"), 1)
            dve.wait_ge(sem("pos_loaded"), 32)
            step(dve.tensor_copy(posf[:, :], posi[:, :]))
            step(tt(ang[:, :, :], posf[:, :, None].broadcast_to([P, 4, 8]),
                    freq[:, None, :].broadcast_to([P, 4, 8]), ALU.mult))
            turns = tmp[:, 0:64].rearrange("p (f s k) -> p f s k", f=2, s=4)
            big = float(1.5 * 2 ** 23)
            for f, shift in enumerate((0.0, 0.25)):
                step(ts(turns[:, f], ang[:, :, :], 1.0 / (2 * math.pi), shift, ALU.mult, ALU.add))
            step(ts(turns, turns, big, None, ALU.add))
            step(ts(turns, turns, -big, None, ALU.add))
            for f in range(2):
                step(tt(red[:, f], ang[:, :, :], ang[:, :, :], ALU.max))
            c1 = 6.28125
            c2 = float(np.float32(2 * math.pi - c1).view(np.uint32) & np.uint32(0xFFFFF000)) and \
                float((np.float32(2 * math.pi - c1).view(np.uint32) & np.uint32(0xFFFFF000)).view(np.float32))
            c3 = 2 * math.pi - c1 - c2
            for c in (c1, c2, c3):
                step(stt(out=red[:, :, :, :], in0=turns, scalar=-c, in1=red[:, :, :, :], op0=ALU.mult, op1=ALU.add))
            step(ts(red[:, 1], red[:, 1], math.pi / 2, None, ALU.add))
            pi = 3.1415925
            ts(red[:, :, :, :], red[:, :, :, :], pi, -pi, ALU.min, ALU.max).then_inc(sem("angles"), 1)

            dve.wait_ge(sem("small_loaded"), 16 * N_SMALL)
            for k in range(2):
                step(tt(lams[:, 2 * k, :], lams[:, 2 * k, :], lams[:, 2 * k + 1, :], ALU.mult))
            dve.tensor_reduce(lam[:, 0:2], lams[:, 0:4:2, :], X, ALU.add).then_inc(sem("lam_sums"), 1)
            step(ts(subln[:, :], subln[:, :], 1.0 - LAMBDA_INIT, None, ALU.mult))

            def norm(k):
                dve.wait_ge(sem("norm_sumsq"), 2 * (k + 1))
                ts(ms, ss, 1.0 / D, EPS, ALU.mult, ALU.add).then_inc(sem("mean_sq"), 1)
                dve.wait_ge(sem("root"), NORM_NTH[k])
                step(dve.reciprocal(rstd, rt))
                for a in range(TT):
                    ts(xs[:, a, :], h[:, a, :], rstd[:, a:a + 1], None, ALU.mult).then_inc(sem("norm_xs"), 1)
                for b in range(4):
                    a, half = b // 2, b % 2
                    dve.wait_ge(sem("norm_turned"), 4 * k + b + 1)
                    tt(xT[:, 4 * half:4 * half + 4, a * P:(a + 1) * P], bank(b).rearrange("p (c t) -> p c t", c=4),
                       gcol[:, k, 4 * half:4 * half + 4, None].broadcast_to([P, 4, P]), ALU.mult)\
                        .then_inc(sem("norm_xT"), 1)

            def head_rms(src, ngroup, width, junk, nth):
                step(tt(junk, src, src, ALU.mult))
                step(dve.tensor_reduce(qss[:, 0:ngroup], junk, X, ALU.add))
                ts(qms[:, 0:ngroup], qss[:, 0:ngroup], 1.0 / width, EPS, ALU.mult, ALU.add).then_inc(sem("mean_sq"), 1)
                dve.wait_ge(sem("root"), nth)
                step(dve.reciprocal(qrs[:, 0:ngroup], qrt[:, 0:ngroup]))

            def rope(view, which, ngroup):
                half = ROT // 2
                sin, cos = (trig[:, f, 2 * which:2 * which + 2, None, :].broadcast_to([P, TT, ngroup, half])
                            for f in range(2))
                t1, t2 = view[:, :, :, 0:half], view[:, :, :, half:ROT]
                r = [tmp[:, 256 * k:256 * k + TT * ngroup * half].rearrange("p (a g k) -> p a g k", a=TT, g=ngroup)
                     for k in range(4)]
                for k, (x, y) in enumerate(((t1, cos), (t2, sin), (t2, cos), (t1, sin))):
                    step(tt(r[k], x, y, ALU.mult))
                step(tt(t1, r[0], r[1], ALU.subtract))
                step(tt(t2, r[2], r[3], ALU.add))

            norm(A_NORM)
            qk = Z[:, :, 0:1024].rearrange("p a (g d) -> p a g d", d=64)
            dve.wait_ge(sem("z_copied"), 4)
            sq = scr[:, 0:2048].rearrange("p (a g d) -> p a g d", a=2, g=16)
            step(tt(sq, qk, qk, ALU.mult))
            step(dve.tensor_reduce(qss[:, 0:32].rearrange("p (a g) -> p a g", a=2), sq, X, ALU.add))
            ts(qms, qss, 1.0 / 64, EPS, ALU.mult, ALU.add).then_inc(sem("mean_sq"), 1)
            dve.wait_ge(sem("root"), QK_NTH)
            step(dve.reciprocal(qrs, qrt))
            dve.wait_ge(sem("trig"), 1)
            for a in range(TT):
                step(tt(qk[:, a], qk[:, a], qrs[:, 16 * a:16 * a + 16, None].broadcast_to([P, 16, 64]), ALU.mult))
                for k in range(2):
                    v = qk[:, a, 8 * k:8 * k + 8, :]
                    step(tt(v, v, qkw[:, k, None, :].broadcast_to([P, 8, 64]), ALU.mult))
            rope(qk, 0, 16)
            ts(lams[:, 3, :], lams[:, 3, :], 1.0, None, ALU.mult).then_inc(sem("roped"), 1)
            for a in range(TT):
                dve.wait_ge(sem("qk_turned"), 2 * a + 2)
                dve.tensor_copy(qkT[:, 4:8, a * P:(a + 1) * P],
                                bank((7, 1)[a]).rearrange("p (g t) -> p g t", g=4)).then_inc(sem("k_copied"), 1)
            for a in range(TT):
                dve.wait_ge(sem("pool_y"), a + 1)
                tt(xs[:, a, 512:1024], bank(2 + a), pscale, ALU.mult).then_inc(sem("mix_ready"), 1)
            for c in range(2):
                dve.wait_ge(sem("scores"), c + 1)
                step(stt(out=sc0[:, 4 * c:4 * c + 4, :], in0=bank(4 + c).rearrange("p (g k) -> p g k", g=4),
                         scalar=0.125, in1=mask_own[:, None, P:2 * P].broadcast_to([P, 4, P]),
                         op0=ALU.mult, op1=ALU.add))
            dve.wait_ge(sem("z_copied"), 8)
            step(dve.tensor_reduce(qrs[:, 0:8], sc0, X, ALU.max))
            ts(qss[:, 0:8], qrs[:, 0:8], -1.0, None, ALU.mult).then_inc(sem("row_max"), 1)
            for k in range(4):
                c, hp = k % 2, k // 2
                dve.wait_ge(sem("scores"), 3 + k)
                step(stt(out=sc1[:, 4 * c + 2 * hp:4 * c + 2 * hp + 2, :],
                         in0=bank((6, 7, 0, 1)[k]).rearrange("p (g k) -> p g k", g=2),
                         scalar=0.125, in1=mask_own[:, None, :].broadcast_to([P, 2, T]),
                         op0=ALU.mult, op1=ALU.add))
            step(dve.tensor_reduce(qrs[:, 8:16], sc1, X, ALU.max))
            ts(qss[:, 8:16], qrs[:, 8:16], -1.0, None, ALU.mult).then_inc(sem("row_max"), 1)
            dve.wait_ge(sem("lam_exp"), 1)
            step(tt(lam[:, 4:5], lam[:, 3:4], lam[:, 2:3], ALU.subtract))
            step(ts(lam[:, 4:5], lam[:, 4:5], -LAMBDA_INIT, None, ALU.add))
            for a, sc, keys in ((0, sc0, P), (1, sc1, T)):
                dve.wait_ge(sem("probs"), 8 * (a + 1))
                step(dve.reciprocal(qrs[:, 8 * a:8 * a + 8], qms[:, 8 * a:8 * a + 8]))
                step(ts(qrs[:, 8 * a + 4:8 * a + 8], qrs[:, 8 * a + 4:8 * a + 8], lam[:, 4:5], None, ALU.mult))
                step(tt(sc, sc, qrs[:, 8 * a:8 * a + 8, None].broadcast_to([P, 8, keys]), ALU.mult))
                tt(sc[:, 0:4, :], sc[:, 0:4, :], sc[:, 4:8, :], ALU.add).then_inc(sem("w_ready"), 1)
            for k in (0, 2):
                dve.wait_ge(sem("w_turned"), k + 1)
                dve.tensor_copy(wT[:, 4 * k:4 * k + 4, :], bank(4 + k).rearrange("p (g q) -> p g q", g=4)).then_inc(sem("w_copied_dve"), 1)
            for a in range(TT):
                dve.wait_ge(sem("pv"), a + 1)
                step(dve.tensor_copy(tmp[:, 512 * a:512 * a + 512], bank((7, 0)[a])))
            o = tmp.rearrange("p (g d) -> p g d", d=P)
            head_rms(o, 8, P, scr[:, 0:1024].rearrange("p (g d) -> p g d", d=P), SUB_NTH)
            step(tt(o, o, qrs[:, 0:8, None].broadcast_to([P, 8, P]), ALU.mult))
            for a in range(TT):
                tt(xs[:, a, 0:512].rearrange("p (g d) -> p g d", d=P), o[:, 4 * a:4 * a + 4, :],
                   subln[:, None, :].broadcast_to([P, 4, P]), ALU.mult).then_inc(sem("mix_ready"), 1)
            for b in (0, 2):
                dve.wait_ge(sem("mix_turned"), b + 1)
                dve.tensor_copy(xT[:, 0:4, (b // 2) * P:(b // 2 + 1) * P],
                                bank(1 + b).rearrange("p (g t) -> p g t", g=4)).then_inc(sem("mix_copied_dve"), 1)
            for b in range(4):
                n, a = b // 2, b % 2
                dve.wait_ge(sem("out1"), b + 1)
                v = h[:, a, 512 * n:512 * n + 512]
                tt(v, bank((5, 6, 7, 0)[b]), v, ALU.add).then_inc(sem("residual"), 1)

            def experts(k):
                norm((F_NORM, N2_NORM)[k])
                off = NR[k] - E
                dve.wait_ge(sem("logits"), k + 1)
                dve.wait_ge(sem("router_loaded"), 16 * (4, 6)[k])
                step(tt(logit[:, :, 0:NR[k]], bank(4)[:, 0:TT * NR[k]].rearrange("p (a e) -> p a e", a=TT),
                        (brt, brt2)[k][:, None, 0:NR[k]].broadcast_to([P, TT, NR[k]]), ALU.add))
                lg = logit[:, :, off:off + E]
                if k == 1:
                    for a in range(TT):
                        grp = logit[:, a, 0:4]
                        step(dve.tensor_reduce(few[:, 4 + a:5 + a], grp, X, ALU.max))
                        step(ts(eqs[:, a, 0:4], grp, few[:, 4 + a:5 + a], None, ALU.is_equal))
                        step(dve.tensor_tensor_scan(pre[:, a, 0:4], ones[:, 0:4], eqs[:, a, 0:4], 0.0, ALU.mult, ALU.add))
                        step(ts(pre[:, a, 0:4], pre[:, a, 0:4], 1.0, None, ALU.is_le))
                        step(tt(msk[:, a, 0:4], pre[:, a, 0:4], eqs[:, a, 0:4], ALU.mult))
                        le = lg[:, a].rearrange("p (g e) -> p g e", g=4)
                        gm = msk[:, a, 0:4, None].broadcast_to([P, 4, 8])
                        step(tt(le, le, gm, ALU.mult))
                        step(ts(msk[:, a, 0:4], msk[:, a, 0:4], 1.0, -NEG, ALU.subtract, ALU.mult))
                        step(tt(le, le, gm, ALU.add))
                    ts(few[:, 8:10], few[:, 4:6], -1.0, None, ALU.mult).then_inc(sem("group_max"), 1)
                for a in range(TT):
                    step(dve.max(top[:, a], lg[:, a]))
                    last = top[:, a, TOPK[k] - 1:TOPK[k]]
                    step(ts(msk[:, a], lg[:, a], last, None, ALU.is_gt))
                    step(ts(eqs[:, a], lg[:, a], last, None, ALU.is_equal))
                    step(dve.tensor_reduce(few[:, 2 + a:3 + a], msk[:, a], X, ALU.add))
                    step(dve.tensor_tensor_scan(pre[:, a], ones[:, 0:E], eqs[:, a], few[:, 2 + a:3 + a], ALU.mult, ALU.add))
                    step(ts(pre[:, a], pre[:, a], float(TOPK[k]), None, ALU.is_le))
                    step(tt(eqs[:, a], eqs[:, a], pre[:, a], ALU.mult))
                    tt(msk[:, a], msk[:, a], eqs[:, a], ALU.add).then_inc(sem("chosen"), 1)
                ts(few[:, 0:TT], top[:, :, 0], -1.0, None, ALU.mult).then_inc(sem("top"), 1)
                dve.wait_ge(sem("gate_exp"), 2 * k + TT)
                dve.wait_ge(sem("chosen"), 2 * k + TT)
                step(tt(gat[:, :, :], gat[:, :, :], msk[:, :, :], ALU.mult))
                step(dve.tensor_reduce(few[:, 2:4], gat[:, :, :], X, ALU.add))
                if k == 1:
                    dve.wait_ge(sem("group_exp"), TT)
                    step(tt(few[:, 2:4], few[:, 2:4], few[:, 12:14], ALU.mult))
                step(dve.reciprocal(few[:, 6:8], few[:, 2:4]))
                tt(gat[:, :, :], gat[:, :, :], few[:, 6:8, None].broadcast_to([P, TT, E]), ALU.mult)\
                    .then_inc(sem("gates"), 1)
                dve.wait_ge(sem("ranks"), k + 1)
                base = pre
                rk = bank(5)[:, 0:TT * E].rearrange("p (a e) -> p a e", a=TT)
                step(stt(out=base, in0=rk, scalar=1.0, in1=msk[:, :, :], op0=ALU.add, op1=ALU.mult))
                for r in range(ROUNDS):
                    step(ts(rank[:, :, E * r:E * (r + 1)], base, -1.0 - CAP * r, None, ALU.add))
                cnt, extra, start = few[0:E, 16:17], few[0:E, 17:18], few[0:E, 18:19]
                step(dve.tensor_copy(cnt, bank(5)[0:E, 64:65]))
                step(ts(few[0:E, 20:20 + ROUNDS - 1], thr[0:E, :], cnt, None, ALU.is_lt))
                dve.tensor_reduce(extra, few[0:E, 20:20 + ROUNDS - 1], X, ALU.add).then_inc(sem("extra"), 1)
                dve.wait_ge(sem("starts"), k + 1)
                step(dve.tensor_copy(start, bank(5)[0:E, 72:73]))
                dve.wait_ge(sem("extra"), k + 1)
                step(tt(few[0:E, 19:20], start, extra, ALU.add))
                within = few[0:E, 32:48]
                step(ts(few[0:E, 48:64], iota[0:E, 0:NLIST], few[0:E, 19:20], None, ALU.is_lt))
                step(ts(within, iota[0:E, 0:NLIST], start, None, ALU.is_ge))
                tt(within, within, few[0:E, 48:64], ALU.mult).then_inc(sem("within"), 1)
                dve.wait_ge(sem("rows"), k + 1)
                row = few[0:1, 64:112]
                step(dve.tensor_copy(row[:, 0:33], bank(5)[0:1, 96:129]))
                r1 = row[:, 17:33]
                step(tt(r1, iota[0:1, 0:NLIST], r1, ALU.subtract))
                step(ts(r1, r1, 1.0, float(E), ALU.add, ALU.mult))
                step(tt(r1, r1, row[:, 1:17], ALU.add))
                step(ts(r1, r1, float(ROUNDS * E - 1), None, ALU.min))
                dve.tensor_copy(lst[0:1, 0:33], row[:, 0:33]).then_inc(sem("list"), 1)

                def choose(q, e, r):
                    for a in range(TT):
                        ts(one_hot[:, a], iota[:, :], rank[:, a, ds(r, 1)], None, ALU.is_equal).then_inc(sem(q + "dve"), 1)
                    if k == 0:
                        dve.tensor_copy(pick_bias, ident[0:E, ds(e, 1)].broadcast_to([E, CAP])).then_inc(sem(q + "dve"), 1)

                def gather(q, p):
                    dve.wait_ge(sem(q + "gathered"), p + 1)
                    tt(picked.rearrange("p (c s) -> p c s", c=DC), bank(6).rearrange("p (c s) -> p c s", c=DC),
                       gcol[:, (F_NORM, N2_NORM)[k], :, None].broadcast_to([P, DC, CAP]), ALU.mult)\
                        .then_inc(sem(q + "dve"), 1)

                def gate(q, p, e, r):
                    for a in range(TT):
                        ts(gated[:, a], iota[:, None, :].broadcast_to([P, 2, CAP]), rank[:, a, ds(r, 1)],
                           gat[:, a, ds(e, 1)], ALU.is_equal, ALU.mult).then_inc(sem(q + "dve"), 1)

                def activate(q, p, n, s0):
                    if k == 0:
                        stage(dve, k, q, n, s0, "gate")
                        ts(act_g, bank(4), 7.0, None, ALU.min).then_inc(sem(q + "dve"), 1)
                        stage(dve, k, q, n, s0, "up")
                        ts(act_h, bank(5), 7.0, -7.0, ALU.min, ALU.max).then_inc(sem(q + "dve"), 1)
                        dve.wait_ge(sem(q + "dve"), count(k, q, "dve", "gate_min", p))
                        dve.wait_ge(sem(q + "dve"), count(k, q, "dve", "clip", p))
                        stt(out=act_h, in0=act_h, scalar=1.0, in1=act_g, op0=ALU.add, op1=ALU.mult)\
                            .then_inc(sem(q + "dve"), 1)
                        dve.wait_ge(sem(q + "dve"), count(k, q, "dve", "prod", p))
                        dve.wait_ge(sem(q + "act"), count(k, q, "act", "sigmoid", p))
                        tt(act_h, act_h, act_t, ALU.mult).then_inc(sem(q + "dve"), 1)
                    else:
                        dve.wait_ge(sem(q + "act"), count(k, q, "act", "sigmoid", p))
                        tt(act_g[:, 0:256], act_t[:, 0:256], bank(4)[:, 0:256], ALU.mult).then_inc(sem(q + "dve"), 1)
                        dve.wait_ge(sem(q + "dve"), count(k, q, "dve", "prod", p))
                        tt(act_h[:, 0:256], act_g[:, 0:256], bank(4)[:, 256:512], ALU.mult).then_inc(sem(q + "dve"), 1)

                def leave(q, p):
                    dve.wait_ge(sem(q + "pe"), count(k, q, "pe", "hid", p))
                    m = HC[k] * P
                    dve.tensor_copy(hid[:, 0:m // 2], bank(5)[:, 0:m // 2]).then_inc(sem(q + "hid_dve"), 1)

                q = f"m{k}_"
                dve.wait_ge(sem("gates"), k + 1)
                choose(q, 0, 0)
                gather(q, 0)
                with dve.Fori(0, E // PAIR[k]) as n:
                    for u in range(PAIR[k]):
                        p = n * PAIR[k] + u
                        gate(q, p, p, p)
                        activate(q, p, n, PER[k] * u)
                        choose(q, p + 1, p + 1)
                        gather(q, p + 1)
                        leave(q, p)
                n = dve.value_load(lst[0:1, 0:1], min_val=0, max_val=NLIST)
                dve.wait_ge(sem(q + "dve"), count(k, q, "dve", "picked", E))
                q = f"o{k}_"
                with dve.If(n > 0):
                    with dve.Fori(0, n) as p:
                        e = dve.value_load(lst[0:1, ds(p + 1, 1)], min_val=0, max_val=E - 1)
                        r = dve.value_load(lst[0:1, ds(p + 17, 1)], min_val=0, max_val=ROUNDS * E - 1)
                        choose(q, e, r)
                        gather(q, p)
                        gate(q, p, e, r)
                        activate(q, p, p, 0)
                        leave(q, p)
                        dve.wait_ge(sem(q + "pe"), count(k, q, "pe", "scattered", p))
                dve.wait_ge(sem("moe_sum"), k + 1)
                dve.tensor_copy(h[:, 0, :], ps[:, 0:2, :]).then_inc(sem("moe_out"), 1)

            experts(0)

            norm(G_NORM)
            dve.wait_ge(sem("emb_sumsq"), 2)
            ts(ms, ss, 1.0 / D, EPS, ALU.mult, ALU.add).then_inc(sem("mean_sq"), 1)
            dve.wait_ge(sem("root"), EMB_NTH)
            step(dve.reciprocal(rstd, rt))
            dve.wait_ge(sem("ple_gate"), 4)
            for a in range(TT):
                step(stt(out=emb[:, a, :], in0=ps[:, 2 * a:2 * a + 2, :].rearrange("p b n -> p (b n)"),
                         scalar=rstd[:, a:a + 1], in1=post, op0=ALU.mult, op1=ALU.mult))
                step(tt(emb[:, a, :], emb[:, a, :], xs[:, a, :], ALU.mult))
                tt(h[:, a, :], h[:, a, :], emb[:, a, :], ALU.add).then_inc(sem("embedded"), 1)
            tt(lb[:, 2, :], lbc[:, 0, :], lbc[:, 1, :], ALU.subtract).then_inc(sem("lb_diff"), 1)

            norm(N1_NORM)
            dve.wait_ge(sem("d2_copied"), 4)
            qk2 = Z[:, :, 0:640].rearrange("p a (g d) -> p a g d", d=64)
            sq2 = scr[:, 4352:5632].rearrange("p (a g d) -> p a g d", a=TT, g=10)
            step(tt(sq2, qk2, qk2, ALU.mult))
            step(dve.tensor_reduce(qss[:, 0:20].rearrange("p (a g) -> p a g", a=TT), sq2, X, ALU.add))
            ts(qms[:, 0:20], qss[:, 0:20], 1.0 / 64, EPS, ALU.mult, ALU.add).then_inc(sem("mean_sq"), 1)
            dve.wait_ge(sem("root"), QK2_NTH)
            step(dve.reciprocal(qrs[:, 0:20], qrt[:, 0:20]))
            for a in range(TT):
                step(tt(qk2[:, a], qk2[:, a], qrs[:, 10 * a:10 * a + 10, None].broadcast_to([P, 10, 64]), ALU.mult))
                for v, k, n in ((qk2[:, a, 0:8, :], 0, 8), (qk2[:, a, 8:10, :], 1, 2)):
                    step(tt(v, v, qkw2[:, k, None, :].broadcast_to([P, n, 64]), ALU.mult))
            rope(qk2, 1, 10)
            ts(lams[:, 3, :], lams[:, 3, :], 1.0, None, ALU.mult).then_inc(sem("roped"), 1)
            for k in range(3):
                dve.wait_ge(sem("qk_turned"), 4 + k + 1)
                if k < 2:
                    ins = dve.tensor_copy(qT2[:, :, k * P:(k + 1) * P], bank(4 + k).rearrange("p (i t) -> p i t", i=4))
                else:
                    ins = dve.tensor_copy(kT2, bank(6)[:, 0:T])
                ins.then_inc(sem("qk2_copied"), 1)
            dve.wait_ge(sem("lb_sig"), 1)
            dve.wait_ge(sem("d2_copied"), 8)
            step(ts(lb[:, 1, :], lb[:, 0, :], -1.0, 1.0, ALU.mult, ALU.add))
            for i in range(4):
                v = fg[:, T * i:T * (i + 1)]
                step(ts(v, v, lb[:, 1, i:i + 1], lb[:, 0, i:i + 1], ALU.mult, ALU.add))
            dve.wait_ge(sem("q_sig"), 1)
            step(tt(hq, hq, xs[:, 0, :], ALU.mult))
            for k in range(2):
                dve.wait_ge(sem("scores"), 6 + k + 1)
                stt(out=sA0[:, 4 * k:4 * k + 4, :], in0=bank(4 + k).rearrange("p (g k) -> p g k", g=4), scalar=0.125,
                    in1=mask_win[:, None, P:T].broadcast_to([P, 4, P]), op0=ALU.mult, op1=ALU.add)\
                    .then_inc(sem("scores2_copied"), 1)
            for k in range(4):
                kv, half = k % 2, k // 2
                dve.wait_ge(sem("scores"), 6 + 3 + k)
                g = 4 * kv + 2 * half
                stt(out=sA1[:, g:g + 2, :], in0=bank((6, 7, 4, 5)[k]).rearrange("p (g k) -> p g k", g=2), scalar=0.125,
                    in1=mask_win[:, None, :].broadcast_to([P, 2, T]), op0=ALU.mult, op1=ALU.add)\
                    .then_inc(sem("scores2_copied"), 1)
            dve.wait_ge(sem("scores2_copied"), 6)
            for a, sc in enumerate((sA0, sA1)):
                m = qrs[:, 8 * a:8 * a + 8]
                step(dve.tensor_reduce(m, sc, X, ALU.max))
                step(tt(m, m, sinks[:, :], ALU.max))
                step(tt(qrt[:, 8 * a:8 * a + 8], sinks[:, :], m, ALU.subtract))
                ts(qss[:, 8 * a:8 * a + 8], m, -1.0, None, ALU.mult).then_inc(sem("row_max"), 1)
            dve.wait_ge(sem("g_sig"), 2)
            for a in range(TT):
                v = Z[:, a, 1280:1792]
                step(tt(v, v, xs[:, 1, 512 * a:512 * (a + 1)], ALU.mult))
            for k in range(6):
                dve.wait_ge(sem("w_turned"), 3 + k + 1)
                dve.tensor_copy(pT2[:, 4 * k:4 * k + 4, :], bank(4 + k % 4).rearrange("p (g q) -> p g q", g=4))\
                    .then_inc(sem("p2_copied"), 1)
            dve.wait_ge(sem("probs"), 32)
            dve.wait_ge(sem("sink_exp"), 1)
            step(tt(qms[:, 0:16], qms[:, 0:16], qrt[:, 0:16], ALU.add))
            step(dve.reciprocal(qrs[:, 0:16], qms[:, 0:16]))
            for a in range(TT):
                dve.wait_ge(sem("pv"), 2 + a + 1)
                tt(ao[:, a, :].rearrange("p (g d) -> p g d", d=64), bank(6 + a).rearrange("p (g d) -> p g d", d=64),
                   qrs[:, 8 * a:8 * a + 8, None].broadcast_to([P, 8, 64]), ALU.mult).then_inc(sem("ao_ready"), 1)
            for a in range(TT):
                dve.wait_ge(sem("ao_turned"), a + 1)
                dve.tensor_copy(Z[:, a, 0:512], bank(4 + a)).then_inc(sem("ao_copied"), 1)

            step(ts(k1, fg, -1.0, 1.0, ALU.mult, ALU.add))
            f_b, k_b, r_b = (v.rearrange(by_sub, j=SUB) for v in (fg, k1, r_q))
            pf_b, sf_b = (v.rearrange(by_sub, j=SUB) for v in (pre_f, suf_f))
            wa_b, wb_b = (v.rearrange(by_sub, j=SUB) for v in (w_a, w_b))
            step(dve.tensor_copy(w_a, fg))
            step(dve.memset(w_b, 0.0))
            step(dve.memset(wa_b[:, :, 0:1], 0.0))
            step(dve.tensor_copy(wb_b[:, :, 0:1], f_b[:, :, 0:1]))
            step(dve.tensor_tensor_scan(pre_f, w_a, w_b, 0.0, ALU.mult, ALU.add))
            step(tt(q_e, hq, pre_f, ALU.mult))
            step(dve.memset(sf_b[:, :, SUB - 1:SUB], 1.0))
            for j in range(SUB - 1, 0, -1):
                step(tt(sf_b[:, :, j - 1:j], sf_b[:, :, j:j + 1], f_b[:, :, j:j + 1], ALU.mult))
            tt(suf_f, suf_f, k1, ALU.mult).then_inc(sem("ke_ready"), 1)
            dve.memset(w_a, 0.0).then_inc(sem("w_zero"), 1)
            dve.memset(w_b, 0.0).then_inc(sem("w_zero"), 1)
            step(dve.tensor_copy(r_q, hq))
            dve.wait_ge(sem("w_zero"), 2)
            nb = TT * P * 4 // SUB
            for n, j in enumerate(range(SUB - 1, -1, -1)):
                if j < SUB - 1:
                    v = r_b[:, :, j + 1:SUB]
                    step(tt(v, v, f_b[:, :, j + 1:j + 2].broadcast_to([P, nb, SUB - 1 - j]), ALU.mult))
                if n >= 2:
                    dve.wait_ge(sem("w_used"), n - 1)
                buf = (wa_b, wb_b)[n % 2]
                tt(buf[:, :, j:SUB], r_b[:, :, j:SUB], k_b[:, :, j:j + 1].broadcast_to([P, nb, SUB - j]), ALU.mult)\
                    .then_inc(sem("w_offset"), 1)
            dve.wait_ge(sem("parity"), 1)
            for a in range(TT):
                dve.wait_ge(sem("ke_turned"), a + 1)
                for v, k in ((ke_even, 0), (ke_odd, 1)):
                    ts(v[:, 512 * a:512 * (a + 1)], bank(7 if a == 0 else 5), par[:, k:k + 1], None, ALU.mult)\
                        .then_inc(sem("ke_copied"), 1)
            dve.wait_ge(sem("w_used"), SUB)
            for a in range(TT):
                tt(r_q[:, 512 * a:512 * (a + 1)].rearrange("p (h b j) -> p h b j", h=4, j=SUB),
                   bank(6)[:, 64 * a:64 * (a + 1)].rearrange("p (h j) -> p h j", h=4)[:, :, None, :].broadcast_to([P, 4, P // SUB, SUB]),
                   blk[:, :].rearrange("p (b j) -> p b j", j=SUB)[:, None, :, :].broadcast_to([P, 4, P // SUB, SUB]),
                   ALU.mult).then_inc(sem("intra"), 1)
            for a in range(TT):
                dve.wait_ge(sem("intra_turned"), a + 1)
                dve.tensor_copy(w_a[:, 512 * a:512 * (a + 1)], bank(4 + a)).then_inc(sem("intra_copied"), 1)
            for i in range(NSUB - 1):
                dve.wait_ge(sem("update"), i + 1)
                if i >= 4:
                    dve.wait_ge(sem("inter"), i - 3)
                new, old = states[:, (i + 1) % 4, :], states[:, i % 4, :]
                if i == 0:
                    dve.tensor_copy(new, bank(6)).then_inc(sem("state"), 4)
                    continue
                dve.wait_ge(sem("state"), 4 * i)
                for n in range(4):
                    r = slice(n * P, (n + 1) * P)
                    stt(out=new[:, r], in0=old[:, r], scalar=pre_f[:, n * T + SUB * i + SUB - 1:n * T + SUB * i + SUB],
                        in1=bank(6 + i % 2)[:, r], op0=ALU.mult, op1=ALU.add).then_inc(sem("state"), 1)
            dve.wait_ge(sem("hgrn_o"), 2)
            dve.tensor_copy(w_b[:, 512:1024], bank(5)).then_inc(sem("oT_dve"), 1)
            for a in range(TT):
                dve.wait_ge(sem("o_turned"), a + 1)
                step(dve.tensor_copy(k1[:, 512 * a:512 * (a + 1)], bank(6 + a)))
            o = k1.rearrange("p (g d) -> p g d", d=P)
            head_rms(o, 8, P, pre_f.rearrange("p (g d) -> p g d", d=P), HG_NTH)
            step(tt(o, o, qrs[:, 0:8, None].broadcast_to([P, 8, P]), ALU.mult))
            step(tt(o, o, hnorm[:, None, :].broadcast_to([P, 8, P]), ALU.mult))
            for a in range(TT):
                v = k1[:, 512 * a:512 * (a + 1)]
                tt(v, v, Z[:, a, 1280:1792], ALU.mult).then_inc(sem("hg_ready"), 1)
            for b in range(4):
                a, n = b // 2, b % 2
                dve.wait_ge(sem("dense2"), 29 + b)
                r = slice(512 * n, 512 * (n + 1))
                tt(xs[:, a, r], bank(b), Z[:, a, 1792 + 512 * n:2304 + 512 * n], ALU.mult).then_inc(sem("branch_a"), 1)
            for a in range(TT):
                dve.wait_ge(sem("hg_turned"), a + 1)
                dve.tensor_copy(Z[:, a, 768:1280], bank(4 + a)).then_inc(sem("hg_copied"), 1)
            dve.wait_ge(sem("branch_a"), 4)
            for b in range(4):
                a, n = b // 2, b % 2
                dve.wait_ge(sem("dense2"), 33 + b)
                r = slice(512 * n, 512 * (n + 1))
                t = scr[:, 2048 + 512 * b:2560 + 512 * b]
                step(tt(t, bank((6, 7, 4, 5)[b]), Z[:, a, 2816 + 512 * n:3328 + 512 * n], ALU.mult))
                tt(xs[:, a, r], xs[:, a, r], t, ALU.add).then_inc(sem("mixed"), 1)
            for b in (0, 2):
                dve.wait_ge(sem("mix_turned"), 4 + b + 1)
                dve.tensor_copy(xT[:, 0:4, (b // 2) * P:(b // 2 + 1) * P],
                                bank(b).rearrange("p (g t) -> p g t", g=4)).then_inc(sem("mix_copied_dve"), 1)
            for b in range(4):
                n, a = b // 2, b % 2
                dve.wait_ge(sem("dense2"), 37 + b)
                v = h[:, a, 512 * n:512 * n + 512]
                tt(v, bank(4 + b), v, ALU.add).then_inc(sem("residual"), 1)

            experts(1)

        @block.tensor
        def _(pe):
            def turn(dst, src, c, stride, n, who):
                for i in range(n):
                    last = pe.transpose(dst[:, i * P:(i + 1) * P], src[:, c + i:c + i + stride * (P - 1) + 1:stride], ident[:, :])
                last.then_inc(sem(who), 1)

            def norm(k):
                for b in range(4):
                    if b % 2 == 0:
                        pe.wait_ge(sem("norm_xs"), 2 * k + b // 2 + 1)
                    turn(bank(b), xs[:, b // 2, :], 4 * (b % 2), DC, 4, "norm_turned")

            pe.wait_ge(sem("consts"), 1)
            norm(A_NORM)
            pe.wait_ge(sem("norm_xT"), 4)
            for j in range(8):
                u, a = j // 2, j % 2
                pe.wait_ge(full[u], 16)
                for c in range(DC):
                    last = pe.matmul(bank((4 + j) % 8), xT[:, c, a * P:(a + 1) * P], slot(u, DC, 512)[:, c, :],
                                     start=c == 0, stop=c == DC - 1)
                last.then_inc(sem("proj"), 1)
            pe.wait_ge(sem("z_copied"), 8)
            pe.wait_ge(sem("small_loaded"), 16 * N_SMALL)
            for g in range(4):
                for s in range(2):
                    last = pe.matmul(bank(4 + g // 2)[:, (g % 2) * T:(g % 2 + 1) * T],
                                     Z[:, s, 1536 + g * P:1536 + (g + 1) * P], poolM[:, s, g, :],
                                     start=s == 0, stop=s == 1)
            last.then_inc(sem("pooled"), 1)
            pe.wait_ge(sem("roped"), 1)
            for k in range(4):
                for i in range(4):
                    lo = 512 * (k % 2) + P * i
                    last = pe.transpose(bank((6, 7, 0, 1)[k])[:, i * P:(i + 1) * P], Z[:, k // 2, lo:lo + P], ident[:, :])
                last.then_inc(sem("qk_turned"), 1)
            pe.wait_ge(sem("pool_copied"), 2)
            for a in range(TT):
                for g in range(4):
                    last = pe.matmul(bank(2 + a)[:, g * P:(g + 1) * P], poolT[:, g, a * P:(a + 1) * P], wpool[:, g, :],
                                     start=True, stop=True)
                last.then_inc(sem("pool_y"), 1)
            pe.wait_ge(sem("q_copied"), 2)
            pe.wait_ge(sem("k_copied"), 2)
            lasts = {}
            for i in range(4):
                for c in range(2):
                    r = slice(64 * c, 64 * c + 64)
                    last = pe.matmul(bank(4 + c)[:, i * P:(i + 1) * P], qkT[r, i, 0:P], qkT[r, 4 + i, 0:P],
                                     start=True, stop=True)
                    if i == 3:
                        last.then_inc(sem("scores"), 1)
            for hp in range(2):
                for i in range(2):
                    for c in range(2):
                        r = slice(64 * c, 64 * c + 64)
                        last = pe.matmul(bank((6, 7, 0, 1)[2 * hp + c])[:, i * T:(i + 1) * T],
                                         qkT[r, 2 * hp + i, P:T], qkT[r, 6 + i - 2 + 2 * hp, :], start=True, stop=True)
                        if i == 1:
                            last.then_inc(sem("scores"), 1)
            for k, (a, kt) in enumerate(((0, 0), (1, 0), (1, 1))):
                pe.wait_ge(sem("w_ready"), a + 1)
                for i in range(4):
                    src = (sc0, sc1)[a][:, i, kt * P:(kt + 1) * P]
                    last = pe.transpose(bank(4 + k)[:, i * P:(i + 1) * P], src, ident[:, :])
                last.then_inc(sem("w_turned"), 1)
            pe.wait_ge(sem("w_copied_dve"), 1)
            for a in range(TT):
                if a == 1:
                    pe.wait_ge(sem("w_copied_dve"), 2)
                    pe.wait_ge(sem("w_copied_act"), 1)
                for i in range(4):
                    for kt in range(a + 1):
                        last = pe.matmul(bank((7, 0)[a])[:, i * P:(i + 1) * P], wT[:, 4 * (a + kt) + i, :],
                                         Z[:, kt, 1024 + i * P:1024 + (i + 1) * P], start=kt == 0, stop=kt == a)
                last.then_inc(sem("pv"), 1)
            pe.wait_ge(sem("mix_ready"), 4)
            for b in range(4):
                turn(bank(1 + b), xs[:, b // 2, :], 4 * (b % 2), DC, 4, "mix_turned")
            pe.wait_ge(sem("mix_copied_dve"), 2)
            pe.wait_ge(sem("mix_copied_act"), 2)
            for b in range(4):
                n, a = b // 2, b % 2
                pe.wait_ge(full[4 + n], 16)
                for c in range(DC):
                    last = pe.matmul(bank((5, 6, 7, 0)[b]), xT[:, c, a * P:(a + 1) * P], slot(4 + n, DC, 512)[:, c, :],
                                     start=c == 0, stop=c == DC - 1)
                last.then_inc(sem("out1"), 1)

            def experts(k):
                norm((F_NORM, N2_NORM)[k])
                pe.wait_ge(sem("norm_xT"), 4 * (F_NORM, N2_NORM)[k] + 4)
                pe.wait_ge(sem("router_loaded"), 16 * (4, 6)[k])
                for a in range(TT):
                    for c in range(DC):
                        last = pe.matmul(bank(4)[:, NR[k] * a:NR[k] * (a + 1)], xT[:, c, a * P:(a + 1) * P],
                                         wrt[:, c, 0:NR[k]], start=c == 0, stop=c == DC - 1)
                last.then_inc(sem("logits"), 1)
                pe.wait_ge(sem("chosen"), 2 * k + TT)
                rk = bank(5)[:, 0:64]
                pe.matmul(rk[:, 0:E], tri[:, :], msk[:, 0], start=True, stop=True)
                pe.matmul(rk[:, E:2 * E], ones[:, :], msk[:, 0], start=True, stop=False)
                pe.matmul(rk[:, E:2 * E], tri[:, :], msk[:, 1], start=False, stop=True)
                for a in range(TT):
                    last = pe.matmul(bank(5)[0:E, 64:65], msk[:, a], ones[:, 0:1], start=a == 0, stop=a == TT - 1)
                last.then_inc(sem("ranks"), 1)
                if k == 0:
                    pe.wait_ge(sem("gates"), 1)
                    for a in range(TT):
                        last = pe.transpose(bank(6)[0:E, a * P:(a + 1) * P], gat[:, a], ident[:, :])
                    last.then_inc(sem("gates_turned"), 1)
                pe.wait_ge(sem("extra"), k + 1)
                pe.matmul(bank(5)[0:E, 72:73], tri[0:E, 0:E], few[0:E, 17:18], start=True, stop=True)\
                    .then_inc(sem("starts"), 1)
                pe.wait_ge(sem("within"), k + 1)
                row = bank(5)[0:1, 96:129]
                pe.matmul(row[:, 0:1], ones[0:E, 0:1], few[0:E, 17:18], start=True, stop=True)
                pe.matmul(row[:, 1:17], pcol[0:E, :], few[0:E, 32:48], start=True, stop=True)
                pe.matmul(row[:, 17:33], few[0:E, 18:19], few[0:E, 32:48], start=True, stop=True)\
                    .then_inc(sem("rows"), 1)
                if k == 0:
                    pe.wait_ge(sem("gates_copied"), 1)
                for a in range(TT):
                    for j in range(2):
                        if k == 0:
                            pe.matmul(bank(2 * a + j), y[0:E, a * P:(a + 1) * P], bias_dn[:, 512 * j:512 * (j + 1)],
                                      start=True, stop=True)
                        else:
                            pe.matmul(bank(2 * a + j), zeros[:, :], h[:, a, 512 * j:512 * (j + 1)], start=True, stop=True)

                def gather(q, p):
                    pe.wait_ge(sem(q + "dve"), count(k, q, "dve", "one_hot", p))
                    for c in range(DC):
                        for a in range(TT):
                            last = pe.matmul(bank(6)[:, c * CAP:(c + 1) * CAP], xs[:, a, c:D:DC], one_hot[:, a],
                                             start=a == 0, stop=a == TT - 1)
                    last.then_inc(sem(q + "gathered"), 1)

                def halves(dst, lhsT, rhs, start):
                    for j in range(2):
                        last = pe.matmul(dst[CAP * j:CAP * (j + 1)], lhsT, rhs(j), start=start, stop=True,
                                         skip_group_check=True)
                    return last

                def gate_up(q, p, s0, filled, freed):
                    pe.wait_ge(sem(q + "dve"), count(k, q, "dve", "picked", p))
                    if k == 0:
                        pe.wait_ge(sem(q + "dve"), count(k, q, "dve", "bias", p))
                        for i, b in enumerate((4, 5)):
                            halves(bank(b), pick_bias, lambda j: bias_gu[:, i, 512 * j:512 * (j + 1)], True)
                            for s in range(2):
                                filled(2 * i + s)
                                v = slot(s0 + 2 * i + s, 4, 1024)
                                for c in range(4):
                                    last = halves(bank(b), picked[:, (4 * s + c) * CAP:(4 * s + c + 1) * CAP],
                                                  lambda j: v[:, c, 512 * j:512 * (j + 1)], False)
                                last.then_inc(freed(2 * i + s), 1)
                        return
                    for s in range(2):
                        filled(s)
                        v = ring[:, s0 + s, :].rearrange("p (g c n) -> p g c n", g=2, c=4)
                        for c in range(4):
                            last = halves(bank(4).rearrange("p (g n) -> p g n", g=2),
                                          picked[:, (4 * s + c) * CAP:(4 * s + c + 1) * CAP],
                                          lambda j: v[:, :, c, 256 * j:256 * (j + 1)], s == 0 and c == 0)
                        last.then_inc(freed(s), 1)

                def back_turn(q, p):
                    pe.wait_ge(sem(q + "dve"), count(k, q, "dve", "gated", p))
                    for a in range(TT):
                        last = pe.transpose(bank(7)[:, a * P:(a + 1) * P], gated[:, a].rearrange("p j s -> p (j s)"), ident[:, :])
                    last.then_inc(sem(q + "pe"), 1)

                def rest(q, p, s0, filled, freed):
                    pe.wait_ge(sem(q + "dve"), count(k, q, "dve", "hidden", p))
                    pe.wait_ge(sem(q + "act"), count(k, q, "act", "back", p))
                    for c in range(HC[k]):
                        n = HC[k] // 2
                        dst = bank(5)[:, c * P:(c + 1) * P] if c < n else bank(7)[:, T + (c - n) * P:T + (c - n + 1) * P]
                        last = pe.transpose(dst, act_h[:, c:FF[k] // 2:HC[k]], ident[:, :])
                    last.then_inc(sem(q + "pe"), 1)
                    pe.wait_ge(sem(q + "act"), count(k, q, "act", "hid", p))
                    pe.wait_ge(sem(q + "hid_dve"), p + 1)
                    for g in range(2):
                        if k == 0 or g == 0:
                            filled(4 + g if k == 0 else 2)
                        v = slot(s0 + 4 + g, 4, 1024) if k == 0 else slot(s0 + 2, 4, 1024)[:, 2 * g:2 * g + 2, :]
                        for c in range(HC[k]):
                            last = halves(bank(4), hid[:, c * P + CAP * g:c * P + CAP * (g + 1)],
                                          lambda j: v[:, c, 512 * j:512 * (j + 1)], g == 0 and c == 0)
                        if k == 0 or g == 1:
                            last.then_inc(freed(4 + g if k == 0 else 2), 1)
                    pe.wait_ge(sem(q + "act"), count(k, q, "act", "y", p))
                    for a in range(TT):
                        for j in range(2):
                            last = pe.matmul(bank(2 * a + j), back[CAP * j:CAP * (j + 1), a * P:(a + 1) * P],
                                             y[CAP * j:CAP * (j + 1), :], start=False, stop=True, skip_group_check=True)
                    last.then_inc(sem(q + "pe"), 1)

                q = f"m{k}_"
                gather(q, 0)
                with pe.Fori(0, E // PAIR[k]) as n:
                    for u in range(PAIR[k]):
                        p, s0 = n * PAIR[k] + u, PER[k] * u

                        def filled(s):
                            pe.wait_ge(full[s0 + s], 16 * LOADS[k][s] * (n + 1) + 16 * FULL0[k][s0 + s])
                        gate_up(q, p, s0, filled, lambda s: free[s0 + s])
                        gather(q, p + 1)
                        back_turn(q, p)
                        rest(q, p, s0, filled, lambda s: free[s0 + s])
                pe.wait_ge(sem("list"), k + 1)
                n = pe.value_load(lst[0:1, 0:1], min_val=0, max_val=NLIST)
                q = f"o{k}_"
                with pe.If(n > 0):
                    with pe.Fori(0, n) as p:
                        def filled(s):
                            pe.wait_ge(sem(f"over_full{k}_{s}"), 16 * LOADS[k][s] * (p + 1))
                        def freed(s):
                            return sem(f"over_free{k}_{s}")
                        gather(q, p)
                        gate_up(q, p, 0, filled, freed)
                        back_turn(q, p)
                        rest(q, p, 0, filled, freed)
                for a in range(TT):
                    for j in range(2):
                        last = pe.matmul(bank(2 * a + j), ident[:, :], h[:, a, 512 * j:512 * (j + 1)], start=False,
                                         stop=True, skip_group_check=True)
                last.then_inc(sem("moe_sum"), 1)

            experts(0)

            def dense(dst, lhs, rhs, nc_):
                for c in range(nc_):
                    last = pe.matmul(dst, lhs(c), rhs(c), start=c == 0, stop=c == nc_ - 1)
                return last

            def tile(a):
                return lambda c: xT[:, c, a * P:(a + 1) * P]

            norm(G_NORM)
            pe.wait_ge(sem("norm_xT"), 4 * G_NORM + 4)
            pe.wait_ge(sem("p_loaded"), 16)
            for c in range(2):
                for a in range(TT):
                    last = pe.transpose(bank(0)[:, c * T + a * P:c * T + (a + 1) * P], p_tok[:, a, c:256:2], ident[:, :])
            last.then_inc(sem("p_turned"), 1)
            for b in range(4):
                n, a = b // 2, b % 2
                pe.wait_ge(*middle_full(n))
                v = slot(n, DC, 512)
                dense(bank(4 + b), tile(a), lambda c: v[:, c, :], DC).then_inc(sem("dense2"), 1)
            pe.wait_ge(*middle_full(2))
            pe.wait_ge(sem("p_copied"), 1)
            v_p = slot(2, 2, 1024)
            for a in range(TT):
                for n in range(2):
                    dense(bank(2 * a + n), lambda c: pT[:, c, a * P:(a + 1) * P],
                          lambda c: v_p[:, c, 512 * n:512 * (n + 1)], 2).then_inc(sem("dense2"), 1)

            norm(N1_NORM)
            pe.wait_ge(sem("norm_xT"), 4 * N1_NORM + 4)

            def project(i):
                m, a = 3 + i // 2, i % 2
                if a == 0:
                    pe.wait_ge(*middle_full(m))
                if i >= 4:
                    pe.wait_ge(sem("d2_copied"), i - 3)
                (_, _, n), _ = middle[m]
                v = slot(m % SLOTS, DC, n)
                if i in (4, 5, 6, 7):
                    for x in range(2):
                        lo = (2 * a + x) * P
                        last = dense(bank(i % 4)[:, x * T:(x + 1) * T], lambda c: v[:, c, lo:lo + P],
                                     lambda c: xT[:, c, :], DC)
                else:
                    last = dense(bank(i % 4)[:, 0:n], tile(a), lambda c: v[:, c, :], DC)
                last.then_inc(sem("dense2"), 1)

            for i in range(8):
                project(i)
            pe.wait_ge(sem("roped"), 2)
            for a in range(TT):
                for i in range(4):
                    last = pe.transpose(bank(4 + a)[:, i * P:(i + 1) * P], Z[:, a, i * P:(i + 1) * P], ident[:, :])
                last.then_inc(sem("qk_turned"), 1)
            for a in range(TT):
                last = pe.transpose(bank(6)[:, a * P:(a + 1) * P], Z[:, a, 512:640], ident[:, :])
            last.then_inc(sem("qk_turned"), 1)
            for i in range(8, 10):
                project(i)
            pe.wait_ge(sem("qk2_copied"), 3)
            for i in range(4):
                for kv in range(2):
                    r = slice(64 * kv, 64 * kv + 64)
                    last = pe.matmul(bank(4 + kv)[:, i * P:(i + 1) * P], qT2[r, i, 0:P], kT2[r, 0:P], start=True, stop=True)
                    if i == 3:
                        last.then_inc(sem("scores"), 1)
            for half in range(2):
                if half == 1:
                    pe.wait_ge(sem("scores2_copied"), 2)
                for i in range(2):
                    for kv in range(2):
                        r = slice(64 * kv, 64 * kv + 64)
                        last = pe.matmul(bank((6, 7, 4, 5)[2 * half + kv])[:, i * T:(i + 1) * T],
                                         qT2[r, 2 * half + i, P:T], kT2[r, :], start=True, stop=True)
                        if i == 1:
                            last.then_inc(sem("scores"), 1)
            for i in range(10, 16):
                project(i)
            for k in range(6):
                g0 = 4 * (k % 2)
                if k == 0:
                    pe.wait_ge(sem("scores2_copied"), 6)
                if k in (0, 2):
                    pe.wait_ge(sem("probs"), 24 if k == 0 else 32)
                if k >= 4:
                    pe.wait_ge(sem("p2_copied"), k - 3)
                for i in range(4):
                    src = sA0[:, g0 + i, :] if k < 2 else sA1[:, g0 + i, (k // 2 - 1) * P:(k // 2) * P]
                    last = pe.transpose(bank(4 + k % 4)[:, i * P:(i + 1) * P], src, ident[:, :])
                last.then_inc(sem("w_turned"), 1)
            for i in range(16, 18):
                project(i)
            pe.wait_ge(sem("p2_copied"), 6)
            for a in range(TT):
                for g in range(8):
                    for kt in range(a + 1):
                        last = pe.matmul(bank(6 + a)[:, g * 64:(g + 1) * 64], pT2[:, 8 * (a + kt) + g, :],
                                         Z[:, kt, 640 + 64 * (g // 4):704 + 64 * (g // 4)], start=kt == 0, stop=kt == a)
                last.then_inc(sem("pv"), 1)
            for a in range(TT):
                pe.wait_ge(sem("ao_ready"), a + 1)
                for c in range(4):
                    last = pe.transpose(bank(4 + a)[:, c * P:(c + 1) * P], ao[:, a, c:512:4], ident[:, :])
                last.then_inc(sem("ao_turned"), 1)
            for i in range(18, 20):
                project(i)

            pe.wait_ge(sem("ke_ready"), 1)
            pe.wait_ge(sem("ao_copied"), 2)
            for a in range(TT):
                for n in range(4):
                    last = pe.transpose(bank(7 if a == 0 else 5)[:, n * P:(n + 1) * P],
                                        suf_f[:, n * T + a * P:n * T + (a + 1) * P], ident[:, :])
                last.then_inc(sem("ke_turned"), 1)
            for n, j in enumerate(range(SUB - 1, -1, -1)):
                pe.wait_ge(sem("w_offset"), n + 1)
                buf = (w_a, w_b)[n % 2]
                for a in range(TT):
                    for x in range(4):
                        o = (4 * a + x) * SUB + j
                        last = pe.matmul(bank(6)[:, o:o + 1], buf[:, x * T + a * P:x * T + (a + 1) * P], ones[:, 0:1],
                                         start=True, stop=True)
                last.then_inc(sem("w_used"), 1)
            pe.wait_ge(sem("ke_copied"), 4)
            for a in range(TT):
                pe.wait_ge(sem("intra"), a + 1)
                for n in range(4):
                    last = pe.transpose(bank(4 + a)[:, n * P:(n + 1) * P], r_q[:, 512 * a + n * P:512 * a + (n + 1) * P], ident[:, :])
                last.then_inc(sem("intra_turned"), 1)

            def update(i):
                if i >= 2:
                    pe.wait_ge(sem("state"), 4 * (i - 1))
                a, r = i // 8, slice(32 * (i // 2 % 4), 32 * (i // 2 % 4) + 32)
                src = (ke_even, ke_odd)[i % 2]
                for n in range(4):
                    last = pe.matmul(bank(6 + i % 2)[:, n * P:(n + 1) * P], src[r, 512 * a + n * P:512 * a + (n + 1) * P],
                                     Z[r, a, 768 + n * P:768 + (n + 1) * P], start=True, stop=True)
                last.then_inc(sem("update"), 1)

            update(0)
            update(1)
            pe.wait_ge(sem("intra_copied"), 2)
            for n in range(4):
                for a in range(TT):
                    pe.matmul(bank(4 + n // 2)[:, (n % 2) * T + a * P:(n % 2) * T + (a + 1) * P],
                              Z[:, a, 768 + n * P:768 + (n + 1) * P], w_a[:, 512 * a + n * P:512 * a + (n + 1) * P],
                              start=n % 2 == 0 and a == 0, stop=True, skip_group_check=True)
            for i in range(1, NSUB):
                pe.wait_ge(sem("state"), 4 * i)
                for n in range(4):
                    lo = (n % 2) * T + SUB * i
                    last = pe.matmul(bank(4 + n // 2)[:, lo:lo + SUB], states[:, i % 4, n * P:(n + 1) * P],
                                     q_e[:, n * T + SUB * i:n * T + SUB * (i + 1)], start=False, stop=True,
                                     skip_group_check=True)
                    if i == NSUB - 1 and n % 2 == 1:
                        last.then_inc(sem("hgrn_o"), 1)
                if i < NSUB - 1:
                    last.then_inc(sem("inter"), 1)
                if i + 1 < NSUB - 1:
                    update(i + 1)
            pe.wait_ge(sem("oT_act"), 1)
            pe.wait_ge(sem("oT_dve"), 1)
            for a in range(TT):
                for n in range(4):
                    last = pe.transpose(bank(6 + a)[:, n * P:(n + 1) * P], w_b[:, n * T + a * P:n * T + (a + 1) * P], ident[:, :])
                last.then_inc(sem("o_turned"), 1)
            pe.wait_ge(*middle_full(13))
            pe.wait_ge(sem("d2_copied"), 20)
            v_a, v_h = slot(13 % SLOTS, 4, 1024), slot(14 % SLOTS, 4, 1024)
            for b in range(4):
                a, n = b // 2, b % 2
                dense(bank(b), lambda c: Z[:, a, c * P:(c + 1) * P], lambda c: v_a[:, c, 512 * n:512 * (n + 1)], 4)\
                    .then_inc(sem("dense2"), 1)
            for a in range(TT):
                pe.wait_ge(sem("hg_ready"), a + 1)
                for c in range(4):
                    last = pe.transpose(bank(4 + a)[:, c * P:(c + 1) * P], k1[:, 512 * a + c:512 * (a + 1):4], ident[:, :])
                last.then_inc(sem("hg_turned"), 1)
            pe.wait_ge(*middle_full(14))
            pe.wait_ge(sem("hg_copied"), 2)
            for b in range(4):
                a, n = b // 2, b % 2
                dense(bank((6, 7, 4, 5)[b]), lambda c: Z[:, a, 768 + c * P:768 + (c + 1) * P],
                      lambda c: v_h[:, c, 512 * n:512 * (n + 1)], 4).then_inc(sem("dense2"), 1)
            for b in range(4):
                pe.wait_ge(sem("mixed"), 2 * (b // 2) + 2)
                turn(bank(b), xs[:, b // 2, :], 4 * (b % 2), DC, 4, "mix_turned")
            pe.wait_ge(sem("mix_copied_act"), 4)
            pe.wait_ge(sem("mix_copied_dve"), 4)
            for b in range(4):
                n, a = b // 2, b % 2
                pe.wait_ge(*middle_full(15 + n))
                v = slot(3 + n, DC, 512)
                dense(bank(4 + b), tile(a), lambda c: v[:, c, :], DC).then_inc(sem("dense2"), 1)

            experts(1)


N_SMALL = 5 + 4 + 4 + 10
NAMES = ["x", "p", "positions", "attn_norm", "w_in", "q_norm", "k_norm", "lam_q1", "lam_k1", "lam_q2", "lam_k2",
         "subln", "w_pool", "pool_scale", "w_out", "ffn_norm", "w_router", "b_router", "w_gate", "b_gate", "w_up",
         "b_up", "w_down", "b_down", "ple_gate_norm", "w_ple_gate", "w_ple_proj", "ple_post_norm", "positions_2",
         "norm1_w_2", "w_in_2", "q_norm_w_2", "k_norm_w_2", "attn_sinks_2", "hgrn_lower_bounds_2", "hgrn_norm_w_2",
         "w_branch_attn_2", "w_branch_hgrn_2", "w_out_2", "norm2_w_2", "w_router_group_2", "b_router_group_2",
         "w_router_expert_2", "b_router_expert_2", "w_gate_experts_2", "w_up_experts_2", "w_down_experts_2"]


def kernel(**inputs):
    import concourse.bacc as bacc
    from concourse.bass_utils import run_bass_kernel_spmd

    nc = bacc.Bacc("TRN2", target_bir_lowering=False, num_devices=1)
    arrays, args = {}, {}
    for name in NAMES:
        a = np.ascontiguousarray(inputs[name])
        arrays["in_" + name] = a
        args[name] = nc.dram_tensor("in_" + name, a.shape, mybir.dt.from_np(a.dtype), kind="ExternalInput").ap()
    out = nc.dram_tensor("out", (1, T, D), F32, kind="ExternalOutput").ap()
    two_blocks(nc, args, out)
    r = run_bass_kernel_spmd(nc, [arrays], core_ids=[0])
    return r.results[0]["out"]
```

```python
import math
from contextlib import ExitStack

import numpy as np

import concourse.bass as bass
from concourse import mybir
from concourse.bass import ds

F32 = mybir.dt.float32
I32 = mybir.dt.int32
ALU = mybir.AluOpType
ACT = mybir.ActivationFunctionType
X = mybir.AxisListType.X

P = 128
T = 256
TT = T // P
D = 1024
DC = D // P
EPS = 1e-6
NEG = -1.0e30
E = 32
CAP = 64
ROUNDS = T // CAP
NLIST = 16
SLOTS = 6
SLOT = 4096
ROPE_THETA = 500000.0
ROT = 16
SUB = 16
NSUB = T // SUB
LAMBDA_INIT = 0.8 - 0.6 * math.exp(-0.3 * 0)
A_NORM, F_NORM, G_NORM, N1_NORM, N2_NORM = range(5)
NORM_NTH = (1, 4, 5, 7, 10)
QK_NTH, SUB_NTH, EMB_NTH, QK2_NTH, HG_NTH = 2, 3, 6, 8, 9


def two_blocks(nc, w, out):
    ctx = ExitStack()
    sems = {}

    def sem(name):
        if name not in sems:
            sems[name] = ctx.enter_context(nc.semaphore(name))
        return sems[name]

    def sb(name, shape, dt=F32):
        return ctx.enter_context(nc.sbuf_tensor(name, shape, dt))

    with ctx:
        ring = sb("ring", [P, SLOTS, SLOT])
        h = sb("h", [P, TT, D])
        xs = sb("xs", [P, TT, D])
        xT = sb("xT", [P, DC, T])
        Z = sb("Z", [P, TT, 4864])
        scr = sb("scr", [P, 9216])
        ps = ctx.enter_context(nc.psum_tensor("ps", [P, 8, 512], F32))

        ident = sb("ident", [P, P])
        zeros = sb("zeros", [P, P])
        ones = sb("ones", [P, P])
        mask_own = sb("mask_own", [P, 2 * P])
        mask_win = sb("mask_win", [P, 2 * P])
        tri = sb("tri", [P, P])
        blk = sb("blk", [P, P])
        spread = sb("spread", [P, P + SUB - 1])
        iota = sb("iota", [P, CAP])
        pcol = sb("pcol", [P, 1])
        par = sb("par", [P, 2])
        thr = sb("thr", [P, ROUNDS - 1])
        gcol = sb("gcol", [P, 5, DC])
        freq = sb("freq", [P, ROT // 2])
        posi = sb("posi", [P, 2 * TT], I32)
        posf = sb("posf", [P, 2 * TT])
        ang = sb("ang", [P, 4, 8])
        red = sb("red", [P, 2, 4, 8])
        trig = sb("trig", [P, 2, 4, 8])
        qkw = sb("qkw", [P, 2, 64])
        qkw2 = sb("qkw2", [P, 2, 64])
        lams = sb("lams", [P, 4, 64])
        subln = sb("subln", [P, P])
        brt = sb("brt", [P, E])
        brt2 = sb("brt2", [P, 36])
        sinks = sb("sinks", [P, 8])
        lbc = sb("lbc", [P, 2, 4])
        lb = sb("lb", [P, 3, 4])
        hnorm = sb("hnorm", [P, P])
        st = sb("st", [P, 160])
        lst = sb("lst", [1, 48], I32)

        def bank(k):
            return ps[:, k, :]

        ss, ms, rt, rstd = (st[:, 2 * k:2 * k + 2] for k in range(4))
        qss, qms, qrt, qrs = (st[:, 8 + 32 * k:40 + 32 * k] for k in range(4))
        lam = st[:, 136:144]

        qkT = scr[:, 0:2048].rearrange("p (g t) -> p g t", t=T)
        sc1 = scr[:, 2048:4096].rearrange("p (g k) -> p g k", k=T)
        sc0 = scr[:, 4096:5120].rearrange("p (g k) -> p g k", k=P)
        tmp = scr[:, 5120:6144]
        wT = scr[:, 6144:7680].rearrange("p (g q) -> p g q", q=P)
        poolT = scr[:, 7680:8704].rearrange("p (g t) -> p g t", t=T)
        poolM = Z[:, 0, 2048:4096].rearrange("p (s g t) -> p s g t", s=2, g=4)
        wpool = Z[:, 1, 2048:2560].rearrange("p (g d) -> p g d", g=4)
        pscale = Z[:, 1, 2560:3072]
        post = Z[:, 1, 3840:4864]

        bias_gu = Z[0:E, 0, 0:2048].rearrange("e (g n) -> e g n", g=2)
        bias_dn = Z[0:E, 0, 2048:3072]
        act_g, act_t, act_h = (Z[:, 0, 3072 + 512 * k:3584 + 512 * k] for k in range(3))
        moe = Z[:, 1, :]
        wrt = moe[:, 0:288].rearrange("p (c e) -> p c e", c=DC)
        logit = moe[:, 288:360].rearrange("p (a e) -> p a e", a=TT)
        msk, gat, eqs, pre = (moe[:, 360 + 64 * k:424 + 64 * k].rearrange("p (a e) -> p a e", a=TT) for k in range(4))
        rank = moe[:, 616:872].rearrange("p (a r) -> p a r", a=TT)
        top = moe[:, 872:888].rearrange("p (a k) -> p a k", a=TT)
        few = moe[:, 888:1000]
        one_hot = moe[:, 1000:1128].rearrange("p (a s) -> p a s", a=TT)
        gated = moe[:, 1128:1384].rearrange("p (a j s) -> p a j s", a=TT, j=2)
        back = moe[:, 1384:1640]
        picked = moe[:, 1640:2152]
        hid = moe[:, 2152:2664]
        y = moe[:, 2664:3176]
        pick_bias = moe[0:E, 3176:3176 + CAP]
        gates_T = moe[0:E, 3240:3240 + T]
        rows = moe[:, 3176:3688]

        def cols(name, lo, n):
            src = w[name][0].rearrange("(p c) n -> p c n", p=P)
            return src[:, :, lo:lo + n], src.shape[1], n

        front = [cols("w_in", 512 * k, 512) for k in range(4)] + [cols("w_out", 512 * k, 512) for k in range(2)]

        def slot(s, c, n):
            return ring[:, s, 0:c * n].rearrange("p (c n) -> p c n", c=c)

        W2 = "w_in_2"
        middle = [(cols("w_ple_proj", 0, 1024), 4), (cols("w_ple_gate", 0, 512), 6), (cols("w_ple_gate", 512, 512), 8),
                  (cols(W2, 0, 512), 10), (cols(W2, 512, 256), 12), (cols(W2, 768, 512), 14),
                  (cols(W2, 1280, 512), 16), (cols(W2, 1792, 512), 18), (cols(W2, 2304, 512), 20),
                  (cols(W2, 2816, 512), 22), (cols(W2, 3328, 512), 24), (cols(W2, 3840, 512), 26),
                  (cols(W2, 4352, 512), 28), (cols("w_branch_attn_2", 0, 1024), 32),
                  (cols("w_branch_hgrn_2", 0, 1024), 36), (cols("w_out_2", 0, 512), 38), (cols("w_out_2", 512, 512), 40)]

        in_slot = [len(range(s, len(middle), SLOTS)) for s in range(SLOTS)]
        FULL0 = ([1] * SLOTS, [1 + E + n for n in in_slot])
        FREE0 = ([0] * SLOTS, [E] * SLOTS)
        FF = (1024, 512)
        HC = (4, 2)
        GATES = ("w_gate", "w_gate_experts_2")
        UPS = ("w_up", "w_up_experts_2")
        DOWNS = ("w_down", "w_down_experts_2")
        PER = (6, 3)
        TOPK = (4, 2)
        NR = (32, 36)

        def expert_loads(k, e, s0):
            def src(name, text, **sizes):
                return w[name][0, ds(e, 1)].rearrange(text, p=P, **sizes)
            if k == 0:
                loads = []
                for i, name in enumerate((GATES[0], UPS[0])):
                    for q in range(2):
                        v = src(name, "a (p c) n -> p (a c n)")
                        loads.append((s0 + 2 * i + q, ring[:, s0 + 2 * i + q, :], v[:, SLOT * q:SLOT * (q + 1)]))
                v = src(DOWNS[0], "a (j p c) n -> p j (a c n)", j=2)
                for j in range(2):
                    loads.append((s0 + 4 + j, ring[:, s0 + 4 + j, :], v[:, j, :]))
                return loads
            loads = []
            for q in range(2):
                for i, name in enumerate((GATES[1], UPS[1])):
                    v = src(name, "a (p c) n -> p (a c n)")
                    loads.append((s0 + q, ring[:, s0 + q, 2048 * i:2048 * (i + 1)], v[:, 2048 * q:2048 * (q + 1)]))
            v = src(DOWNS[1], "a (j p c) n -> p j (a c n)", j=2)
            loads.append((s0 + 2, ring[:, s0 + 2, :].rearrange("p (j n) -> p j n", j=2), v))
            return loads

        LOADS = ((1,) * 6, (2, 2, 1))
        LAST = ({"gate": 1, "up": 3, "down": 5}, {"gate_up": 1, "down": 2})

        PAIR = (1, 2)

        NEXT = (["one_hot", "one_hot", "bias", "picked"], ["one_hot", "one_hot", "picked"])
        OWN = (["gated", "gated", "gate_min", "clip", "prod", "hidden"], ["gated", "gated", "prod", "hidden"])
        MAIN = ["gated", "gated", "one_hot", "one_hot", "gate_min", "clip", "prod", "hidden", "bias", "picked"]
        STEPS = {"act": ["sigmoid", "back", "hid", "y"], "pe": ["back", "hid", "scattered"]}

        def count(k, q, who, step, p):
            if q == "m1_":
                return (2 if step in ("one_hot", "gated") else 1) * (p + 1)
            steps = STEPS[who] if who != "dve" else MAIN if q == "m0_" else NEXT[k] + OWN[k]
            last = len(steps) - steps[::-1].index(step)
            if q != "m0_" or who != "dve":
                return p * len(steps) + last
            if step not in NEXT[0]:
                return p * len(steps) + len(NEXT[0]) + last
            if isinstance(p, int) and p == 0:
                return NEXT[0].index(step) + 1 + (step == "one_hot")
            return p * len(steps) + last + len(NEXT[0]) - len(steps)

        def done_by(q, who, step):
            return sem(q + who + ("_" + step if q == "m1_" else ""))

        def after(eng, k, q, who, step, p):
            eng.wait_ge(done_by(q, who, step), count(k, q, who, step, p))

        def stage(eng, k, q, n, s0, name):
            s = s0 + LAST[k][name]
            if q[0] == "m":
                eng.wait_ge(free[s], n + 1 + FREE0[k][s])
            else:
                eng.wait_ge(sem(f"over_free{k}_{s}"), n + 1)

        def middle_full(i):
            s = i % SLOTS
            return full[s], 16 * (1 + E + i // SLOTS + 1)

        p_tok = scr[:, 0:512].rearrange("p (a n) -> p a n", a=TT)
        pT = scr[:, 512:1024].rearrange("p (c t) -> p c t", t=T)
        emb = scr[:, 2048:4096].rearrange("p (a n) -> p a n", a=TT)
        junk2 = scr[:, 4096:6144].rearrange("p (a n) -> p a n", a=TT)
        qT2 = scr[:, 0:1024].rearrange("p (i t) -> p i t", t=T)
        kT2 = scr[:, 1024:1280]
        sA0 = scr[:, 1280:2304].rearrange("p (g k) -> p g k", k=P)
        sA1 = scr[:, 2304:4352].rearrange("p (g k) -> p g k", k=T)
        pT2 = scr[:, 4352:7424].rearrange("p (g q) -> p g q", q=P)
        ao = scr[:, 8192:9216].rearrange("p (a n) -> p a n", a=TT)
        hq, fg = Z[:, 0, 3840:4864], Z[:, 1, 3840:4864]
        k1, pre_f, suf_f, r_q, w_a, w_b, q_e, ke_even, ke_odd = (scr[:, 1024 * k:1024 * (k + 1)] for k in range(9))
        by_sub = "p (b j) -> p b j"
        states = xs[:, :, :].rearrange("p a n -> p (a n)").rearrange("p (k n) -> p k n", k=4)

        full = [sem(f"slot_full{s}") for s in range(SLOTS)]
        free = [sem(f"slot_free{s}") for s in range(SLOTS)]

        block = ctx.enter_context(nc.Block())

        @block.sync
        def _(sp):
            for a in range(TT):
                sp.dma_start(h[:, a, :], w["x"][0, a * P:(a + 1) * P, :]).then_inc(sem("x_loaded"), 16)
            for k, name in enumerate(("attn_norm", "ffn_norm", "ple_gate_norm", "norm1_w_2", "norm2_w_2")):
                sp.dma_start(gcol[:, k, :], w[name][0].rearrange("(p c) -> p c", p=P)).then_inc(sem("gains_loaded"), 16)
            for s, (src, c, n) in enumerate(front):
                sp.dma_start(slot(s, c, n), src).then_inc(full[s], 16)
            def experts(k, first):
                for u in range(PAIR[k]):
                    for s, dst, src in expert_loads(k, u, PER[k] * u):
                        first(s)
                        sp.dma_start(dst, src).then_inc(full[s], 16)
                with sp.Fori(1, E // PAIR[k]) as n:
                    for u in range(PAIR[k]):
                        for s, dst, src in expert_loads(k, n * PAIR[k] + u, PER[k] * u):
                            sp.wait_ge(free[s], n + FREE0[k][s])
                            sp.dma_start(dst, src).then_inc(full[s], 16)
                sp.wait_ge(sem("list"), k + 1)
                n = sp.value_load(lst[0:1, 0:1], min_val=0, max_val=NLIST)
                with sp.If(n > 0):
                    with sp.Fori(0, n) as i:
                        e = sp.value_load(lst[0:1, ds(i + 1, 1)], min_val=0, max_val=E - 1)
                        seen = [0] * SLOTS
                        for s, dst, src in expert_loads(k, e, 0):
                            if not seen[s]:
                                sp.wait_ge(free[s], E // PAIR[k] + FREE0[k][s])
                                sp.wait_ge(sem(f"over_free{k}_{s}"), i)
                            seen[s] = 1
                            sp.dma_start(dst, src).then_inc(sem(f"over_full{k}_{s}"), 16)
                    sp.wait_ge(sem(f"over_free{k}_{PER[k] - 1}"), n)
                    sp.sem_inc(sem("over_left"), 1)

            experts(0, lambda s: sp.wait_ge(sem("proj"), 2 * s + 2) if s < 4 else sp.wait_ge(sem("out1"), 2 * s - 6))
            for i, ((src, c, n), _) in enumerate(middle):
                s = i % SLOTS
                if i < SLOTS:
                    sp.wait_ge(free[s], E)
                else:
                    sp.wait_ge(sem("dense2"), middle[i - SLOTS][1])
                sp.dma_start(slot(s, c, n), src).then_inc(full[s], 16)
            last_use = [max(x[1] for x in middle[s::SLOTS]) for s in range(SLOTS)]
            experts(1, lambda s: sp.wait_ge(sem("dense2"), last_use[s]))
            for a in range(TT):
                sp.wait_ge(sem("moe_out"), TT + a + 1)
                sp.dma_start(out[0, a * P:(a + 1) * P, :], h[:, a, :]).then_inc(sem("stored"), 16)
            sp.wait_ge(sem("stored"), 16 * TT)

        @block.gpsimd
        def _(pool):
            done = [0]

            def step(ins):
                ins.then_inc(sem("pool_chain"), 1)
                done[0] += 1
                pool.wait_ge(sem("pool_chain"), done[0])

            def select(view, op, fill, base, pattern, cm):
                step(pool.affine_select(out=view, in_=view, compare_op=op, fill=fill, base=base,
                                        pattern=pattern, channel_multiplier=cm))

            step(pool.memset(ident[:, :], 0.0))
            pool.affine_select(out=ident[:, :], in_=ident[:, :], compare_op=ALU.not_equal, fill=1.0, base=0,
                               pattern=[[-1, P]], channel_multiplier=1).then_inc(sem("ident"), 1)
            for k in range(ROT // 2):
                pool.memset(freq[:, k:k + 1], float(np.float32(ROPE_THETA) ** np.float32(-2 * k / ROT)))
            pool.memset(zeros[:, :], 0.0)
            step(pool.memset(ones[:, :], 1.0))
            pool.memset(mask_own[:, :], 0.0)
            pool.memset(mask_win[:, :], 0.0)
            pool.memset(tri[:, :], 1.0)
            step(pool.memset(blk[:, :], 1.0))
            for m in (mask_own, mask_win):
                select(m[:, P:2 * P], ALU.is_ge, NEG, 0, [[-1, P]], 1)
            select(mask_win[:, 0:P], ALU.is_gt, NEG, 0, [[1, P]], -1)
            select(tri[:, :], ALU.is_gt, 0.0, 0, [[1, P]], -1)
            select(blk[:, :], ALU.is_ge, 0.0, 0, [[-SUB, P // SUB], [0, SUB]], 1)
            select(blk[:, :], ALU.is_ge, 0.0, SUB - 1, [[SUB, P // SUB], [0, SUB]], -1)
            step(pool.iota(iota[:, :], pattern=[[1, CAP]], base=0, channel_multiplier=0,
                           allow_small_or_imprecise_dtypes=True))
            step(pool.iota(pcol[:, :], pattern=[[1, 1]], base=0, channel_multiplier=1,
                           allow_small_or_imprecise_dtypes=True))
            for k in range(ROUNDS - 1):
                pool.memset(thr[:, k:k + 1], float(CAP * (k + 1)))
            for g, win in enumerate((2, 4, 8, 16)):
                band = poolM[:, :, g, :]
                step(pool.memset(band, 1.0 / win))
                for t in range(win - 1):
                    last = pool.memset(poolM[:, 0, g, t:t + 1], 1.0 / (t + 1))
                step(last)
                select(band, ALU.is_ge, 0.0, 0, [[-P, 2], [1, T]], -1)
                select(band, ALU.is_ge, 0.0, win - 1, [[P, 2], [-1, T]], 1)
            for s in range(2):
                v = poolM[:, s, :, s * P:(s + 1) * P]
                step(pool.tensor_tensor(v, v, ident[:, None, :].broadcast_to([P, 4, P]), ALU.subtract))
            step(pool.memset(st[:, 150:152], 0.0))
            step(pool.memset(spread[:, :], 0.0))
            pool.memset(spread[:, SUB - 1::SUB], 1.0)
            pool.memset(st[:, 152:153], 0.0).then_inc(sem("consts"), 1)

            pool.wait_ge(sem("mix_ready"), 4)
            for dst, src in ((wrt[:, :, 0:E], w["w_router"][0].rearrange("(p c) e -> p c e", p=P)),
                             (bias_gu[:, 0, :], w["b_gate"][0]), (bias_gu[:, 1, :], w["b_up"][0]),
                             (bias_dn, w["b_down"][0])):
                pool.dma_start(dst, src).then_inc(sem("router_loaded"), 16)
            pool.dma_start(p_tok, w["p"][0, 0].rearrange("(a p) n -> p a n", p=P)).then_inc(sem("p_loaded"), 16)
            step(pool.tensor_copy(par[:, 1:2], blk[:, SUB:SUB + 1]))
            for k in (3, 5, 7):
                step(pool.tensor_tensor(par[:, 1:2], par[:, 1:2], blk[:, SUB * k:SUB * k + 1], ALU.add))
            pool.tensor_tensor(par[:, 0:1], ones[:, 0:1], par[:, 1:2], ALU.subtract).then_inc(sem("parity"), 1)
            pool.wait_ge(sem("mixed"), 4)
            for dst, src in ((wrt[:, :, 0:4], w["w_router_group_2"][0].rearrange("(p c) e -> p c e", p=P)),
                             (wrt[:, :, 4:36], w["w_router_expert_2"][0].rearrange("(p c) e -> p c e", p=P))):
                pool.dma_start(dst, src).then_inc(sem("router_loaded"), 16)

        @block.scalar
        def _(act):
            def load(dst, src, name="small_loaded"):
                act.dma_start(dst, src, allow_slow_non_contiguous=src.shape[-1] * src.ap[-1][0] != src.shape[-1]).then_inc(sem(name), 16)

            def norm(k, ready):
                for a in range(TT):
                    ready(a)
                    act.activation(xs[:, a, :], h[:, a, :], ACT.Square,
                                   accum_out=ss[:, a:a + 1]).then_inc(sem("norm_sumsq"), 1)
                act.wait_ge(sem("mean_sq"), NORM_NTH[k])
                act.activation(rt, ms, ACT.Sqrt).then_inc(sem("root"), 1)

            norm(A_NORM, lambda a: act.wait_ge(sem("x_loaded"), 16 * TT))

            for k, name in enumerate(("positions", "positions_2")):
                load(posi[:, 2 * k:2 * k + 2], w[name][0].rearrange("(a p) -> p a", p=P), "pos_loaded")
            n_small = [0]

            def small(dst, src):
                n_small[0] += 1
                load(dst, src)

            for k, name in enumerate(("q_norm", "k_norm")):
                small(qkw[:, k, :], w[name][0].partition_broadcast(P))
                small(qkw2[:, k, :], w[name + "_w_2"][0].partition_broadcast(P))
            for k, name in enumerate(("lam_q1", "lam_k1", "lam_q2", "lam_k2")):
                small(lams[:, k, :], w[name][0].partition_broadcast(P))
            small(subln[:, :], w["subln"][0].partition_broadcast(P))
            small(pscale, w["pool_scale"][0].partition_broadcast(P))
            small(wpool, w["w_pool"][0].rearrange("g c d -> c g d"))
            small(brt[:, :], w["b_router"][0].partition_broadcast(P))
            small(brt2[:, 0:4], w["b_router_group_2"][0].partition_broadcast(P))
            small(brt2[:, 4:36], w["b_router_expert_2"][0].partition_broadcast(P))
            small(post, w["ple_post_norm"][0].partition_broadcast(P))
            small(sinks[:, :], w["attn_sinks_2"][0].partition_broadcast(P))
            small(lbc[:, :, :], w["hgrn_lower_bounds_2"].rearrange("l (h p) -> p l h", p=P))
            small(hnorm[:, :], w["hgrn_norm_w_2"][0].partition_broadcast(P))
            assert n_small[0] == N_SMALL

            act.wait_ge(sem("angles"), 1)
            act.activation(trig[:, :, :, :], red[:, :, :, :], ACT.Sin).then_inc(sem("trig"), 1)
            for j in range(8):
                act.wait_ge(sem("proj"), j + 1)
                act.copy(Z[:, j % 2, (j // 2) * 512:(j // 2 + 1) * 512], bank((4 + j) % 8)).then_inc(sem("z_copied"), 1)
                if j == 5:
                    act.wait_ge(sem("mean_sq"), QK_NTH)
                    act.activation(qrt, qms, ACT.Sqrt).then_inc(sem("root"), 1)
            act.wait_ge(sem("pooled"), 1)
            for g in range(2):
                act.copy(poolT[:, 2 * g:2 * g + 2, :], bank(4 + g).rearrange("p (g t) -> p g t", g=2)).then_inc(sem("pool_copied"), 1)
            for a in range(TT):
                act.wait_ge(sem("qk_turned"), 2 * a + 1)
                act.copy(qkT[:, 0:4, a * P:(a + 1) * P],
                         bank((6, 0)[a]).rearrange("p (g t) -> p g t", g=4)).then_inc(sem("q_copied"), 1)
            act.wait_ge(sem("lam_sums"), 1)
            act.activation(lam[:, 2:4], lam[:, 0:2], ACT.Exp).then_inc(sem("lam_exp"), 1)
            act.wait_ge(sem("row_max"), 1)
            for g in range(8):
                act.activation(sc0[:, g, :], sc0[:, g, :], ACT.Exp, bias=qss[:, g:g + 1],
                               accum_out=qms[:, g:g + 1]).then_inc(sem("probs"), 1)
            act.wait_ge(sem("row_max"), 2)
            for g in range(8):
                act.activation(sc1[:, g, :], sc1[:, g, :], ACT.Exp, bias=qss[:, 8 + g:9 + g],
                               accum_out=qms[:, 8 + g:9 + g]).then_inc(sem("probs"), 1)
            act.wait_ge(sem("w_turned"), 2)
            act.copy(wT[:, 4:8, :], bank(5).rearrange("p (g q) -> p g q", g=4)).then_inc(sem("w_copied_act"), 1)
            act.wait_ge(sem("mean_sq"), SUB_NTH)
            act.activation(qrt[:, 0:8], qms[:, 0:8], ACT.Sqrt).then_inc(sem("root"), 1)
            for b in (1, 3):
                act.wait_ge(sem("mix_turned"), b + 1)
                act.copy(xT[:, 4:8, (b // 2) * P:(b // 2 + 1) * P],
                         bank(1 + b).rearrange("p (g t) -> p g t", g=4)).then_inc(sem("mix_copied_act"), 1)

            def experts(k, ready):
                norm((F_NORM, N2_NORM)[k], ready)
                if k == 1:
                    act.wait_ge(sem("group_max"), 1)
                    for a in range(TT):
                        act.activation(few[:, 100 + 4 * a:104 + 4 * a], logit[:, a, 0:4], ACT.Exp, bias=few[:, 8 + a:9 + a],
                                       accum_out=few[:, 12 + a:13 + a]).then_inc(sem("group_exp"), 1)
                act.wait_ge(sem("top"), k + 1)
                for a in range(TT):
                    act.activation(gat[:, a, :], logit[:, a, NR[k] - E:NR[k]], ACT.Exp, bias=few[:, a:a + 1])\
                        .then_inc(sem("gate_exp"), 1)
                if k == 0:
                    act.wait_ge(sem("gates_turned"), 1)
                    act.copy(gates_T, bank(7)[0:E, 0:T]).then_inc(sem("gates_copied"), 1)

                def sigmoid(q, p, n, s0):
                    if k == 0:
                        after(act, k, q, "dve", "gate_min", p)
                        act.activation(act_t, act_g, ACT.Sigmoid, scale=1.702).then_inc(done_by(q, "act", "sigmoid"), 1)
                    else:
                        stage(act, k, q, n, s0, "gate_up")
                        act.activation(act_t[:, 0:256], bank(4)[:, 0:256], ACT.Sigmoid).then_inc(done_by(q, "act", "sigmoid"), 1)

                def leave_back(q, p):
                    after(act, k, q, "pe", "back", p)
                    act.copy(back, bank(7)[:, 0:T]).then_inc(done_by(q, "act", "back"), 1)

                def leave_hid(q, p):
                    after(act, k, q, "pe", "hid", p)
                    lo = T if k == 0 else 0
                    act.copy(hid[:, lo:lo + T], bank(7)[:, T:2 * T]).then_inc(done_by(q, "act", "hid"), 1)

                def leave_y(q, p, n, s0):
                    stage(act, k, q, n, s0, "down")
                    act.copy(y, bank(4 + k)).then_inc(done_by(q, "act", "y"), 1)

                def one(q, p, n):
                    sigmoid(q, p, n, 0)
                    leave_back(q, p)
                    leave_hid(q, p)
                    leave_y(q, p, n, 0)

                q = f"m{k}_"
                if k == 0:
                    with act.Fori(0, E) as n:
                        one(q, n, n)
                else:
                    def leave_rows(p):
                        act.wait_ge(sem(q + "gathered"), p + 1)
                        act.copy(rows, bank(6)).then_inc(sem(q + "rows_copied"), 1)

                    def overlapped(p, n, s0, prev=None):
                        sigmoid(q, p, n, s0)
                        leave_rows(p + 1)
                        if prev:
                            leave_y(q, *prev)
                        leave_hid(q, p)
                        leave_back(q, p)

                    leave_rows(0)
                    overlapped(0, 0, 0)
                    with act.Fori(0, E // 2 - 1) as n:
                        overlapped(2 * n + 1, n, 3, (2 * n, n, 0))
                        overlapped(2 * n + 2, n + 1, 0, (2 * n + 1, n, 3))
                    overlapped(E - 1, E // 2 - 1, 3, (E - 2, E // 2 - 1, 0))
                    leave_y(q, E - 1, E // 2 - 1, 3)
                act.wait_ge(sem("list"), k + 1)
                n = act.value_load(lst[0:1, 0:1], min_val=0, max_val=NLIST)
                with act.If(n > 0):
                    with act.Fori(0, n) as p:
                        one(f"o{k}_", p, p)

            experts(0, lambda a: act.wait_ge(sem("residual"), 3 + a))

            norm(G_NORM, lambda a: act.wait_ge(sem("moe_out"), a + 1))
            act.wait_ge(sem("p_turned"), 1)
            act.copy(pT, bank(4).rearrange("p (c t) -> p c t", c=2)).then_inc(sem("p_copied"), 1)
            for a in range(TT):
                act.wait_ge(sem("dense2"), 2 + 2 * a)
                act.activation(junk2[:, a, :], ps[:, 2 * a:2 * a + 2, :].rearrange("p b n -> p (b n)"), ACT.Square,
                               accum_out=ss[:, a:a + 1]).then_inc(sem("emb_sumsq"), 1)
            act.wait_ge(sem("mean_sq"), EMB_NTH)
            act.activation(rt, ms, ACT.Sqrt).then_inc(sem("root"), 1)
            for b in range(4):
                n, a = b // 2, b % 2
                act.wait_ge(sem("dense2"), 5 + b)
                act.activation(xs[:, a, 512 * n:512 * (n + 1)], bank(4 + b), ACT.Sigmoid).then_inc(sem("ple_gate"), 1)

            norm(N1_NORM, lambda a: act.wait_ge(sem("embedded"), a + 1))

            def leave(i):
                act.wait_ge(sem("dense2"), 9 + i)
                b, a = bank(i % 4), i % 2
                if i < 2:
                    ins = act.copy(Z[:, a, 0:512].rearrange("p (i j d) -> p j i d", i=4, j=2),
                                   b.rearrange("p (j i d) -> p j i d", j=2, i=4))
                elif i < 4:
                    ins = act.copy(Z[:, a, 512:768], b[:, 0:256])
                elif i < 6:
                    ins = act.copy(hq[:, 512 * a:512 * (a + 1)], b)
                elif i < 8:
                    ins = act.activation(fg[:, 512 * a:512 * (a + 1)], b, ACT.Sigmoid)
                elif i < 12:
                    lo = 768 + 512 * ((i - 8) // 2)
                    ins = act.copy(Z[:, a, lo:lo + 512], b)
                else:
                    lo = 1792 + 512 * ((i - 12) // 2)
                    ins = act.activation(Z[:, a, lo:lo + 512], b, ACT.Sigmoid)
                ins.then_inc(sem("d2_copied"), 1)

            for i in range(4):
                leave(i)
            act.wait_ge(sem("mean_sq"), QK2_NTH)
            act.activation(qrt[:, 0:20], qms[:, 0:20], ACT.Sqrt).then_inc(sem("root"), 1)
            for i in range(4, 8):
                leave(i)
            act.wait_ge(sem("lb_diff"), 1)
            act.activation(lb[:, 0, :], lb[:, 2, :], ACT.Sigmoid).then_inc(sem("lb_sig"), 1)
            act.wait_ge(sem("d2_copied"), 6)
            act.activation(xs[:, 0, :], hq, ACT.Sigmoid).then_inc(sem("q_sig"), 1)
            for i in range(8, 12):
                leave(i)
            act.wait_ge(sem("d2_copied"), 12)
            for a in range(TT):
                act.activation(xs[:, 1, 512 * a:512 * (a + 1)], Z[:, a, 1280:1792], ACT.Sigmoid).then_inc(sem("g_sig"), 1)
            act.wait_ge(sem("row_max"), 3)
            for g in range(8):
                act.activation(sA0[:, g, :], sA0[:, g, :], ACT.Exp, bias=qss[:, g:g + 1],
                               accum_out=qms[:, g:g + 1]).then_inc(sem("probs"), 1)
            for i in range(12, 16):
                leave(i)
            act.wait_ge(sem("row_max"), 4)
            for g in range(8):
                act.activation(sA1[:, g, :], sA1[:, g, :], ACT.Exp, bias=qss[:, 8 + g:9 + g],
                               accum_out=qms[:, 8 + g:9 + g]).then_inc(sem("probs"), 1)
            act.activation(qrt[:, 0:16], qrt[:, 0:16], ACT.Exp).then_inc(sem("sink_exp"), 1)
            for i in range(16, 20):
                leave(i)
            act.wait_ge(sem("hgrn_o"), 1)
            act.copy(w_b[:, 0:512], bank(0)).then_inc(sem("oT_act"), 1)
            act.wait_ge(sem("mean_sq"), HG_NTH)
            act.activation(qrt[:, 0:8], qms[:, 0:8], ACT.Sqrt).then_inc(sem("root"), 1)
            for b in (1, 3):
                act.wait_ge(sem("mix_turned"), 4 + b + 1)
                act.copy(xT[:, 4:8, (b // 2) * P:(b // 2 + 1) * P],
                         bank(b).rearrange("p (g t) -> p g t", g=4)).then_inc(sem("mix_copied_act"), 1)

            experts(1, lambda a: act.wait_ge(sem("residual"), 7 + a))

        @block.vector
        def _(dve):
            done = [0]

            def step(ins):
                ins.then_inc(sem("dve_chain"), 1)
                done[0] += 1
                dve.wait_ge(sem("dve_chain"), done[0])

            tt, ts, stt = dve.tensor_tensor, dve.tensor_scalar, dve.scalar_tensor_tensor

            def norm(k):
                dve.wait_ge(sem("norm_sumsq"), 2 * (k + 1))
                ts(ms, ss, 1.0 / D, EPS, ALU.mult, ALU.add).then_inc(sem("mean_sq"), 1)
                dve.wait_ge(sem("root"), NORM_NTH[k])
                step(dve.reciprocal(rstd, rt))
                for a in range(TT):
                    ts(xs[:, a, :], h[:, a, :], rstd[:, a:a + 1], None, ALU.mult).then_inc(sem("norm_xs"), 1)
                for b in range(4):
                    a, half = b // 2, b % 2
                    dve.wait_ge(sem("norm_turned"), 4 * k + b + 1)
                    tt(xT[:, 4 * half:4 * half + 4, a * P:(a + 1) * P], bank(b).rearrange("p (c t) -> p c t", c=4),
                       gcol[:, k, 4 * half:4 * half + 4, None].broadcast_to([P, 4, P]), ALU.mult)\
                        .then_inc(sem("norm_xT"), 1)

            def head_rms(src, ngroup, width, junk, nth):
                step(tt(junk, src, src, ALU.mult))
                step(dve.tensor_reduce(qss[:, 0:ngroup], junk, X, ALU.add))
                ts(qms[:, 0:ngroup], qss[:, 0:ngroup], 1.0 / width, EPS, ALU.mult, ALU.add).then_inc(sem("mean_sq"), 1)
                dve.wait_ge(sem("root"), nth)
                step(dve.reciprocal(qrs[:, 0:ngroup], qrt[:, 0:ngroup]))

            def rope(view, which, ngroup):
                half = ROT // 2
                sin, cos = (trig[:, f, 2 * which:2 * which + 2, None, :].broadcast_to([P, TT, ngroup, half])
                            for f in range(2))
                t1, t2 = view[:, :, :, 0:half], view[:, :, :, half:ROT]
                r = [tmp[:, 256 * k:256 * k + TT * ngroup * half].rearrange("p (a g k) -> p a g k", a=TT, g=ngroup)
                     for k in range(4)]
                for k, (x, y) in enumerate(((t1, cos), (t2, sin), (t2, cos), (t1, sin))):
                    step(tt(r[k], x, y, ALU.mult))
                step(tt(t1, r[0], r[1], ALU.subtract))
                tt(t2, r[2], r[3], ALU.add).then_inc(sem("roped"), 1)

            dve.wait_ge(sem("gains_loaded"), 16 * 5)
            norm(A_NORM)
            dve.wait_ge(sem("consts"), 1)
            dve.wait_ge(sem("pos_loaded"), 32)
            step(dve.tensor_copy(posf[:, :], posi[:, :]))
            step(tt(ang[:, :, :], posf[:, :, None].broadcast_to([P, 4, 8]),
                    freq[:, None, :].broadcast_to([P, 4, 8]), ALU.mult))
            turns = tmp[:, 0:64].rearrange("p (f s k) -> p f s k", f=2, s=4)
            big = float(1.5 * 2 ** 23)
            for f, shift in enumerate((0.0, 0.25)):
                step(ts(turns[:, f], ang[:, :, :], 1.0 / (2 * math.pi), shift, ALU.mult, ALU.add))
            step(ts(turns, turns, big, None, ALU.add))
            step(ts(turns, turns, -big, None, ALU.add))
            for f in range(2):
                step(tt(red[:, f], ang[:, :, :], ang[:, :, :], ALU.max))
            c1 = 6.28125
            c2 = float((np.float32(2 * math.pi - c1).view(np.uint32) & np.uint32(0xFFFFF000)).view(np.float32))
            c3 = 2 * math.pi - c1 - c2
            for c in (c1, c2, c3):
                step(stt(out=red[:, :, :, :], in0=turns, scalar=-c, in1=red[:, :, :, :], op0=ALU.mult, op1=ALU.add))
            step(ts(red[:, 1], red[:, 1], math.pi / 2, None, ALU.add))
            pi = 3.1415925
            ts(red[:, :, :, :], red[:, :, :, :], pi, -pi, ALU.min, ALU.max).then_inc(sem("angles"), 1)

            dve.wait_ge(sem("small_loaded"), 16 * N_SMALL)
            for k in range(2):
                step(tt(lams[:, 2 * k, :], lams[:, 2 * k, :], lams[:, 2 * k + 1, :], ALU.mult))
            dve.tensor_reduce(lam[:, 0:2], lams[:, 0:4:2, :], X, ALU.add).then_inc(sem("lam_sums"), 1)
            step(ts(subln[:, :], subln[:, :], 1.0 - LAMBDA_INIT, None, ALU.mult))
            qk = Z[:, :, 0:1024].rearrange("p a (g d) -> p a g d", d=64)
            dve.wait_ge(sem("z_copied"), 4)
            sq = scr[:, 0:2048].rearrange("p (a g d) -> p a g d", a=2, g=16)
            step(tt(sq, qk, qk, ALU.mult))
            step(dve.tensor_reduce(qss[:, 0:32].rearrange("p (a g) -> p a g", a=2), sq, X, ALU.add))
            ts(qms, qss, 1.0 / 64, EPS, ALU.mult, ALU.add).then_inc(sem("mean_sq"), 1)
            dve.wait_ge(sem("root"), QK_NTH)
            step(dve.reciprocal(qrs, qrt))
            dve.wait_ge(sem("trig"), 1)
            for a in range(TT):
                step(tt(qk[:, a], qk[:, a], qrs[:, 16 * a:16 * a + 16, None].broadcast_to([P, 16, 64]), ALU.mult))
                for k in range(2):
                    v = qk[:, a, 8 * k:8 * k + 8, :]
                    step(tt(v, v, qkw[:, k, None, :].broadcast_to([P, 8, 64]), ALU.mult))
            rope(qk, 0, 16)
            for a in range(TT):
                dve.wait_ge(sem("qk_turned"), 2 * a + 2)
                dve.tensor_copy(qkT[:, 4:8, a * P:(a + 1) * P],
                                bank((7, 1)[a]).rearrange("p (g t) -> p g t", g=4)).then_inc(sem("k_copied"), 1)
            for a in range(TT):
                dve.wait_ge(sem("pool_y"), a + 1)
                tt(xs[:, a, 512:1024], bank(2 + a), pscale, ALU.mult).then_inc(sem("mix_ready"), 1)
            for c in range(2):
                dve.wait_ge(sem("scores"), c + 1)
                step(stt(out=sc0[:, 4 * c:4 * c + 4, :], in0=bank(4 + c).rearrange("p (g k) -> p g k", g=4),
                         scalar=0.125, in1=mask_own[:, None, P:2 * P].broadcast_to([P, 4, P]),
                         op0=ALU.mult, op1=ALU.add))
            dve.wait_ge(sem("z_copied"), 8)
            step(dve.tensor_reduce(qrs[:, 0:8], sc0, X, ALU.max))
            ts(qss[:, 0:8], qrs[:, 0:8], -1.0, None, ALU.mult).then_inc(sem("row_max"), 1)
            for k in range(4):
                c, hp = k % 2, k // 2
                dve.wait_ge(sem("scores"), 3 + k)
                step(stt(out=sc1[:, 4 * c + 2 * hp:4 * c + 2 * hp + 2, :],
                         in0=bank((6, 7, 0, 1)[k]).rearrange("p (g k) -> p g k", g=2),
                         scalar=0.125, in1=mask_own[:, None, :].broadcast_to([P, 2, T]),
                         op0=ALU.mult, op1=ALU.add))
            step(dve.tensor_reduce(qrs[:, 8:16], sc1, X, ALU.max))
            ts(qss[:, 8:16], qrs[:, 8:16], -1.0, None, ALU.mult).then_inc(sem("row_max"), 1)
            dve.wait_ge(sem("lam_exp"), 1)
            step(tt(lam[:, 4:5], lam[:, 3:4], lam[:, 2:3], ALU.subtract))
            step(ts(lam[:, 4:5], lam[:, 4:5], -LAMBDA_INIT, None, ALU.add))
            for a, sc, keys in ((0, sc0, P), (1, sc1, T)):
                dve.wait_ge(sem("probs"), 8 * (a + 1))
                step(dve.reciprocal(qrs[:, 8 * a:8 * a + 8], qms[:, 8 * a:8 * a + 8]))
                step(ts(qrs[:, 8 * a + 4:8 * a + 8], qrs[:, 8 * a + 4:8 * a + 8], lam[:, 4:5], None, ALU.mult))
                step(tt(sc, sc, qrs[:, 8 * a:8 * a + 8, None].broadcast_to([P, 8, keys]), ALU.mult))
                tt(sc[:, 0:4, :], sc[:, 0:4, :], sc[:, 4:8, :], ALU.add).then_inc(sem("w_ready"), 1)
            for k in (0, 2):
                dve.wait_ge(sem("w_turned"), k + 1)
                dve.tensor_copy(wT[:, 4 * k:4 * k + 4, :], bank(4 + k).rearrange("p (g q) -> p g q", g=4)).then_inc(sem("w_copied_dve"), 1)
            for a in range(TT):
                dve.wait_ge(sem("pv"), a + 1)
                step(dve.tensor_copy(tmp[:, 512 * a:512 * a + 512], bank((7, 0)[a])))
            o = tmp.rearrange("p (g d) -> p g d", d=P)
            head_rms(o, 8, P, scr[:, 0:1024].rearrange("p (g d) -> p g d", d=P), SUB_NTH)
            step(tt(o, o, qrs[:, 0:8, None].broadcast_to([P, 8, P]), ALU.mult))
            for a in range(TT):
                tt(xs[:, a, 0:512].rearrange("p (g d) -> p g d", d=P), o[:, 4 * a:4 * a + 4, :],
                   subln[:, None, :].broadcast_to([P, 4, P]), ALU.mult).then_inc(sem("mix_ready"), 1)
            for b in (0, 2):
                dve.wait_ge(sem("mix_turned"), b + 1)
                dve.tensor_copy(xT[:, 0:4, (b // 2) * P:(b // 2 + 1) * P],
                                bank(1 + b).rearrange("p (g t) -> p g t", g=4)).then_inc(sem("mix_copied_dve"), 1)
            for b in range(4):
                n, a = b // 2, b % 2
                dve.wait_ge(sem("out1"), b + 1)
                v = h[:, a, 512 * n:512 * n + 512]
                tt(v, bank((5, 6, 7, 0)[b]), v, ALU.add).then_inc(sem("residual"), 1)

            def experts(k):
                norm((F_NORM, N2_NORM)[k])
                off = NR[k] - E
                dve.wait_ge(sem("logits"), k + 1)
                dve.wait_ge(sem("router_loaded"), 16 * (4, 6)[k])
                step(tt(logit[:, :, 0:NR[k]], bank(4)[:, 0:TT * NR[k]].rearrange("p (a e) -> p a e", a=TT),
                        (brt, brt2)[k][:, None, 0:NR[k]].broadcast_to([P, TT, NR[k]]), ALU.add))
                lg = logit[:, :, off:off + E]
                if k == 1:
                    for a in range(TT):
                        grp = logit[:, a, 0:4]
                        step(dve.tensor_reduce(few[:, 4 + a:5 + a], grp, X, ALU.max))
                        step(ts(eqs[:, a, 0:4], grp, few[:, 4 + a:5 + a], None, ALU.is_equal))
                        step(dve.tensor_tensor_scan(pre[:, a, 0:4], ones[:, 0:4], eqs[:, a, 0:4], 0.0, ALU.mult, ALU.add))
                        step(ts(pre[:, a, 0:4], pre[:, a, 0:4], 1.0, None, ALU.is_le))
                        step(tt(msk[:, a, 0:4], pre[:, a, 0:4], eqs[:, a, 0:4], ALU.mult))
                        le = lg[:, a].rearrange("p (g e) -> p g e", g=4)
                        gm = msk[:, a, 0:4, None].broadcast_to([P, 4, 8])
                        step(tt(le, le, gm, ALU.mult))
                        step(ts(msk[:, a, 0:4], msk[:, a, 0:4], 1.0, -NEG, ALU.subtract, ALU.mult))
                        step(tt(le, le, gm, ALU.add))
                    ts(few[:, 8:10], few[:, 4:6], -1.0, None, ALU.mult).then_inc(sem("group_max"), 1)
                for a in range(TT):
                    step(dve.max(top[:, a], lg[:, a]))
                    last = top[:, a, TOPK[k] - 1:TOPK[k]]
                    step(ts(msk[:, a], lg[:, a], last, None, ALU.is_gt))
                    step(ts(eqs[:, a], lg[:, a], last, None, ALU.is_equal))
                    step(dve.tensor_reduce(few[:, 2 + a:3 + a], msk[:, a], X, ALU.add))
                    step(dve.tensor_tensor_scan(pre[:, a], ones[:, 0:E], eqs[:, a], few[:, 2 + a:3 + a], ALU.mult, ALU.add))
                    step(ts(pre[:, a], pre[:, a], float(TOPK[k]), None, ALU.is_le))
                    step(tt(eqs[:, a], eqs[:, a], pre[:, a], ALU.mult))
                    tt(msk[:, a], msk[:, a], eqs[:, a], ALU.add).then_inc(sem("chosen"), 1)
                ts(few[:, 0:TT], top[:, :, 0], -1.0, None, ALU.mult).then_inc(sem("top"), 1)
                dve.wait_ge(sem("gate_exp"), 2 * k + TT)
                dve.wait_ge(sem("chosen"), 2 * k + TT)
                step(tt(gat[:, :, :], gat[:, :, :], msk[:, :, :], ALU.mult))
                step(dve.tensor_reduce(few[:, 2:4], gat[:, :, :], X, ALU.add))
                if k == 1:
                    dve.wait_ge(sem("group_exp"), TT)
                    step(tt(few[:, 2:4], few[:, 2:4], few[:, 12:14], ALU.mult))
                step(dve.reciprocal(few[:, 6:8], few[:, 2:4]))
                tt(gat[:, :, :], gat[:, :, :], few[:, 6:8, None].broadcast_to([P, TT, E]), ALU.mult)\
                    .then_inc(sem("gates"), 1)
                dve.wait_ge(sem("ranks"), k + 1)
                base = pre
                rk = bank(5)[:, 0:TT * E].rearrange("p (a e) -> p a e", a=TT)
                step(stt(out=base, in0=rk, scalar=1.0, in1=msk[:, :, :], op0=ALU.add, op1=ALU.mult))
                for r in range(ROUNDS):
                    step(ts(rank[:, :, E * r:E * (r + 1)], base, -1.0 - CAP * r, None, ALU.add))
                def choose(q, r):
                    for a in range(TT):
                        ts(one_hot[:, a], iota[:, :], rank[:, a, ds(r, 1)], None, ALU.is_equal)\
                            .then_inc(done_by(q, "dve", "one_hot"), 1)

                def choose_bias(q, e):
                    if k == 0:
                        dve.tensor_copy(pick_bias, ident[0:E, ds(e, 1)].broadcast_to([E, CAP])).then_inc(sem(q + "dve"), 1)

                def gather(q, p):
                    if q == "m1_":
                        dve.wait_ge(sem(q + "rows_turned"), p + 1)
                        tt(picked.rearrange("p (c j s) -> p c j s", c=4, j=2), bank(6).rearrange("p (c j s) -> p c j s", c=4, j=2),
                           gcol[:, N2_NORM, :].rearrange("p (j c) -> p c j", j=2)[:, :, :, None].broadcast_to([P, 4, 2, CAP]),
                           ALU.mult).then_inc(done_by(q, "dve", "picked"), 1)
                        return
                    dve.wait_ge(sem(q + "gathered"), p + 1)
                    tt(picked.rearrange("p (c s) -> p c s", c=DC), bank(6).rearrange("p (c s) -> p c s", c=DC),
                       gcol[:, (F_NORM, N2_NORM)[k], :, None].broadcast_to([P, DC, CAP]), ALU.mult)\
                        .then_inc(done_by(q, "dve", "picked"), 1)

                def gate(q, p, e, r):
                    for a in range(TT):
                        ts(gated[:, a], iota[:, None, :].broadcast_to([P, 2, CAP]), rank[:, a, ds(r, 1)],
                           gat[:, a, ds(e, 1)], ALU.is_equal, ALU.mult).then_inc(done_by(q, "dve", "gated"), 1)

                def activate(q, p, n, s0):
                    if k == 0:
                        stage(dve, k, q, n, s0, "gate")
                        ts(act_g, bank(4), 7.0, None, ALU.min).then_inc(sem(q + "dve"), 1)
                        stage(dve, k, q, n, s0, "up")
                        ts(act_h, bank(5), 7.0, -7.0, ALU.min, ALU.max).then_inc(sem(q + "dve"), 1)
                        after(dve, k, q, "dve", "gate_min", p)
                        after(dve, k, q, "dve", "clip", p)
                        stt(out=act_h, in0=act_h, scalar=1.0, in1=act_g, op0=ALU.add, op1=ALU.mult)\
                            .then_inc(sem(q + "dve"), 1)
                        after(dve, k, q, "dve", "prod", p)
                        after(dve, k, q, "act", "sigmoid", p)
                        tt(act_h, act_h, act_t, ALU.mult).then_inc(sem(q + "dve"), 1)
                    else:
                        after(dve, k, q, "act", "sigmoid", p)
                        tt(act_g[:, 0:256], act_t[:, 0:256], bank(4)[:, 0:256], ALU.mult).then_inc(done_by(q, "dve", "prod"), 1)
                        after(dve, k, q, "dve", "prod", p)
                        tt(act_h[:, 0:256], act_g[:, 0:256], bank(4)[:, 256:512], ALU.mult)\
                            .then_inc(done_by(q, "dve", "hidden"), 1)

                def leave(q, p):
                    if k == 0:
                        after(dve, k, q, "pe", "hid", p)
                        dve.tensor_copy(hid[:, 0:T], bank(5)[:, 0:T]).then_inc(sem(q + "hid_dve"), 1)

                q = f"m{k}_"
                choose(q, 0)
                choose_bias(q, 0)
                cnt, extra, start = few[0:E, 16:17], few[0:E, 17:18], few[0:E, 18:19]
                step(dve.tensor_copy(cnt, bank(5)[0:E, 64:65]))
                step(ts(few[0:E, 20:20 + ROUNDS - 1], thr[0:E, :], cnt, None, ALU.is_lt))
                dve.tensor_reduce(extra, few[0:E, 20:20 + ROUNDS - 1], X, ALU.add).then_inc(sem("extra"), 1)
                dve.wait_ge(sem("starts"), k + 1)
                step(dve.tensor_copy(start, bank(5)[0:E, 72:73]))
                dve.wait_ge(sem("extra"), k + 1)
                step(tt(few[0:E, 19:20], start, extra, ALU.add))
                within = few[0:E, 32:48]
                step(ts(few[0:E, 48:64], iota[0:E, 0:NLIST], few[0:E, 19:20], None, ALU.is_lt))
                step(ts(within, iota[0:E, 0:NLIST], start, None, ALU.is_ge))
                tt(within, within, few[0:E, 48:64], ALU.mult).then_inc(sem("within"), 1)
                dve.wait_ge(sem("rows"), k + 1)
                row = few[0:1, 64:112]
                step(dve.tensor_copy(row[:, 0:33], bank(5)[0:1, 96:129]))
                r1 = row[:, 17:33]
                step(tt(r1, iota[0:1, 0:NLIST], r1, ALU.subtract))
                step(ts(r1, r1, 1.0, float(E), ALU.add, ALU.mult))
                step(tt(r1, r1, row[:, 1:17], ALU.add))
                step(ts(r1, r1, float(ROUNDS * E - 1), None, ALU.min))
                dve.tensor_copy(lst[0:1, 0:33], row[:, 0:33]).then_inc(sem("list"), 1)
                dve.wait_ge(sem("gates"), k + 1)
                gather(q, 0)
                if k == 0:
                    with dve.Fori(0, E) as p:
                        gate(q, p, p, p)
                        choose(q, p + 1)
                        activate(q, p, p, 0)
                        choose_bias(q, p + 1)
                        leave(q, p)
                        gather(q, p + 1)
                    dve.wait_ge(sem(q + "dve"), count(k, q, "dve", "picked", E))
                else:
                    def overlapped(p, n, s0):
                        choose(q, p + 1)
                        if n is not None:
                            after(dve, k, q, "pe", "back", p - 1)
                        gate(q, p, p, p)
                        if n is not None:
                            after(dve, k, q, "pe", "hid", p - 1)
                        activate(q, p, n, s0)
                        gather(q, p + 1)

                    overlapped(0, None, 0)
                    with dve.Fori(0, E // 2 - 1) as n:
                        overlapped(2 * n + 1, n, 3)
                        overlapped(2 * n + 2, n + 1, 0)
                    overlapped(E - 1, E // 2 - 1, 3)
                n = dve.value_load(lst[0:1, 0:1], min_val=0, max_val=NLIST)
                after(dve, k, q, "pe", "scattered", E - 1)
                q = f"o{k}_"
                with dve.If(n > 0):
                    with dve.Fori(0, n) as p:
                        e = dve.value_load(lst[0:1, ds(p + 1, 1)], min_val=0, max_val=E - 1)
                        r = dve.value_load(lst[0:1, ds(p + 17, 1)], min_val=0, max_val=ROUNDS * E - 1)
                        choose(q, r)
                        choose_bias(q, e)
                        gather(q, p)
                        gate(q, p, e, r)
                        activate(q, p, p, 0)
                        leave(q, p)
                        after(dve, k, q, "pe", "scattered", p)
                if k == 0:
                    dve.wait_ge(sem("down_bias"), 1)
                for a in range(TT):
                    tt(h[:, a, :], ps[:, 2 * a:2 * a + 2, :].rearrange("p b n -> p (b n)"), h[:, a, :], ALU.add)\
                        .then_inc(sem("moe_out"), 1)

            experts(0)

            norm(G_NORM)
            dve.wait_ge(sem("emb_sumsq"), 2)
            ts(ms, ss, 1.0 / D, EPS, ALU.mult, ALU.add).then_inc(sem("mean_sq"), 1)
            dve.wait_ge(sem("root"), EMB_NTH)
            step(dve.reciprocal(rstd, rt))
            for a in range(TT):
                step(stt(out=emb[:, a, :], in0=ps[:, 2 * a:2 * a + 2, :].rearrange("p b n -> p (b n)"),
                         scalar=rstd[:, a:a + 1], in1=post, op0=ALU.mult, op1=ALU.mult))
            for b in range(4):
                n, a = b // 2, b % 2
                r = slice(512 * n, 512 * (n + 1))
                dve.wait_ge(sem("ple_gate"), b + 1)
                step(tt(emb[:, a, r], emb[:, a, r], xs[:, a, r], ALU.mult))
                ins = tt(h[:, a, r], h[:, a, r], emb[:, a, r], ALU.add)
                if n == 0:
                    step(ins)
                else:
                    ins.then_inc(sem("embedded"), 1)
            tt(lb[:, 2, :], lbc[:, 0, :], lbc[:, 1, :], ALU.subtract).then_inc(sem("lb_diff"), 1)

            norm(N1_NORM)
            dve.wait_ge(sem("d2_copied"), 4)
            qk2 = Z[:, :, 0:640].rearrange("p a (g d) -> p a g d", d=64)
            sq2 = scr[:, 4352:5632].rearrange("p (a g d) -> p a g d", a=TT, g=10)
            step(tt(sq2, qk2, qk2, ALU.mult))
            step(dve.tensor_reduce(qss[:, 0:20].rearrange("p (a g) -> p a g", a=TT), sq2, X, ALU.add))
            ts(qms[:, 0:20], qss[:, 0:20], 1.0 / 64, EPS, ALU.mult, ALU.add).then_inc(sem("mean_sq"), 1)
            dve.wait_ge(sem("root"), QK2_NTH)
            step(dve.reciprocal(qrs[:, 0:20], qrt[:, 0:20]))
            for a in range(TT):
                step(tt(qk2[:, a], qk2[:, a], qrs[:, 10 * a:10 * a + 10, None].broadcast_to([P, 10, 64]), ALU.mult))
                for v, k, n in ((qk2[:, a, 0:8, :], 0, 8), (qk2[:, a, 8:10, :], 1, 2)):
                    step(tt(v, v, qkw2[:, k, None, :].broadcast_to([P, n, 64]), ALU.mult))
            rope(qk2, 1, 10)
            for k in range(3):
                dve.wait_ge(sem("qk_turned"), 4 + k + 1)
                if k < 2:
                    ins = dve.tensor_copy(qT2[:, :, k * P:(k + 1) * P], bank(4 + k).rearrange("p (i t) -> p i t", i=4))
                else:
                    ins = dve.tensor_copy(kT2, bank(6)[:, 0:T])
                ins.then_inc(sem("qk2_copied"), 1)
            dve.wait_ge(sem("lb_sig"), 1)
            dve.wait_ge(sem("d2_copied"), 8)
            step(ts(lb[:, 1, :], lb[:, 0, :], -1.0, 1.0, ALU.mult, ALU.add))
            for i in range(4):
                v = fg[:, T * i:T * (i + 1)]
                step(ts(v, v, lb[:, 1, i:i + 1], lb[:, 0, i:i + 1], ALU.mult, ALU.add))
            dve.wait_ge(sem("q_sig"), 1)
            step(tt(hq, hq, xs[:, 0, :], ALU.mult))
            for k in range(2):
                dve.wait_ge(sem("scores"), 6 + k + 1)
                stt(out=sA0[:, 4 * k:4 * k + 4, :], in0=bank(4 + k).rearrange("p (g k) -> p g k", g=4), scalar=0.125,
                    in1=mask_win[:, None, P:T].broadcast_to([P, 4, P]), op0=ALU.mult, op1=ALU.add)\
                    .then_inc(sem("scores2_copied"), 1)
            for k in range(4):
                kv, half = k % 2, k // 2
                dve.wait_ge(sem("scores"), 6 + 3 + k)
                g = 4 * kv + 2 * half
                stt(out=sA1[:, g:g + 2, :], in0=bank((6, 7, 4, 5)[k]).rearrange("p (g k) -> p g k", g=2), scalar=0.125,
                    in1=mask_win[:, None, :].broadcast_to([P, 2, T]), op0=ALU.mult, op1=ALU.add)\
                    .then_inc(sem("scores2_copied"), 1)
            dve.wait_ge(sem("scores2_copied"), 6)
            for a, sc in enumerate((sA0, sA1)):
                m = qrs[:, 8 * a:8 * a + 8]
                step(dve.tensor_reduce(m, sc, X, ALU.max))
                step(tt(m, m, sinks[:, :], ALU.max))
                step(tt(qrt[:, 8 * a:8 * a + 8], sinks[:, :], m, ALU.subtract))
                ts(qss[:, 8 * a:8 * a + 8], m, -1.0, None, ALU.mult).then_inc(sem("row_max"), 1)
            dve.wait_ge(sem("g_sig"), 2)
            for a in range(TT):
                v = Z[:, a, 1280:1792]
                step(tt(v, v, xs[:, 1, 512 * a:512 * (a + 1)], ALU.mult))
            for k in range(6):
                dve.wait_ge(sem("w_turned"), 3 + k + 1)
                dve.tensor_copy(pT2[:, 4 * k:4 * k + 4, :], bank(4 + k % 4).rearrange("p (g q) -> p g q", g=4))\
                    .then_inc(sem("p2_copied"), 1)
            step(ts(k1, fg, -1.0, 1.0, ALU.mult, ALU.add))
            f_b, k_b, r_b = (v.rearrange(by_sub, j=SUB) for v in (fg, k1, r_q))
            pf_b, sf_b = (v.rearrange(by_sub, j=SUB) for v in (pre_f, suf_f))
            wa_b, wb_b = (v.rearrange(by_sub, j=SUB) for v in (w_a, w_b))
            factor, start = xs[:, 0, :], xs[:, 1, :]
            factor_b, start_b = (v.rearrange(by_sub, j=SUB) for v in (factor, start))
            dve.tensor_copy(factor, fg)
            step(dve.memset(start, 0.0))
            dve.memset(factor_b[:, :, 0:1], 0.0)
            step(dve.tensor_copy(start_b[:, :, 0:1], f_b[:, :, 0:1]))
            step(dve.tensor_tensor_scan(pre_f, factor, start, 0.0, ALU.mult, ALU.add))
            step(dve.memset(sf_b[:, :, SUB - 1:SUB], 1.0))
            for j in range(SUB - 1, 0, -1):
                step(tt(sf_b[:, :, j - 1:j], sf_b[:, :, j:j + 1], f_b[:, :, j:j + 1], ALU.mult))
            tt(suf_f, suf_f, k1, ALU.mult).then_inc(sem("ke_ready"), 1)
            dve.wait_ge(sem("probs"), 32)
            dve.wait_ge(sem("sink_exp"), 1)
            step(tt(qms[:, 0:16], qms[:, 0:16], qrt[:, 0:16], ALU.add))
            step(dve.reciprocal(qrs[:, 0:16], qms[:, 0:16]))
            for a in range(TT):
                dve.wait_ge(sem("pv"), 2 + a + 1)
                tt(ao[:, a, :].rearrange("p (g d) -> p g d", d=64), bank(6 + a).rearrange("p (g d) -> p g d", d=64),
                   qrs[:, 8 * a:8 * a + 8, None].broadcast_to([P, 8, 64]), ALU.mult).then_inc(sem("branch_ready"), 1)
            for a in range(TT):
                dve.wait_ge(sem("branch_turned"), a + 1)
                dve.tensor_copy(Z[:, a, 0:512], bank(4 + a)).then_inc(sem("branch_copied"), 1)

            step(tt(q_e, hq, pre_f, ALU.mult))
            step(dve.tensor_copy(r_q, hq))
            nb = TT * P * 4 // SUB

            def offset(n):
                j = SUB - 1 - n
                if n:
                    v = r_b[:, :, j + 1:SUB]
                    step(tt(v, v, f_b[:, :, j + 1:j + 2].broadcast_to([P, nb, SUB - 1 - j]), ALU.mult))
                if n >= 2:
                    dve.wait_ge(sem("w_used"), n - 1)
                buf = (wa_b, wb_b)[n % 2]
                tt(buf[:, :, j:SUB], r_b[:, :, j:SUB], k_b[:, :, j:j + 1].broadcast_to([P, nb, SUB - j]), ALU.mult)\
                    .then_inc(sem("w_offset"), 1)

            def state(i):
                dve.wait_ge(sem("update"), i + 1)
                if i >= 4:
                    dve.wait_ge(sem("inter"), i - 3)
                new, old = states[:, (i + 1) % 4, :], states[:, i % 4, :]
                if i == 0:
                    dve.tensor_copy(new, bank(5)).then_inc(sem("state"), 4)
                    return
                dve.wait_ge(sem("state"), 4 * i)
                for n in range(4):
                    r = slice(n * P, (n + 1) * P)
                    stt(out=new[:, r], in0=old[:, r], scalar=pre_f[:, n * T + SUB * i + SUB - 1:n * T + SUB * i + SUB],
                        in1=bank(5 + 2 * (i % 2))[:, r], op0=ALU.mult, op1=ALU.add).then_inc(sem("state"), 1)

            offset(0)
            offset(1)
            dve.wait_ge(sem("parity"), 1)
            for a in range(TT):
                dve.wait_ge(sem("ke_turned"), a + 1)
                for v, k in ((ke_even, 0), (ke_odd, 1)):
                    ts(v[:, 512 * a:512 * (a + 1)], bank(7 if a == 0 else 5), par[:, k:k + 1], None, ALU.mult)\
                        .then_inc(sem("ke_copied"), 1)
            for n in range(2, SUB):
                offset(n)
                state(n - 2)
            dve.wait_ge(sem("w_used"), SUB)
            for g in range(2):
                tt(r_q[:, 512 * g:512 * (g + 1)].rearrange("p (g t) -> p g t", g=4), bank(4 + 2 * g).rearrange("p (g t) -> p g t", g=4),
                   blk[:, None, :].broadcast_to([P, 4, P]), ALU.mult).then_inc(sem("intra"), 1)
            state(NSUB - 2)
            dve.wait_ge(sem("hgrn_o"), 2)
            dve.tensor_copy(w_b[:, 512:1024], bank(1)).then_inc(sem("oT_dve"), 1)
            for a in range(TT):
                dve.wait_ge(sem("o_turned"), a + 1)
                step(dve.tensor_copy(k1[:, 512 * a:512 * (a + 1)], bank(6 + a)))
            o = k1.rearrange("p (g d) -> p g d", d=P)
            head_rms(o, 8, P, pre_f.rearrange("p (g d) -> p g d", d=P), HG_NTH)
            step(tt(o, o, qrs[:, 0:8, None].broadcast_to([P, 8, P]), ALU.mult))
            step(tt(o, o, hnorm[:, None, :].broadcast_to([P, 8, P]), ALU.mult))
            for a in range(TT):
                v = k1[:, 512 * a:512 * (a + 1)]
                tt(v, v, Z[:, a, 1280:1792], ALU.mult).then_inc(sem("branch_ready"), 1)
            for b in range(4):
                a, n = b // 2, b % 2
                dve.wait_ge(sem("dense2"), 29 + b)
                r = slice(512 * n, 512 * (n + 1))
                tt(xs[:, a, r], bank(b), Z[:, a, 1792 + 512 * n:2304 + 512 * n], ALU.mult).then_inc(sem("branch_a"), 1)
            for a in range(TT):
                dve.wait_ge(sem("branch_turned"), a + 3)
                dve.tensor_copy(Z[:, a, 768:1280], bank(4 + a)).then_inc(sem("branch_copied"), 1)
            dve.wait_ge(sem("branch_a"), 4)
            for b in range(4):
                a, n = b // 2, b % 2
                dve.wait_ge(sem("dense2"), 33 + b)
                r = slice(512 * n, 512 * (n + 1))
                t = scr[:, 2048 + 512 * b:2560 + 512 * b]
                step(tt(t, bank((6, 7, 4, 5)[b]), Z[:, a, 2816 + 512 * n:3328 + 512 * n], ALU.mult))
                tt(xs[:, a, r], xs[:, a, r], t, ALU.add).then_inc(sem("mixed"), 1)
            for b in (0, 2):
                dve.wait_ge(sem("mix_turned"), 4 + b + 1)
                dve.tensor_copy(xT[:, 0:4, (b // 2) * P:(b // 2 + 1) * P],
                                bank(b).rearrange("p (g t) -> p g t", g=4)).then_inc(sem("mix_copied_dve"), 1)
            for b in range(4):
                n, a = b // 2, b % 2
                dve.wait_ge(sem("dense2"), 37 + b)
                v = h[:, a, 512 * n:512 * n + 512]
                tt(v, bank(4 + b), v, ALU.add).then_inc(sem("residual"), 1)

            experts(1)

        @block.tensor
        def _(pe):
            def turn(dst, src, c, stride, n, who):
                for i in range(n):
                    last = pe.transpose(dst[:, i * P:(i + 1) * P], src[:, c + i:c + i + stride * (P - 1) + 1:stride], ident[:, :])
                last.then_inc(sem(who), 1)

            def norm(k):
                for b in range(4):
                    if b % 2 == 0:
                        pe.wait_ge(sem("norm_xs"), 2 * k + b // 2 + 1)
                    turn(bank(b), xs[:, b // 2, :], 4 * (b % 2), DC, 4, "norm_turned")

            pe.wait_ge(sem("ident"), 1)
            norm(A_NORM)
            pe.wait_ge(sem("norm_xT"), 4)
            for j in range(8):
                u, a = j // 2, j % 2
                pe.wait_ge(full[u], 16)
                for c in range(DC):
                    last = pe.matmul(bank((4 + j) % 8), xT[:, c, a * P:(a + 1) * P], slot(u, DC, 512)[:, c, :],
                                     start=c == 0, stop=c == DC - 1)
                last.then_inc(sem("proj"), 1)
            pe.wait_ge(sem("z_copied"), 8)
            pe.wait_ge(sem("consts"), 1)
            pe.wait_ge(sem("small_loaded"), 16 * N_SMALL)
            for g in range(4):
                for s in range(2):
                    last = pe.matmul(bank(4 + g // 2)[:, (g % 2) * T:(g % 2 + 1) * T],
                                     Z[:, s, 1536 + g * P:1536 + (g + 1) * P], poolM[:, s, g, :],
                                     start=s == 0, stop=s == 1)
            last.then_inc(sem("pooled"), 1)
            pe.wait_ge(sem("roped"), 1)
            for k in range(4):
                for i in range(4):
                    lo = 512 * (k % 2) + P * i
                    last = pe.transpose(bank((6, 7, 0, 1)[k])[:, i * P:(i + 1) * P], Z[:, k // 2, lo:lo + P], ident[:, :])
                last.then_inc(sem("qk_turned"), 1)
            pe.wait_ge(sem("pool_copied"), 2)
            for a in range(TT):
                for g in range(4):
                    last = pe.matmul(bank(2 + a)[:, g * P:(g + 1) * P], poolT[:, g, a * P:(a + 1) * P], wpool[:, g, :],
                                     start=True, stop=True)
                last.then_inc(sem("pool_y"), 1)
            pe.wait_ge(sem("q_copied"), 2)
            pe.wait_ge(sem("k_copied"), 2)
            lasts = {}
            for i in range(4):
                for c in range(2):
                    r = slice(64 * c, 64 * c + 64)
                    last = pe.matmul(bank(4 + c)[:, i * P:(i + 1) * P], qkT[r, i, 0:P], qkT[r, 4 + i, 0:P],
                                     start=True, stop=True)
                    if i == 3:
                        last.then_inc(sem("scores"), 1)
            for hp in range(2):
                for i in range(2):
                    for c in range(2):
                        r = slice(64 * c, 64 * c + 64)
                        last = pe.matmul(bank((6, 7, 0, 1)[2 * hp + c])[:, i * T:(i + 1) * T],
                                         qkT[r, 2 * hp + i, P:T], qkT[r, 6 + i - 2 + 2 * hp, :], start=True, stop=True)
                        if i == 1:
                            last.then_inc(sem("scores"), 1)
            for k, (a, kt) in enumerate(((0, 0), (1, 0), (1, 1))):
                pe.wait_ge(sem("w_ready"), a + 1)
                for i in range(4):
                    src = (sc0, sc1)[a][:, i, kt * P:(kt + 1) * P]
                    last = pe.transpose(bank(4 + k)[:, i * P:(i + 1) * P], src, ident[:, :])
                last.then_inc(sem("w_turned"), 1)
            pe.wait_ge(sem("w_copied_dve"), 1)
            for a in range(TT):
                if a == 1:
                    pe.wait_ge(sem("w_copied_dve"), 2)
                    pe.wait_ge(sem("w_copied_act"), 1)
                for i in range(4):
                    for kt in range(a + 1):
                        last = pe.matmul(bank((7, 0)[a])[:, i * P:(i + 1) * P], wT[:, 4 * (a + kt) + i, :],
                                         Z[:, kt, 1024 + i * P:1024 + (i + 1) * P], start=kt == 0, stop=kt == a)
                last.then_inc(sem("pv"), 1)
            pe.wait_ge(sem("mix_ready"), 4)
            for b in range(4):
                turn(bank(1 + b), xs[:, b // 2, :], 4 * (b % 2), DC, 4, "mix_turned")
            pe.wait_ge(sem("mix_copied_dve"), 2)
            pe.wait_ge(sem("mix_copied_act"), 2)
            for b in range(4):
                n, a = b // 2, b % 2
                pe.wait_ge(full[4 + n], 16)
                for c in range(DC):
                    last = pe.matmul(bank((5, 6, 7, 0)[b]), xT[:, c, a * P:(a + 1) * P], slot(4 + n, DC, 512)[:, c, :],
                                     start=c == 0, stop=c == DC - 1)
                last.then_inc(sem("out1"), 1)

            def experts(k):
                norm((F_NORM, N2_NORM)[k])
                pe.wait_ge(sem("norm_xT"), 4 * (F_NORM, N2_NORM)[k] + 4)
                pe.wait_ge(sem("router_loaded"), 16 * (4, 6)[k])
                for a in range(TT):
                    for c in range(DC):
                        last = pe.matmul(bank(4)[:, NR[k] * a:NR[k] * (a + 1)], xT[:, c, a * P:(a + 1) * P],
                                         wrt[:, c, 0:NR[k]], start=c == 0, stop=c == DC - 1)
                last.then_inc(sem("logits"), 1)
                pe.wait_ge(sem("norm_xT"), 4 * (F_NORM, N2_NORM)[k] + 4)
                for b in range(2 * TT):
                    pe.matmul(bank(b), zeros[:, :], h[:, 0, 0:512], start=True, stop=True)
                pe.wait_ge(sem("chosen"), 2 * k + TT)
                rk = bank(5)[:, 0:64]
                pe.matmul(rk[:, 0:E], tri[:, :], msk[:, 0], start=True, stop=True)
                pe.matmul(rk[:, E:2 * E], ones[:, :], msk[:, 0], start=True, stop=False)
                pe.matmul(rk[:, E:2 * E], tri[:, :], msk[:, 1], start=False, stop=True)
                for a in range(TT):
                    last = pe.matmul(bank(5)[0:E, 64:65], msk[:, a], ones[:, 0:1], start=a == 0, stop=a == TT - 1)
                last.then_inc(sem("ranks"), 1)
                if k == 0:
                    pe.wait_ge(sem("gates"), 1)
                    for a in range(TT):
                        last = pe.transpose(bank(7)[0:E, a * P:(a + 1) * P], gat[:, a], ident[:, :])
                    last.then_inc(sem("gates_turned"), 1)
                def gather(q, p, chunks=range(DC)):
                    if chunks[0] == 0:
                        after(pe, k, q, "dve", "one_hot", p)
                    for c in chunks:
                        for a in range(TT):
                            last = pe.matmul(bank(6)[:, c * CAP:(c + 1) * CAP], xs[:, a, c:D:DC], one_hot[:, a],
                                             start=a == 0, stop=a == TT - 1)
                    if chunks[-1] == DC - 1:
                        last.then_inc(sem(q + "gathered"), 1)

                def halves(dst, lhsT, rhs, start):
                    for j in range(2):
                        last = pe.matmul(dst[CAP * j:CAP * (j + 1)], lhsT, rhs(j), start=start, stop=True,
                                         skip_group_check=True)
                    return last

                def gate_up(q, p, s0, filled, freed):
                    after(pe, k, q, "dve", "picked", p)
                    if k == 0:
                        after(pe, k, q, "dve", "bias", p)
                        for i, b in enumerate((4, 5)):
                            halves(bank(b), pick_bias, lambda j: bias_gu[:, i, 512 * j:512 * (j + 1)], True)
                            for s in range(2):
                                filled(2 * i + s)
                                v = slot(s0 + 2 * i + s, 4, 1024)
                                for c in range(4):
                                    last = halves(bank(b), picked[:, (4 * s + c) * CAP:(4 * s + c + 1) * CAP],
                                                  lambda j: v[:, c, 512 * j:512 * (j + 1)], False)
                                last.then_inc(freed(2 * i + s), 1)
                        return
                    for s in range(2):
                        filled(s)
                        v = ring[:, s0 + s, :].rearrange("p (g c n) -> p g c n", g=2, c=4)
                        for c in range(4):
                            chunk = 2 * c + s if q == "m1_" else 4 * s + c
                            last = halves(bank(4).rearrange("p (g n) -> p g n", g=2),
                                          picked[:, chunk * CAP:(chunk + 1) * CAP],
                                          lambda j: v[:, :, c, 256 * j:256 * (j + 1)], s == 0 and c == 0)
                        last.then_inc(freed(s), 1)

                def back_turn(q, p):
                    after(pe, k, q, "dve", "gated", p)
                    for a in range(TT):
                        last = pe.transpose(bank(7)[:, a * P:(a + 1) * P], gated[:, a].rearrange("p j s -> p (j s)"), ident[:, :])
                    last.then_inc(done_by(q, "pe", "back"), 1)

                def hid_turn(q, p):
                    after(pe, k, q, "dve", "hidden", p)
                    for c in range(HC[k]):
                        dst = bank(5)[:, c * P:(c + 1) * P] if c < HC[k] - 2 else bank(7)[:, T + c % 2 * P:T + (c % 2 + 1) * P]
                        last = pe.transpose(dst, act_h[:, c:FF[k] // 2:HC[k]], ident[:, :])
                    last.then_inc(done_by(q, "pe", "hid"), 1)

                def down(q, p, s0, filled, freed):
                    after(pe, k, q, "act", "hid", p)
                    if k == 0:
                        pe.wait_ge(sem(q + "hid_dve"), p + 1)
                    for g in range(2):
                        if k == 0 or g == 0:
                            filled(4 + g if k == 0 else 2)
                        v = slot(s0 + 4 + g, 4, 1024) if k == 0 else slot(s0 + 2, 4, 1024)[:, 2 * g:2 * g + 2, :]
                        for c in range(HC[k]):
                            last = halves(bank(4 + k), hid[:, c * P + CAP * g:c * P + CAP * (g + 1)],
                                          lambda j: v[:, c, 512 * j:512 * (j + 1)], g == 0 and c == 0)
                        if k == 0 or g == 1:
                            last.then_inc(freed(4 + g if k == 0 else 2), 1)

                def scatter(q, p):
                    after(pe, k, q, "act", "back", p)
                    after(pe, k, q, "act", "y", p)
                    for a in range(TT):
                        for j in range(2):
                            last = pe.matmul(bank(2 * a + j), back[CAP * j:CAP * (j + 1), a * P:(a + 1) * P],
                                             y[CAP * j:CAP * (j + 1), :], start=False, stop=True, skip_group_check=True)
                    last.then_inc(done_by(q, "pe", "scattered"), 1)

                def rest(q, p, s0, filled, freed):
                    after(pe, k, q, "act", "back", p)
                    hid_turn(q, p)
                    down(q, p, s0, filled, freed)
                    scatter(q, p)

                def main(n, s0):
                    def filled(s):
                        pe.wait_ge(full[s0 + s], 16 * LOADS[k][s] * (n + 1) + 16 * FULL0[k][s0 + s])
                    return s0, filled, lambda s: free[s0 + s]

                def gather_rows(p):
                    after(pe, k, q, "dve", "one_hot", p)
                    for a in range(TT):
                        for j in range(2):
                            last = pe.matmul(bank(6)[CAP * j:CAP * (j + 1)].rearrange("p (q c) -> p q c", c=4), one_hot[:, a],
                                             xs[:, a, :].rearrange("p (q c) -> p q c", c=DC)[:, :, 4 * j:4 * j + 4],
                                             start=a == 0, stop=a == TT - 1, skip_group_check=True)
                    last.then_inc(sem(q + "gathered"), 1)

                def turn_rows(p):
                    pe.wait_ge(sem(q + "rows_copied"), p + 1)
                    for c in range(4):
                        last = pe.transpose(bank(6)[:, c * P:(c + 1) * P], rows[:, c:512:4], ident[:, :])
                    last.then_inc(sem(q + "rows_turned"), 1)

                q = f"m{k}_"
                if k == 0:
                    gather(q, 0)
                else:
                    gather_rows(0)
                    turn_rows(0)
                pe.wait_ge(sem("extra"), k + 1)
                pe.matmul(bank(5)[0:E, 72:73], tri[0:E, 0:E], few[0:E, 17:18], start=True, stop=True)\
                    .then_inc(sem("starts"), 1)
                pe.wait_ge(sem("within"), k + 1)
                row = bank(5)[0:1, 96:129]
                pe.matmul(row[:, 0:1], ones[0:E, 0:1], few[0:E, 17:18], start=True, stop=True)
                pe.matmul(row[:, 1:17], pcol[0:E, :], few[0:E, 32:48], start=True, stop=True)
                pe.matmul(row[:, 17:33], few[0:E, 18:19], few[0:E, 32:48], start=True, stop=True)\
                    .then_inc(sem("rows"), 1)
                if k == 0:
                    pe.wait_ge(sem("gates_copied"), 1)
                    with pe.Fori(0, E) as p:
                        gate_up(q, p, *main(p, 0))
                        back_turn(q, p)
                        gather(q, p + 1, range(4))
                        after(pe, k, q, "act", "back", p)
                        hid_turn(q, p)
                        gather(q, p + 1, range(4, 6))
                        down(q, p, *main(p, 0))
                        gather(q, p + 1, range(6, DC))
                        scatter(q, p)
                else:
                    def overlapped(p, n, s0, prev=None):
                        gate_up(q, p, *main(n, s0))
                        gather_rows(p + 1)
                        if prev:
                            down(q, prev[0], *main(*prev[1:]))
                        turn_rows(p + 1)
                        if prev:
                            after(pe, k, q, "act", "back", prev[0])
                        hid_turn(q, p)
                        if prev:
                            scatter(q, prev[0])
                        after(pe, k, q, "act", "hid", p)
                        back_turn(q, p)

                    overlapped(0, 0, 0)
                    with pe.Fori(0, E // 2 - 1) as n:
                        overlapped(2 * n + 1, n, 3, (2 * n, n, 0))
                        overlapped(2 * n + 2, n + 1, 0, (2 * n + 1, n, 3))
                    overlapped(E - 1, E // 2 - 1, 3, (E - 2, E // 2 - 1, 0))
                    down(q, E - 1, *main(E // 2 - 1, 3))
                    scatter(q, E - 1)
                if k == 0:
                    for a in range(TT):
                        for j in range(2):
                            last = pe.matmul(bank(2 * a + j), gates_T[:, a * P:(a + 1) * P], bias_dn[:, 512 * j:512 * (j + 1)],
                                             start=False, stop=True, skip_group_check=True)
                    last.then_inc(sem("down_bias"), 1)
                pe.wait_ge(sem("list"), k + 1)
                n = pe.value_load(lst[0:1, 0:1], min_val=0, max_val=NLIST)
                q = f"o{k}_"
                with pe.If(n > 0):
                    with pe.Fori(0, n) as p:
                        def filled(s):
                            pe.wait_ge(sem(f"over_full{k}_{s}"), 16 * LOADS[k][s] * (p + 1))
                        def freed(s):
                            return sem(f"over_free{k}_{s}")
                        gather(q, p)
                        gate_up(q, p, 0, filled, freed)
                        back_turn(q, p)
                        rest(q, p, 0, filled, freed)

            experts(0)

            def dense(dst, lhs, rhs, nc_):
                for c in range(nc_):
                    last = pe.matmul(dst, lhs(c), rhs(c), start=c == 0, stop=c == nc_ - 1)
                return last

            def tile(a):
                return lambda c: xT[:, c, a * P:(a + 1) * P]

            norm(G_NORM)
            pe.wait_ge(sem("norm_xT"), 4 * G_NORM + 4)
            pe.wait_ge(sem("p_loaded"), 16)
            for c in range(2):
                for a in range(TT):
                    last = pe.transpose(bank(4)[:, c * T + a * P:c * T + (a + 1) * P], p_tok[:, a, c:256:2], ident[:, :])
            last.then_inc(sem("p_turned"), 1)
            pe.wait_ge(*middle_full(0))
            pe.wait_ge(sem("p_copied"), 1)
            v_p = slot(0, 2, 1024)
            for a in range(TT):
                for n in range(2):
                    dense(bank(2 * a + n), lambda c: pT[:, c, a * P:(a + 1) * P],
                          lambda c: v_p[:, c, 512 * n:512 * (n + 1)], 2).then_inc(sem("dense2"), 1)
            for b in range(4):
                n, a = b // 2, b % 2
                pe.wait_ge(*middle_full(1 + n))
                v = slot(1 + n, DC, 512)
                dense(bank(4 + b), tile(a), lambda c: v[:, c, :], DC).then_inc(sem("dense2"), 1)

            norm(N1_NORM)
            pe.wait_ge(sem("norm_xT"), 4 * N1_NORM + 4)

            def project(i):
                m, a = 3 + i // 2, i % 2
                if a == 0:
                    pe.wait_ge(*middle_full(m))
                if i >= 4:
                    pe.wait_ge(sem("d2_copied"), i - 3)
                (_, _, n), _ = middle[m]
                v = slot(m % SLOTS, DC, n)
                if i in (4, 5, 6, 7):
                    for x in range(2):
                        lo = (2 * a + x) * P
                        last = dense(bank(i % 4)[:, x * T:(x + 1) * T], lambda c: v[:, c, lo:lo + P],
                                     lambda c: xT[:, c, :], DC)
                else:
                    last = dense(bank(i % 4)[:, 0:n], tile(a), lambda c: v[:, c, :], DC)
                last.then_inc(sem("dense2"), 1)

            for i in range(8):
                project(i)
            pe.wait_ge(sem("roped"), 2)
            for a in range(TT):
                for i in range(4):
                    last = pe.transpose(bank(4 + a)[:, i * P:(i + 1) * P], Z[:, a, i * P:(i + 1) * P], ident[:, :])
                last.then_inc(sem("qk_turned"), 1)
            for a in range(TT):
                last = pe.transpose(bank(6)[:, a * P:(a + 1) * P], Z[:, a, 512:640], ident[:, :])
            last.then_inc(sem("qk_turned"), 1)
            for i in range(8, 10):
                project(i)
            pe.wait_ge(sem("qk2_copied"), 3)
            for i in range(4):
                for kv in range(2):
                    r = slice(64 * kv, 64 * kv + 64)
                    last = pe.matmul(bank(4 + kv)[:, i * P:(i + 1) * P], qT2[r, i, 0:P], kT2[r, 0:P], start=True, stop=True)
                    if i == 3:
                        last.then_inc(sem("scores"), 1)
            for half in range(2):
                if half == 1:
                    pe.wait_ge(sem("scores2_copied"), 2)
                for i in range(2):
                    for kv in range(2):
                        r = slice(64 * kv, 64 * kv + 64)
                        last = pe.matmul(bank((6, 7, 4, 5)[2 * half + kv])[:, i * T:(i + 1) * T],
                                         qT2[r, 2 * half + i, P:T], kT2[r, :], start=True, stop=True)
                        if i == 1:
                            last.then_inc(sem("scores"), 1)
            for i in range(10, 16):
                project(i)
            for k in range(6):
                g0 = 4 * (k % 2)
                if k == 0:
                    pe.wait_ge(sem("scores2_copied"), 6)
                if k in (0, 2):
                    pe.wait_ge(sem("probs"), 24 if k == 0 else 32)
                if k >= 4:
                    pe.wait_ge(sem("p2_copied"), k - 3)
                for i in range(4):
                    src = sA0[:, g0 + i, :] if k < 2 else sA1[:, g0 + i, (k // 2 - 1) * P:(k // 2) * P]
                    last = pe.transpose(bank(4 + k % 4)[:, i * P:(i + 1) * P], src, ident[:, :])
                last.then_inc(sem("w_turned"), 1)
            for i in range(16, 18):
                project(i)
            pe.wait_ge(sem("p2_copied"), 6)
            for a in range(TT):
                for g in range(8):
                    for kt in range(a + 1):
                        last = pe.matmul(bank(6 + a)[:, g * 64:(g + 1) * 64], pT2[:, 8 * (a + kt) + g, :],
                                         Z[:, kt, 640 + 64 * (g // 4):704 + 64 * (g // 4)], start=kt == 0, stop=kt == a)
                last.then_inc(sem("pv"), 1)
            for a in range(TT):
                pe.wait_ge(sem("branch_ready"), a + 1)
                for c in range(4):
                    last = pe.transpose(bank(4 + a)[:, c * P:(c + 1) * P], ao[:, a, c:512:4], ident[:, :])
                last.then_inc(sem("branch_turned"), 1)
            pe.wait_ge(sem("ke_ready"), 1)
            pe.wait_ge(sem("branch_copied"), 2)
            for a in range(TT):
                for n in range(4):
                    last = pe.transpose(bank(7 if a == 0 else 5)[:, n * P:(n + 1) * P],
                                        suf_f[:, n * T + a * P:n * T + (a + 1) * P], ident[:, :])
                last.then_inc(sem("ke_turned"), 1)

            def sums(n):
                j = SUB - 1 - n
                pe.wait_ge(sem("w_offset"), n + 1)
                buf = (w_a, w_b)[n % 2].rearrange(by_sub, j=SUB)
                nb = 512 // SUB
                for g in range(2):
                    last = pe.matmul(bank(4 + 2 * g).rearrange(by_sub, j=SUB)[:, :, j:SUB], spread[:, n:n + P],
                                     buf[:, nb * g:nb * (g + 1), j:SUB], start=n == 0, stop=True, skip_group_check=True)
                last.then_inc(sem("w_used"), 1)

            def update(i):
                if i >= 2:
                    pe.wait_ge(sem("state"), 4 * (i - 1))
                a, r = i // 8, slice(32 * (i // 2 % 4), 32 * (i // 2 % 4) + 32)
                src = (ke_even, ke_odd)[i % 2]
                for n in range(4):
                    last = pe.matmul(bank(5 + 2 * (i % 2))[:, n * P:(n + 1) * P], src[r, 512 * a + n * P:512 * a + (n + 1) * P],
                                     Z[r, a, 768 + n * P:768 + (n + 1) * P], start=True, stop=True)
                last.then_inc(sem("update"), 1)

            def inter(i):
                pe.wait_ge(sem("state"), 4 * i)
                for n in range(4):
                    lo = (n % 2) * T + SUB * i
                    last = pe.matmul(bank(n // 2)[:, lo:lo + SUB], states[:, i % 4, n * P:(n + 1) * P],
                                     q_e[:, n * T + SUB * i:n * T + SUB * (i + 1)], start=False, stop=True,
                                     skip_group_check=True)
                    if i == NSUB - 1 and n % 2 == 1:
                        last.then_inc(sem("hgrn_o"), 1)
                if i < NSUB - 1:
                    last.then_inc(sem("inter"), 1)

            def last_projections(n):
                a, c = n // DC, n % DC
                if c == 0:
                    pe.wait_ge(*middle_full(12))
                    pe.wait_ge(sem("d2_copied"), 15 + a)
                last = pe.matmul(bank(2 + a), tile(a)(c), slot(12 % SLOTS, DC, 512)[:, c, :], start=c == 0, stop=c == DC - 1)
                if c == DC - 1:
                    last.then_inc(sem("dense2"), 1)

            sums(0)
            last_projections(0)
            sums(1)
            last_projections(1)
            pe.wait_ge(sem("ke_copied"), 4)
            pe.wait_ge(sem("d2_copied"), 18)
            for b in range(2):
                pe.matmul(bank(b), zeros[:, :], q_e[:, 0:512], start=True, stop=True)
            update(0)
            update(1)
            for n in range(2, SUB):
                sums(n)
                last_projections(n)
                inter(n - 1)
                if n < NSUB - 1:
                    update(n)
            pe.wait_ge(sem("intra"), 2)
            for n in range(4):
                for a in range(TT):
                    lo = n * T + a * P
                    pe.matmul(bank(n // 2)[:, (n % 2) * T + a * P:(n % 2) * T + (a + 1) * P],
                              Z[:, a, 768 + n * P:768 + (n + 1) * P], r_q[:, lo:lo + P],
                              start=False, stop=True, skip_group_check=True)
            inter(NSUB - 1)
            pe.wait_ge(sem("oT_act"), 1)
            pe.wait_ge(sem("oT_dve"), 1)
            for a in range(TT):
                for n in range(4):
                    last = pe.transpose(bank(6 + a)[:, n * P:(n + 1) * P], w_b[:, n * T + a * P:n * T + (a + 1) * P], ident[:, :])
                last.then_inc(sem("o_turned"), 1)
            pe.wait_ge(*middle_full(13))
            pe.wait_ge(sem("d2_copied"), 20)
            v_a, v_h = slot(13 % SLOTS, 4, 1024), slot(14 % SLOTS, 4, 1024)
            for b in range(4):
                a, n = b // 2, b % 2
                dense(bank(b), lambda c: Z[:, a, c * P:(c + 1) * P], lambda c: v_a[:, c, 512 * n:512 * (n + 1)], 4)\
                    .then_inc(sem("dense2"), 1)
            for a in range(TT):
                pe.wait_ge(sem("branch_ready"), a + 3)
                for c in range(4):
                    last = pe.transpose(bank(4 + a)[:, c * P:(c + 1) * P], k1[:, 512 * a + c:512 * (a + 1):4], ident[:, :])
                last.then_inc(sem("branch_turned"), 1)
            pe.wait_ge(*middle_full(14))
            pe.wait_ge(sem("branch_copied"), 4)
            for b in range(4):
                a, n = b // 2, b % 2
                dense(bank((6, 7, 4, 5)[b]), lambda c: Z[:, a, 768 + c * P:768 + (c + 1) * P],
                      lambda c: v_h[:, c, 512 * n:512 * (n + 1)], 4).then_inc(sem("dense2"), 1)
            for b in range(4):
                pe.wait_ge(sem("mixed"), 2 * (b // 2) + 2)
                turn(bank(b), xs[:, b // 2, :], 4 * (b % 2), DC, 4, "mix_turned")
            pe.wait_ge(sem("mix_copied_act"), 4)
            pe.wait_ge(sem("mix_copied_dve"), 4)
            for b in range(4):
                n, a = b // 2, b % 2
                pe.wait_ge(*middle_full(15 + n))
                v = slot(3 + n, DC, 512)
                dense(bank(4 + b), tile(a), lambda c: v[:, c, :], DC).then_inc(sem("dense2"), 1)

            experts(1)


N_SMALL = 4 + 4 + 10
NAMES = ["x", "p", "positions", "attn_norm", "w_in", "q_norm", "k_norm", "lam_q1", "lam_k1", "lam_q2", "lam_k2",
         "subln", "w_pool", "pool_scale", "w_out", "ffn_norm", "w_router", "b_router", "w_gate", "b_gate", "w_up",
         "b_up", "w_down", "b_down", "ple_gate_norm", "w_ple_gate", "w_ple_proj", "ple_post_norm", "positions_2",
         "norm1_w_2", "w_in_2", "q_norm_w_2", "k_norm_w_2", "attn_sinks_2", "hgrn_lower_bounds_2", "hgrn_norm_w_2",
         "w_branch_attn_2", "w_branch_hgrn_2", "w_out_2", "norm2_w_2", "w_router_group_2", "b_router_group_2",
         "w_router_expert_2", "b_router_expert_2", "w_gate_experts_2", "w_up_experts_2", "w_down_experts_2"]


def kernel(**inputs):
    import concourse.bacc as bacc
    from concourse.bass_utils import run_bass_kernel_spmd

    nc = bacc.Bacc("TRN2", target_bir_lowering=False, num_devices=1)
    arrays, args = {}, {}
    for name in NAMES:
        a = np.ascontiguousarray(inputs[name])
        arrays["in_" + name] = a
        args[name] = nc.dram_tensor("in_" + name, a.shape, mybir.dt.from_np(a.dtype), kind="ExternalInput").ap()
    out = nc.dram_tensor("out", (1, T, D), F32, kind="ExternalOutput").ap()
    two_blocks(nc, args, out)
    r = run_bass_kernel_spmd(nc, [arrays], core_ids=[0])
    return r.results[0]["out"]
```
